# Optimizing a Trainium2 kernel written in Bass

```python
import jax
import jax.numpy as jnp
from jax import lax
import numpy as np

D_MODEL = 1024
BATCH = 1
SEQ = 1024
DEPTH = 1
DEC_BATCH = 1
DEC_SEQ = 64
PAST_LEN = 1024

CHUNK = 64
N_PAST_CHUNKS = 8
ATTN_REACH = N_PAST_CHUNKS * CHUNK
BAND = (N_PAST_CHUNKS + 1) * CHUNK
N_HEADS_A = 8
HEAD_DIM_A = 64
D_ATTN = N_HEADS_A * HEAD_DIM_A
REL_CLIP = 256
N_REL = 2 * REL_CLIP + 1
ATTN_SCALE = HEAD_DIM_A ** -0.5
N_HEADS_B = 4
DK_B = 128
DV_B = 128
D_RNN = N_HEADS_B * DK_B
IN_WIDTHS = (D_ATTN, D_ATTN, D_ATTN, D_RNN, D_RNN, D_RNN, D_RNN, D_MODEL, D_MODEL)
D_IN = sum(IN_WIDTHS)
IN_SPLITS = tuple(sum(IN_WIDTHS[:i + 1]) for i in range(len(IN_WIDTHS) - 1))
PEER_HEADS = 8
N_KEYS = 128
N_EXPERTS = N_KEYS * N_KEYS
PEER_HALF = 128
PEER_TOPK = 16
PEER_BLOCK = 128
EPS = 1e-6

kernel_name = 'streaming_hybrid_bandattn_hgrn2_peer'

def rmsnorm(x, gain):
    xf = x.astype(jnp.float32)
    y = xf * lax.rsqrt(jnp.mean(xf * xf, axis=-1, keepdims=True) + EPS)
    return (y * gain.astype(jnp.float32)).astype(x.dtype)

def mixer_proj(x, norm_g, w_in, lb):
    b, t, _ = x.shape
    z = rmsnorm(x, norm_g) @ w_in
    q_a, k_a, v_a, f_b, i_b, q_b, g_b, gate_a, gate_b = jnp.split(z, IN_SPLITS, axis=-1)

    def heads_a(a):
        return a.reshape(b, t, N_HEADS_A, HEAD_DIM_A)

    def heads_b(a):
        return a.reshape(b, t, N_HEADS_B, -1).transpose(0, 2, 1, 3).astype(jnp.float32)

    lbh = lb.reshape(N_HEADS_B, 1, DK_B)
    fg = lbh + (1.0 - lbh) * jax.nn.sigmoid(heads_b(f_b))
    logf = jnp.log(fg)
    k_b = 1.0 - fg
    qb = jax.nn.silu(heads_b(q_b))
    vb = heads_b(i_b)
    return heads_a(q_a), heads_a(k_a), heads_a(v_a), qb, k_b, vb, logf, g_b, gate_a, gate_b

def band_attention_prompt(q, k, v, rel_bias):
    b, s, h, d = q.shape
    nc = s // CHUNK
    qc = q.reshape(b, nc, CHUNK, h, d)
    pad = ((0, 0), (ATTN_REACH, 0), (0, 0), (0, 0))
    kc = jnp.pad(k, pad).reshape(b, nc + N_PAST_CHUNKS, CHUNK, h, d)
    vc = jnp.pad(v, pad).reshape(b, nc + N_PAST_CHUNKS, CHUNK, h, d)
    kb = jnp.concatenate([kc[:, i:i + nc] for i in range(N_PAST_CHUNKS + 1)], axis=2)
    vb = jnp.concatenate([vc[:, i:i + nc] for i in range(N_PAST_CHUNKS + 1)], axis=2)
    t_idx = jnp.arange(CHUNK)[:, None]
    j_idx = jnp.arange(BAND)[None, :]
    dist = ATTN_REACH + t_idx - j_idx
    bias = rel_bias[:, jnp.clip(dist, -REL_CLIP, REL_CLIP) + REL_CLIP].astype(jnp.float32)
    key_pos = (jnp.arange(nc)[:, None] - N_PAST_CHUNKS) * CHUNK + j_idx
    scores = jnp.einsum('bnthd,bnjhd->bnhtj', qc, kb).astype(jnp.float32) * ATTN_SCALE + bias
    scores = jnp.where((key_pos >= 0)[None, :, None, None, :], scores, -jnp.inf)
    p = jax.nn.softmax(scores, axis=-1).astype(v.dtype)
    return jnp.einsum('bnhtj,bnjhd->bnthd', p, vb).reshape(b, s, h, d)

def band_attention_step(q, k_new, v_new, k_cache, v_cache, rel_bias):
    past = k_cache.shape[1]
    t = q.shape[1]
    keys = jnp.concatenate([k_cache.astype(k_new.dtype), k_new], axis=1)
    vals = jnp.concatenate([v_cache.astype(v_new.dtype), v_new], axis=1)
    dist = past + jnp.arange(t)[:, None] - jnp.arange(past + t)[None, :]
    bias = rel_bias[:, jnp.clip(dist, -REL_CLIP, REL_CLIP) + REL_CLIP].astype(jnp.float32)
    scores = jnp.einsum('bthd,bjhd->bhtj', q, keys).astype(jnp.float32) * ATTN_SCALE + bias
    p = jax.nn.softmax(scores, axis=-1).astype(vals.dtype)
    return jnp.einsum('bhtj,bjhd->bthd', p, vals)

def hgrn2_chunk(s0, q, k, v, logf):
    t = q.shape[2]
    cum = jnp.cumsum(logf, axis=2)
    causal = jnp.arange(t)[:, None] >= jnp.arange(t)[None, :]
    decay = jnp.exp(jnp.where(causal[..., None], cum[:, :, :, None, :] - cum[:, :, None, :, :], -jnp.inf))
    attn = jnp.einsum('bhtk,bhsk,bhtsk->bhts', q, k, decay)
    o = jnp.einsum('bhtk,bhkv->bhtv', q * jnp.exp(cum), s0) + jnp.einsum('bhts,bhsv->bhtv', attn, v)
    last = cum[:, :, -1:, :]
    s_new = jnp.exp(last[:, :, 0, :])[..., None] * s0 + jnp.einsum('bhsk,bhsv->bhkv', k * jnp.exp(last - cum), v)
    return s_new, o

def hgrn2_prompt(q, k, v, logf):
    b, h, s, _ = q.shape
    nc = s // CHUNK

    def to_chunks(a):
        return a.reshape(b, h, nc, CHUNK, a.shape[-1]).transpose(2, 0, 1, 3, 4)

    s0 = jnp.zeros((b, h, DK_B, DV_B), jnp.float32)

    def step(state, inp):
        return hgrn2_chunk(state, *inp)

    s_fin, o = lax.scan(step, s0, (to_chunks(q), to_chunks(k), to_chunks(v), to_chunks(logf)))
    return s_fin, o.transpose(1, 2, 0, 3, 4).reshape(b, h, s, DV_B)

def peer(x, w_query, sub_keys, u_tab, v_tab):
    shp = x.shape
    xt = x.reshape(-1, D_MODEL)
    n = xt.shape[0]
    q = (xt @ w_query).reshape(n, PEER_HEADS, 2, PEER_HALF)
    s = jnp.einsum('nhpd,phkd->nhpk', q, sub_keys).astype(jnp.float32)
    sv, si = lax.top_k(s, PEER_TOPK)
    comb = (sv[:, :, 0, :, None] + sv[:, :, 1, None, :]).reshape(n, PEER_HEADS, PEER_TOPK * PEER_TOPK)
    cv, ci = lax.top_k(comb, PEER_TOPK)
    i1 = jnp.take_along_axis(si[:, :, 0], ci // PEER_TOPK, axis=-1)
    i2 = jnp.take_along_axis(si[:, :, 1], ci % PEER_TOPK, axis=-1)
    idx = i1 * N_KEYS + i2
    gate = jax.nn.softmax(cv, axis=-1)
    pad = (-n) % PEER_BLOCK
    nb = (n + pad) // PEER_BLOCK
    xt_p = jnp.pad(xt, ((0, pad), (0, 0))).reshape(nb, PEER_BLOCK, D_MODEL)
    idx_p = jnp.pad(idx, ((0, pad), (0, 0), (0, 0))).reshape(nb, PEER_BLOCK, PEER_HEADS, PEER_TOPK)
    gate_p = jnp.pad(gate, ((0, pad), (0, 0), (0, 0))).reshape(nb, PEER_BLOCK, PEER_HEADS, PEER_TOPK)

    def block(args):
        xb, ib, gb = args
        hid = jax.nn.gelu(jnp.einsum('nd,nhkd->nhk', xb, u_tab[ib]).astype(jnp.float32), approximate=False)
        return jnp.einsum('nhk,nhkd->nd', (gb * hid).astype(v_tab.dtype), v_tab[ib])

    out = lax.map(block, (xt_p, idx_p, gate_p))
    return out.reshape(-1, D_MODEL)[:n].reshape(shp).astype(x.dtype)

def finish_layer(x, o_a, o_b, g_b, gate_a, gate_b, hgrn_g, w_a, w_b, w_out,
                 norm_ffn, w_query, sub_keys, u_tab, v_tab):
    b, t, _ = x.shape
    oa = o_a.reshape(b, t, D_ATTN)
    ob = o_b.transpose(0, 2, 1, 3)
    ob = ob * lax.rsqrt(jnp.mean(ob * ob, axis=-1, keepdims=True) + EPS) * hgrn_g.astype(jnp.float32)
    ob = ob * jax.nn.silu(g_b.reshape(b, t, N_HEADS_B, DV_B).astype(jnp.float32))
    ob = ob.reshape(b, t, D_RNN).astype(x.dtype)
    merged = jax.nn.sigmoid(gate_a) * (oa @ w_a) + jax.nn.sigmoid(gate_b) * (ob @ w_b)
    h = x + merged @ w_out
    return h + peer(rmsnorm(h, norm_ffn), w_query, sub_keys, u_tab, v_tab)

def setup_inputs(seed: int = 0) -> dict:
    key = jax.random.key(seed)
    ks = jax.random.split(key, 20)

    def nrm(k, shape, scale):
        return jax.random.normal(k, shape, jnp.float32) * scale

    a_len = min(ATTN_REACH, PAST_LEN)
    return {
        'x_prompt': nrm(ks[0], (BATCH, SEQ, D_MODEL), 1.0),
        'x_sample': nrm(ks[1], (DEC_BATCH, DEC_SEQ, D_MODEL), 1.0),
        'cache_attn_k': nrm(ks[2], (DEPTH, DEC_BATCH, a_len, N_HEADS_A, HEAD_DIM_A), 1.0),
        'cache_attn_v': nrm(ks[3], (DEPTH, DEC_BATCH, a_len, N_HEADS_A, HEAD_DIM_A), 1.0),
        'state_hgrn': nrm(ks[4], (DEPTH, DEC_BATCH, N_HEADS_B, DK_B, DV_B), 0.5),
        'norm_mix': 1.0 + nrm(ks[5], (DEPTH, D_MODEL), 0.05),
        'w_in': nrm(ks[6], (DEPTH, D_MODEL, D_IN), D_MODEL ** -0.5),
        'rel_bias': nrm(ks[7], (DEPTH, N_HEADS_A, N_REL), 0.2),
        'lb_logits': nrm(ks[8], (DEPTH + 1, D_RNN), 0.1),
        'hgrn_norm': 1.0 + nrm(ks[9], (DEPTH, N_HEADS_B, DV_B), 0.05),
        'w_branch_a': nrm(ks[10], (DEPTH, D_ATTN, D_MODEL), D_ATTN ** -0.5),
        'w_branch_b': nrm(ks[11], (DEPTH, D_RNN, D_MODEL), D_RNN ** -0.5),
        'w_out': nrm(ks[12], (DEPTH, D_MODEL, D_MODEL), D_MODEL ** -0.5),
        'norm_ffn': 1.0 + nrm(ks[13], (DEPTH, D_MODEL), 0.05),
        'peer_query': nrm(ks[14], (DEPTH, D_MODEL, PEER_HEADS * 2 * PEER_HALF), D_MODEL ** -0.5),
        'peer_subkeys': nrm(ks[15], (DEPTH, 2, PEER_HEADS, N_KEYS, PEER_HALF), PEER_HALF ** -0.5),
        'peer_u': nrm(ks[16], (DEPTH, N_EXPERTS, D_MODEL), D_MODEL ** -0.5),
        'peer_v': nrm(ks[17], (DEPTH, N_EXPERTS, D_MODEL), PEER_HEADS ** -0.5),
        'norm_final': 1.0 + nrm(ks[18], (D_MODEL,), 0.05),
    }

def reference(x_prompt, x_sample, cache_attn_k, cache_attn_v, state_hgrn, norm_mix, w_in, rel_bias,
              lb_logits, hgrn_norm, w_branch_a, w_branch_b, w_out, norm_ffn, peer_query, peer_subkeys,
              peer_u, peer_v, norm_final):
    lb_all = jnp.cumsum(jax.nn.softmax(lb_logits.astype(jnp.float32), axis=0), axis=0)
    xp = x_prompt
    xs = x_sample
    keep = min(ATTN_REACH, x_prompt.shape[1])
    kp_rows, vp_rows, sp_states = [], [], []
    ks_rows, vs_rows, ss_states = [], [], []
    for l in range(DEPTH):
        lb = lb_all[l]
        qa, ka, va, qb, kb, vb, logf, gb, ga_gate, gb_gate = mixer_proj(xp, norm_mix[l], w_in[l], lb)
        oa = band_attention_prompt(qa, ka, va, rel_bias[l])
        s_fin, ob = hgrn2_prompt(qb, kb, vb, logf)
        kp_rows.append(ka[:, ka.shape[1] - keep:])
        vp_rows.append(va[:, va.shape[1] - keep:])
        sp_states.append(s_fin.astype(x_prompt.dtype))
        xp = finish_layer(xp, oa, ob, gb, ga_gate, gb_gate, hgrn_norm[l], w_branch_a[l], w_branch_b[l],
                          w_out[l], norm_ffn[l], peer_query[l], peer_subkeys[l], peer_u[l], peer_v[l])
        qa, ka, va, qb, kb, vb, logf, gb, ga_gate, gb_gate = mixer_proj(xs, norm_mix[l], w_in[l], lb)
        oa = band_attention_step(qa, ka, va, cache_attn_k[l], cache_attn_v[l], rel_bias[l])
        s_new, ob = hgrn2_chunk(state_hgrn[l].astype(jnp.float32), qb, kb, vb, logf)
        ks_rows.append(ka)
        vs_rows.append(va)
        ss_states.append(s_new.astype(x_sample.dtype))
        xs = finish_layer(xs, oa, ob, gb, ga_gate, gb_gate, hgrn_norm[l], w_branch_a[l], w_branch_b[l],
                          w_out[l], norm_ffn[l], peer_query[l], peer_subkeys[l], peer_u[l], peer_v[l])
    y_prompt = rmsnorm(xp, norm_final)
    y_sample = rmsnorm(xs, norm_final)
    new_k_prompt = jnp.stack(kp_rows, axis=0)
    new_v_prompt = jnp.stack(vp_rows, axis=0)
    new_state_prompt = jnp.stack(sp_states, axis=0)
    new_k_sample = jnp.stack(ks_rows, axis=0)
    new_v_sample = jnp.stack(vs_rows, axis=0)
    new_state_sample = jnp.stack(ss_states, axis=0)
    return (y_prompt, y_sample, new_k_prompt, new_v_prompt, new_state_prompt, new_k_sample, new_v_sample, new_state_sample)


_drawn_inputs = setup_inputs


def setup_inputs(seed=0):
    import zlib

    import numpy as np

    out = dict(_drawn_inputs(seed))
    spreads = {}
    factors = {'rel_bias': 3.104}
    for name, (base, spread) in spreads.items():
        noise = np.random.default_rng([zlib.crc32(name.encode()), seed]).standard_normal(out[name].shape)
        drawn = base * np.exp(spread * noise) if base else spread * noise
        out[name] = jnp.asarray(drawn.astype(out[name].dtype))
    for name, factor in factors.items():
        out[name] = (out[name] * factor).astype(out[name].dtype)
    return out
```

```python
from contextlib import ExitStack

import concourse.bass as bass
from concourse import mybir

F32 = mybir.dt.float32
U32 = mybir.dt.uint32
ALU = mybir.AluOpType
ACT = mybir.ActivationFunctionType
AX = mybir.AxisListType.X

P = 128
D = 1024
DK = D // P
SEQ = 1024
DEC = 64
CH = 64
HA = 8
DA = 512
CB = DA // P
HB = 4
EPS = 1e-6
NREL = 513
CLIP = 256
REACH = 512
WIN = 640
SCALE = 64 ** -0.5
NEG = -1e30
LOWEST = -3.0e38
NEXP = 16384
PH = 8
TOPK = 16
NL = 6
LEVELS = [32, 16, 8, 4, 2, 1]
SAMPLE = 8
GROUPS = [[(SAMPLE, 64, 0), (0, 128, 64), (1, 128, 192)]] + [
    [(2 * g, 128, 0), (2 * g + 1, 128, 128)] for g in range(1, 4)]
WG = 320
STAGES = "ABCDEFGHI"
R = 8


def width(g):
    return sum(t[1] for t in GROUPS[g])


def stage_no(g, s):
    return 1 + g * len(STAGES) + STAGES.index(s)


def plan_projections():
    blocks, products = [], []

    def add(g, stage, w, nk, c0, nc_, kind, what):
        b = len(blocks)
        blocks.append((w, nk, c0, nc_))
        if kind == "fm":
            for s in range(nc_ // P):
                products.append((g, stage, b, "fm", what, c0 // P + s, s, None))
        else:
            for ti in range(len(GROUPS[g])):
                products.append((g, stage, b, "tm", what, c0, 0, ti))

    for g in range(len(GROUPS)):
        for c in (0, 256):
            add(g, "B", "w_in", 8, c, 256, "fm", "q")
        for c in (512, 768):
            add(g, "B", "w_in", 8, c, 256, "fm", "k")
        for c in (1024, 1280):
            add(g, "B", "w_in", 8, c, 256, "tm", "v")
        for i in range(4):
            add(g, "D", "w_in", 8, 3584 + 256 * i, 256, "fm", "gate")
            if i % 2:
                add(g, "D", "w_a", 4, 512 * (i // 2), 512, "fm", "branch")
        for c in (1536, 1792):
            add(g, "E", "w_in", 8, c, 256, "fm", "f")
        for c in (2560, 2816):
            add(g, "E", "w_in", 8, c, 256, "fm", "qb")
        for c in (2048, 2304):
            add(g, "E", "w_in", 8, c, 256, "tm", "i")
        for c in (3072, 3328):
            add(g, "E", "w_in", 8, c, 256, "tm", "g")
        for i in range(4):
            add(g, "G", "w_in", 8, 4608 + 256 * i, 256, "fm", "gate")
            if i % 2:
                add(g, "G", "w_b", 4, 512 * (i // 2), 512, "fm", "branch")
        for i in range(4):
            add(g, "H", "w_out", 8, 256 * i, 256, "tm", "o")
        for i in range(8):
            add(g, "I", "w_query", 8, 256 * i, 256, "fm", "query")
    return blocks, products


def build(nc, x_prompt, x_sample, cache_k, cache_v, state_in, norm_mix, w_in, rel_bias, lb_logits,
          hgrn_norm, w_a, w_b, w_out, norm_ffn, w_query, sub_keys, u_tab, v_tab, norm_final,
          y_prompt, y_sample, k_prompt, v_prompt, state_prompt, k_sample, v_sample, state_sample):
    weights = {"w_in": w_in[0], "w_a": w_a[0], "w_b": w_b[0], "w_out": w_out[0], "w_query": w_query[0]}
    xp, xs = x_prompt[0], x_sample[0]
    blocks, products = plan_projections()
    last_product = {}
    for n, pr in enumerate(products):
        last_product[pr[2]] = n
    by_stage = {}
    for n, pr in enumerate(products):
        by_stage.setdefault((pr[0], pr[1]), []).append(n)
    NG = len(GROUPS)
    att = [(g, h, ti) for g in range(NG) for h in range(HA) for ti in range(len(GROUPS[g]))]
    att_no = {s: n for n, s in enumerate(att)}
    tile_no = {(g, ti): n for n, (g, ti) in enumerate((g, ti) for g in range(NG) for ti in range(len(GROUPS[g])))}
    norm_no = {}
    for g in range(NG):
        for s in "AH":
            for ti in range(len(GROUPS[g])):
                norm_no[g, s, ti] = len(norm_no)
    norm_batch = {(g, s): 2 * g + n for g in range(NG) for n, s in enumerate("AH")}
    top_no = {}
    for g in range(NG):
        for h in range(PH):
            for ti in range(len(GROUPS[g])):
                top_no[g, h, ti] = len(top_no)

    h_scr = nc.dram_tensor("h_scr", (SEQ + DEC, D), F32, kind="Internal").ap()
    xn_scr = nc.dram_tensor("xn_scr", (SEQ + DEC, D), F32, kind="Internal").ap()
    rel_scr = nc.dram_tensor("rel_scr", (HA, P, WIN), F32, kind="Internal").ap()
    sk_scr = nc.dram_tensor("sk_scr", (P, 16 * P), F32, kind="Internal").ap()

    def rows_of(ap_prompt, ap_sample, tid):
        return ap_sample if tid == SAMPLE else ap_prompt[tid * P:(tid + 1) * P, :]

    with ExitStack() as ctx:
        def sb(name, shape, dt=F32):
            return ctx.enter_context(nc.sbuf_tensor(name, shape, dt))

        def sem(name):
            return ctx.enter_context(nc.semaphore(name))

        PS = ctx.enter_context(nc.psum_tensor("PS", [P, 8, 512], F32))
        ident = sb("ident", [P, P])
        masks = sb("masks", [P, NL + 1, P])
        gain_mix = sb("gain_mix", [P, DK])
        gain_ffn = sb("gain_ffn", [P, D])
        gain_final = sb("gain_final", [P, D])
        gain_hgrn = sb("gain_hgrn", [P, DA])
        lbl = sb("lbl", [P, 2, HB])
        lb = sb("lb", [P, HB])
        one_lb = sb("one_lb", [P, HB])
        iota16 = sb("iota16", [P, TOPK])
        restart = sb("restart", [P, WG])
        mark_a = sb("mark_a", [P, 1])
        mark_d = sb("mark_d", [P, 1])
        xnT = sb("xnT", [P, DK, WG])
        M = sb("M", [P, DK, WG])
        kT = sb("kT", [P, CB, SEQ])
        v = sb("v", [P, SEQ // P, DA])
        kS = sb("kS", [P, CB, DEC])
        vS = sb("vS", [P, DA])
        Q = sb("Q", [P, CB, WG])
        K2 = sb("K2", [P, CB, WG])
        Q2 = sb("Q2", [P, CB, WG])
        T12 = sb("T12", [P, 2, 3, DA])
        T1 = T12[:, 0]
        T2 = T12[:, 1]
        skT = T12[:, :, :, :].rearrange("p a b c -> p (a b c)")[:, 0:16 * P]
        wring = sb("wring", [P, 2, 2048])
        bias = sb("bias", [P, 2, WIN])
        S_tile = sb("S_tile", [P, HB, 2, P])
        S_mid = sb("S_mid", [P, HB, P])
        idx = sb("idx", [P, 9 * P], U32)
        gates = sb("gates", [P, 9 * P])
        ss = sb("ss", [P, 8])
        rstd = sb("rstd", [P, 8])
        tmp = sb("tmp", [P, 7680])
        ring = sb("ring", [P, R, D])
        xt = sb("xt", [P, D])
        acc = sb("acc", [P, D])
        ixs = sb("ixs", [P, 2, TOPK], U32)
        hid = sb("hid", [P, TOPK])
        glu = sb("glu", [P, TOPK])
        wk = sb("wk", [P, TOPK])

        def part(at, *shape):
            n = 1
            for k in shape:
                n *= k
            ap = tmp[:, at:at + n]
            names = "abcd"[:len(shape)]
            if len(shape) == 1:
                return ap
            return ap.rearrange(f"p ({' '.join(names)}) -> p {' '.join(names)}", **dict(zip(names, shape)))

        hx = part(0, 3, D)
        xn = part(3 * D, 3, D)
        kc = part(0, 4, DA)
        sc = part(0, 2, WIN)
        pt = part(2 * WIN, 2, WIN)
        nmax = part(4 * WIN, 2)
        rsum = part(4 * WIN + 2, 2)
        rinv = part(4 * WIN + 4, 2)
        sg = part(0, DK, WG)
        E = part(0, NL + 1, HB, P)
        Lq = part(3584, NL, P)
        Lk = part(4352, NL, P)
        Am = part(5120, NL + 1, P)
        attnT = part(6016, 2, P)
        ecum = part(6272, HB, P)
        kdT = part(6784, P)
        ob = part(6912, HB, P)
        ssq = part(7424, HB)
        rsq = part(7428, HB)
        elast = part(7432, HB, 2)
        junk = part(7440, P)
        qp = part(0, 2, 2, WG)
        s1 = part(1280, 2, 2, P)
        s2 = part(1792, 2, P)
        comb = part(2048, TOPK, TOPK)
        comb2 = part(2304, TOPK * TOPK)
        eq = part(2560, 2, TOPK, TOPK)
        sv = part(3072, 2, TOPK)
        sif = part(3104, 2, TOPK)
        cv = part(3136, TOPK)
        abf = part(3152, 2, TOPK)
        i12 = part(3184, 2, TOPK)
        ge = part(3216, TOPK)
        gsum = part(3232, 1)
        ginv = part(3233, 1)
        ncv = part(3234, 1)
        si = part(3240, 2, TOPK).bitcast(U32)
        ci = part(3272, TOPK).bitcast(U32)
        ab = part(3288, 2, TOPK).bitcast(U32)
        rel = tmp[0:HA, 0:767]
        sk = part(1024, 16, P)
        skTs = part(1024 + 2048, 16, P)

        const_in, rel_in, sk_in, relE, rel_out, sk_tr, sk_cp, sk_out, consts, lb_d, lb_a, state_loaded = [
            sem(n) for n in ("const_in", "rel_in", "sk_in", "relE", "rel_out", "sk_tr", "sk_cp", "sk_out",
                             "consts", "lb_d", "lb_a", "state_loaded")]
        dve_chain = sem("dve_chain")
        bar_act, bar_dve = sem("bar_act"), sem("bar_dve")
        w_in_sem = [sem("w_landed0"), sem("w_landed1")]
        pj_ready = sem("pj_ready")
        pj_free = [sem("pj_free0"), sem("pj_free1")]
        x_in, n_sq, n_ms, n_rt, xn_ready, tr_ready = [sem(n) for n in (
            "x_in", "n_sq", "n_ms", "n_rt", "xn_ready", "tr_ready")]
        tr_free = sem("tr_free")
        kc_in, vc_in, kt_tr, kt_cp, kv_out = [sem(n) for n in ("kc_in", "vc_in", "kt_tr", "kt_cp", "kv_out")]
        bias_in = [sem("bias_in0"), sem("bias_in1")]
        at_sc, at_biased, at_max, at_exp, at_pT, at_ptc, at_pv, at_rinv, at_oa = [sem(n) for n in (
            "at_sc", "at_biased", "at_max", "at_exp", "at_pT", "at_ptc", "at_pv", "at_rinv", "at_oa")]
        oT_tr, oT_cp = sem("oT_tr"), sem("oT_cp")
        f_sig, f_fg, f_ln, g_silu = [sem(n) for n in ("f_sig", "f_fg", "f_ln", "g_silu")]
        hg_D, hg_E, hg_kq, hg_L, hg_at, hg_red, hg_kdT, hg_kdc, hg_st, hg_S, hg_o, hg_oc, hg_ms, hg_rt, hg_ob, \
            hg_oT, hg_obc, st_out = [sem(n) for n in (
                "hg_D", "hg_E", "hg_kq", "hg_L", "hg_at", "hg_red", "hg_kdT", "hg_kdc", "hg_st", "hg_S", "hg_o",
                "hg_oc", "hg_ms", "hg_rt", "hg_ob", "hg_oT", "hg_obc", "st_out")]
        h_out = sem("h_out")
        skT_in, tk_sc, tk_cp, tk_done, tk_cv, tk_exp = [sem(n) for n in (
            "skT_in", "tk_sc", "tk_cp", "tk_done", "tk_cv", "tk_exp")]
        row_in = [sem(f"row_in{r}") for r in range(R)]
        ring_used, ix_ready, xt_in, e_gelu, e_w, e_sq, e_ms, e_rt, e_y, y_out, e_w2 = [sem(n) for n in (
            "ring_used", "ix_ready", "xt_in", "e_gelu", "e_w", "e_sq", "e_ms", "e_rt", "e_y", "y_out", "e_w2")]

        passed, passed_dve, passed_sp = sem("passed"), sem("passed_dve"), sem("passed_sp")

        block = ctx.enter_context(nc.Block())

        def n_tr(g, s, ti):
            return 2 * norm_no[g, s, ti]

        def geometry(g, ti):
            tid, rows, _ = GROUPS[g][ti]
            return rows, (REACH + DEC if tid == SAMPLE else P * (min(tid, 4) + 1))

        def gate_product(g, s, c):
            return [n for n in by_stage[g, s] if products[n][4] == "gate" and (products[n][5] - 28) % 8 == c][0]

        def enter(eng, g, s):
            eng.wait_ge(bar_act, stage_no(g, s))
            eng.wait_ge(bar_dve, stage_no(g, s))

        k_tiles = {g: [ti for ti, (tid, _, _) in enumerate(GROUPS[g]) if tid >= 4] for g in range(NG)}
        kt_before = {g: sum(len(k_tiles[q]) for q in range(g)) + (4 if g > 0 else 0) for g in range(NG + 1)}
        x_tiles = {(g, s): 16 * (sum(2 * len(GROUPS[q]) for q in range(g)) + (2 if s == "H" else 1) * len(GROUPS[g]))
                   for g in range(NG) for s in "AH"}

        @block.sync
        def _(sp):
            with nc.allow_non_contiguous_dma(reason="small vectors laid over partitions"):
                sp.dma_start(gain_mix[:, :], norm_mix[0].rearrange("(k p) -> p k", p=P)).then_inc(const_in, 16)
                sp.dma_start(lbl[:, :, :], lb_logits.rearrange("a (h p) -> p a h", p=P)).then_inc(const_in, 16)
                sp.dma_start(rel[:, 383:767], bass.AP(rel_bias.tensor, NREL - 1, [[NREL, HA], [-1, 384]]))\
                  .then_inc(rel_in, 16)
            sp.dma_start(gain_ffn[:, :], bass.AP(norm_ffn.tensor, 0, [[0, P], [1, D]])).then_inc(const_in, 16)
            sp.dma_start(gain_final[:, :], bass.AP(norm_final.tensor, 0, [[0, P], [1, D]])).then_inc(const_in, 16)
            sp.dma_start(gain_hgrn[:, :], bass.AP(hgrn_norm.tensor, 0, [[0, P], [1, DA]])).then_inc(const_in, 16)
            sp.dma_start(sk, sub_keys[0].rearrange("a h k d -> k (a h) d")).then_inc(sk_in, 16)
            sp.dma_start(S_tile[:, :, 1, :], state_in[0, 0].rearrange("h k v -> k h v")).then_inc(state_loaded, 16)
            sp.wait_ge(relE, 1)
            lines = rel[:, 0:767]
            sp.dma_start(rel_scr, bass.AP(lines.tensor, lines.offset + 127, [list(lines.ap[0]), [-1, P], [1, WIN]]))\
              .then_inc(rel_out, 16)
            sp.wait_ge(sk_cp, 4)
            sp.dma_start(sk_scr, skTs.rearrange("p a b -> p (a b)")).then_inc(sk_out, 16)
            sp.wait_ge(rel_out, 16)
            sp.wait_ge(sk_out, 16)

            def load_weights(b):
                w, nk, c0, n = blocks[b]
                if b >= 2:
                    sp.wait_ge(pj_ready, last_product[b - 2] + 1)
                sp.dma_start(wring[:, b % 2, 0:nk * n].rearrange("p (k n) -> p k n", k=nk),
                             weights[w].rearrange("(k p) n -> p k n", p=P)[:, :, c0:c0 + n])\
                  .then_inc(w_in_sem[b % 2], 16)

            def load_stage(g, s):
                for b in sorted({products[n][2] for n in by_stage.get((g, s), [])}):
                    load_weights(b)

            for g, tiles in enumerate(GROUPS):
                enter(sp, g, "A")
                for ti, (tid, rows, _) in enumerate(tiles):
                    sp.dma_start(hx[0:rows, ti, :], rows_of(xp, xs, tid)).then_inc(x_in, 16)
                load_stage(g, "B")
                if g == 0:
                    enter(sp, g, "B")
                    sp.dma_start(kc, cache_k[0, 0].rearrange("(t p) h d -> p t (h d)", p=P)).then_inc(kc_in, 16)
                    sp.dma_start(v[:, 4:8, :], cache_v[0, 0].rearrange("(t p) h d -> p t (h d)", p=P))\
                      .then_inc(vc_in, 16)
                enter(sp, g, "C")
                for ti in k_tiles[g]:
                    tid, rows, _ = tiles[ti]
                    ko = k_sample[0, 0] if tid == SAMPLE else k_prompt[0, 0, (tid - 4) * P:(tid - 3) * P]
                    vo = v_sample[0, 0] if tid == SAMPLE else v_prompt[0, 0, (tid - 4) * P:(tid - 3) * P]
                    sp.dma_start(ko.rearrange("t h d -> t (h d)"), T2[0:rows, ti, :]).then_inc(kv_out, 16)
                    vt = vS[0:rows, :] if tid == SAMPLE else v[:, tid, :]
                    sp.dma_start(vo.rearrange("t h d -> t (h d)"), vt).then_inc(kv_out, 16)
                for h in range(HA):
                    bh = g * HA + h
                    if bh >= 2:
                        q = att_no[((bh - 2) // HA, (bh - 2) % HA, len(GROUPS[(bh - 2) // HA]) - 1)]
                        sp.wait_ge(at_biased, q + 1)
                    for t0, j0 in ((0, 0), (64, 64)):
                        sp.dma_start(bias[t0:t0 + 64, bh % 2, j0:j0 + 576], rel_scr[h, t0:t0 + 64, j0:j0 + 576])\
                          .then_inc(bias_in[bh % 2], 16)
                load_stage(g, "D")
                load_stage(g, "E")
                if g == 0:
                    sp.wait_ge(hg_S, HB)
                    sp.dma_start(state_sample[0, 0].rearrange("h k v -> k h v"), S_mid[:, :, :]).then_inc(st_out, 16)
                load_stage(g, "G")
                enter(sp, g, "H")
                for ti, (tid, rows, _) in enumerate(tiles):
                    sp.dma_start(hx[0:rows, ti, :], rows_of(xp, xs, tid)).then_inc(x_in, 16)
                load_stage(g, "H")
                enter(sp, g, "I")
                sp.dma_start(skT, sk_scr).then_inc(skT_in, 16)
                for ti, (tid, rows, _) in enumerate(tiles):
                    sp.dma_start(h_scr[tid * P:tid * P + rows, :], hx[0:rows, ti, :]).then_inc(h_out, 16)
                    sp.dma_start(xn_scr[tid * P:tid * P + rows, :], xn[0:rows, ti, :]).then_inc(h_out, 16)
                load_stage(g, "I")
            sp.wait_ge(hg_S, HB * 9)
            sp.dma_start(state_prompt[0, 0].rearrange("h k v -> k h v"), S_tile[:, :, 0, :]).then_inc(st_out, 16)
            sp.wait_ge(h_out, 32 * 9)

            def tile_io(it, rows, dst):
                at = it * P
                sp.dma_start(xt[0:rows, :], xn_scr[bass.ds(at, rows), :]).then_inc(xt_in, 16)
                sp.dma_start(acc[0:rows, :], h_scr[bass.ds(at, rows), :]).then_inc(xt_in, 16)
                sp.wait_ge(e_y, it + 1)
                sp.dma_start(dst, xt[0:rows, :]).then_inc(y_out, 16)
                sp.wait_ge(y_out, 16 * it + 16)
                sp.sem_inc(passed_sp, 1)

            with sp.Fori(0, 8) as it:
                tile_io(it, P, y_prompt[0][bass.ds(it * P, P), :])
            tile_io(8, DEC, y_sample[0])
            sp.wait_ge(kv_out, 32 * 5)
            sp.wait_ge(st_out, 32)

        @block.gpsimd
        def _(pool):
            pool.memset(ident[:, :], 0.0).then_inc(consts, 1)
            pool.memset(masks[:, :, :], 0.0).then_inc(consts, 1)
            for lev, s in enumerate(LEVELS):
                pool.wait_ge(consts, 2 + lev)
                pool.memset(masks[:, lev, :].rearrange("p (b t s) -> p b t s", t=2, s=s)[:, :, 1, :], 1.0)\
                    .then_inc(consts, 1)
            pool.wait_ge(consts, 8)
            n = 8
            for m in (ident[:, :], masks[:, NL, :]):
                pool.affine_select(out=m, in_=m, compare_op=ALU.not_equal, fill=1.0, base=0,
                                   pattern=[[-1, P]], channel_multiplier=1).then_inc(consts, 1)
                n += 1
            for lev, s in enumerate(LEVELS):
                m = masks[:, lev, :].rearrange("p (b w) -> p b w", w=2 * s)
                nb = P // (2 * s)
                pool.affine_select(out=m, in_=m, compare_op=ALU.is_ge, fill=0.0, base=0,
                                   pattern=[[-2 * s, nb], [0, 2 * s]], channel_multiplier=1).then_inc(consts, 1)
                n += 1
            for lev, s in enumerate(LEVELS):
                m = masks[:, lev, :].rearrange("p (b w) -> p b w", w=2 * s)
                nb = P // (2 * s)
                pool.wait_ge(consts, n)
                pool.affine_select(out=m, in_=m, compare_op=ALU.is_ge, fill=0.0, base=s - 1,
                                   pattern=[[2 * s, nb], [0, 2 * s]], channel_multiplier=-1).then_inc(consts, 1)
                n += 1
            pool.iota(iota16[:, :], pattern=[[1, TOPK]], base=0, channel_multiplier=0,
                      allow_small_or_imprecise_dtypes=True).then_inc(consts, 1)

            def gathers(q, rows):
                for half, table in ((0, u_tab), (1, v_tab)):
                    pool.tensor_copy(ixs[0:rows, half, :], idx[0:rows, bass.ds(q * TOPK, TOPK)]).then_inc(ix_ready, 1)
                    pool.wait_ge(ix_ready, 2 * q + half + 1)
                    for k in range(TOPK):
                        j = half * TOPK + k
                        pool.wait_ge(ring_used, q * 32 + j + 1)
                        pool.sem_inc(passed, 1)
                        pool.indirect_dma_start(
                            ring[0:rows, j % R, :], None, table,
                            bass.IndirectOffsetOnAxis(ap=ixs[0:rows, half, k:k + 1], axis=0))\
                            .then_inc(row_in[j % R], 16)

            pool.wait_ge(bar_dve, stage_no(NG, "A"))
            with pool.Fori(0, 64) as q:
                gathers(q, P)
            for h in range(PH):
                gathers(64 + h, DEC)

        @block.tensor
        def _(pe):
            def product(n, act_in):
                g, _, b, kind, what, _, s, ti = products[n]
                _, nk, _, ncol = blocks[b]
                w = wring[:, b % 2, 0:nk * ncol].rearrange("p (k n) -> p k n", k=nk)
                pe.wait_ge(w_in_sem[b % 2], 16 * (b // 2 + 1))
                if n >= 2:
                    pe.wait_ge(pj_free[n % 2], n // 2)
                for k in range(nk):
                    if kind == "fm":
                        W = width(g)
                        mm = pe.matmul(PS[:, n % 2, 0:W], w[:, k, s * P:(s + 1) * P], act_in[:, k, 0:W],
                                       start=(k == 0), stop=(k == nk - 1))
                    else:
                        _, rows, c0 = GROUPS[g][ti]
                        mm = pe.matmul(PS[0:rows, n % 2, 0:ncol], act_in[:, k, c0:c0 + rows], w[:, k, :],
                                       start=(k == 0), stop=(k == nk - 1))
                mm.then_inc(pj_ready, 1)

            def transpose_norm(g, s, source_sem):
                for ti, (tid, rows, c0) in enumerate(GROUPS[g]):
                    pe.wait_ge(source_sem, norm_no[g, s, ti] + 1)
                    for half in range(2):
                        m = n_tr(g, s, ti) + half
                        if m >= 4:
                            pe.wait_ge(tr_free, m - 3)
                        for k in range(4):
                            kk = 4 * half + k
                            mm = pe.transpose(PS[:, m % 4, k * P:k * P + rows], xn[0:rows, ti, kk * P:(kk + 1) * P],
                                              ident[0:rows, 0:rows])
                        mm.then_inc(tr_ready, 1)

            pe.wait_ge(consts, 23)
            pe.wait_ge(sk_in, 16)
            for b in range(4):
                for k in range(4):
                    mm = pe.transpose(PS[:, b, k * P:(k + 1) * P], sk[:, 4 * b + k, :], ident[:, :])
                mm.then_inc(sk_tr, 1)

            for g, tiles in enumerate(GROUPS):
                nt = len(tiles)
                enter(pe, g, "A")
                transpose_norm(g, "A", xn_ready)
                enter(pe, g, "B")
                for n in by_stage[g, "B"]:
                    product(n, xnT)
                for n in by_stage[g, "B"][-2:]:
                    pe.wait_ge(pj_free[n % 2], n // 2 + 1)
                kt = kt_before[g]
                for i, ti in enumerate(k_tiles[g]):
                    tid, rows, c0 = tiles[ti]
                    src = kS if tid == SAMPLE else kT[:, :, tid * P:(tid + 1) * P]
                    for c in range(CB):
                        mm = pe.transpose(PS[0:rows, 2 + i, c * P:(c + 1) * P], src[:, c, 0:rows], ident[:, :])
                    mm.then_inc(kt_tr, 1)
                if g == 0:
                    pe.wait_ge(kc_in, 16)
                    for t in range(4):
                        for c in range(CB):
                            mm = pe.transpose(PS[:, 4 + t, c * P:(c + 1) * P], kc[:, t, c * P:(c + 1) * P], ident[:, :])
                        mm.then_inc(kt_tr, 1)
                enter(pe, g, "C")
                if g == 0:
                    pe.wait_ge(vc_in, 16)
                steps = [s for s in att if s[0] == g]

                def keys_of(ti):
                    tid, rows, _ = tiles[ti]
                    if tid == SAMPLE:
                        return [(kT[:, :, REACH + t * P:REACH + (t + 1) * P], v[:, 4 + t, :], P) for t in range(4)] + [
                            (kS, vS, DEC)]
                    return [(kT[:, :, t * P:(t + 1) * P], v[:, t, :], P) for t in range(max(0, tid - 4), tid + 1)]

                def scores(step):
                    i = att_no[step]
                    _, h, ti = step
                    tid, rows, c0 = tiles[ti]
                    if i >= 2:
                        pe.wait_ge(at_biased, i - 1)
                    p0 = 64 * (h % 2)
                    q = Q[p0:p0 + 64, h // 2, c0:c0 + rows]
                    bank = 2 + 2 * (i % 2)
                    for n, (kk, _, nk) in enumerate(keys_of(ti)):
                        mm = pe.matmul(PS[0:rows, bank + n // 4, (n % 4) * P:(n % 4) * P + nk], q,
                                       kk[p0:p0 + 64, h // 2, 0:nk], start=True, stop=True)
                    mm.then_inc(at_sc, 1)

                def values(step):
                    i = att_no[step]
                    _, h, ti = step
                    tid, rows, c0 = tiles[ti]
                    pe.wait_ge(at_exp, i + 1)
                    if i >= 1:
                        pe.wait_ge(at_ptc, i)
                    kv = keys_of(ti)
                    for n, (_, _, nk) in enumerate(kv):
                        mm = pe.transpose(PS[0:nk, 6 + n // 4, (n % 4) * P:(n % 4) * P + rows],
                                          sc[0:rows, i % 2, n * P:n * P + nk], ident[0:rows, 0:rows])
                    mm.then_inc(at_pT, 1)
                    pe.wait_ge(at_ptc, i + 1)
                    if i >= 2:
                        pe.wait_ge(at_oa, i - 1)
                    for n, (_, vv, nk) in enumerate(kv):
                        mm = pe.matmul(PS[0:rows, i % 2, 0:64], pt[0:nk, i % 2, n * P:n * P + rows],
                                       vv[0:nk, h * 64:(h + 1) * 64], start=(n == 0), stop=(n == len(kv) - 1))
                    mm.then_inc(at_pv, 1)

                scores(steps[0])
                for a, b in zip(steps, steps[1:] + [None]):
                    if b:
                        scores(b)
                    values(a)
                enter(pe, g, "D")
                for ti, (tid, rows, c0) in enumerate(tiles):
                    for c in range(CB):
                        mm = pe.transpose(PS[:, 2 + ti, c * P:c * P + rows], T1[0:rows, ti, c * P:(c + 1) * P],
                                          ident[0:rows, 0:rows])
                    mm.then_inc(oT_tr, 1)
                pe.wait_ge(oT_cp, tile_no[g, nt - 1] + 1)
                for n in by_stage[g, "D"]:
                    product(n, Q if products[n][4] == "branch" else xnT)
                enter(pe, g, "E")
                for n in by_stage[g, "E"]:
                    product(n, xnT)
                enter(pe, g, "F")
                pe.wait_ge(state_loaded, 16)
                for ti, (tid, rows, c0) in enumerate(tiles):
                    ft = tile_no[g, ti]
                    nch = rows // CH
                    pe.wait_ge(hg_kq, ft + 1)
                    for h in range(HB):
                        fh = ft * HB + h
                        if fh >= 1:
                            pe.wait_ge(hg_kdc, fh)
                        if h == 0 and ft >= 1:
                            pe.wait_ge(hg_obc, ft)
                        pe.transpose(PS[0:rows, 5, 0:P], E[:, NL, h, 0:rows], ident[:, :]).then_inc(hg_kdT, 1)
                        pe.wait_ge(hg_L, fh + 1)
                        if fh >= 2:
                            pe.wait_ge(hg_red, fh - 1)
                        b0 = 2 * (fh % 2)
                        for lev in range(NL):
                            pe.matmul(PS[0:rows, b0 + lev // 4, (lev % 4) * P:(lev % 4) * P + rows],
                                      Lk[:, lev, 0:rows], Lq[:, lev, 0:rows], start=True, stop=True)
                        pe.matmul(PS[0:rows, b0 + 1, 2 * P:2 * P + rows], K2[:, h, c0:c0 + rows],
                                  Q2[:, h, c0:c0 + rows], start=True, stop=True).then_inc(hg_at, 1)
                        pe.wait_ge(hg_kdc, fh + 1)
                        if fh >= 1:
                            pe.wait_ge(hg_S, fh)
                        for c in range(nch):
                            mm = pe.matmul(PS[:, 6 + c, 0:P], kdT[c * CH:(c + 1) * CH, :],
                                           T1[c * CH:(c + 1) * CH, ti, h * P:(h + 1) * P], start=True, stop=True)
                        mm.then_inc(hg_st, 1)
                        pe.wait_ge(hg_red, fh + 1)
                        if fh >= 1:
                            pe.wait_ge(hg_oc, fh)
                        pe.matmul(PS[0:rows, 4, 0:P], attnT[0:rows, fh % 2, 0:rows], T1[0:rows, ti, h * P:(h + 1) * P],
                                  start=True, stop=True, skip_group_check=True)
                        pe.wait_ge(hg_S, fh + 1)
                        s_in = S_tile[:, h, 1 if tid == SAMPLE else tid % 2, :]
                        for c in range(nch):
                            mm = pe.matmul(PS[c * CH:(c + 1) * CH, 4, 0:P], ecum[:, h, c * CH:(c + 1) * CH],
                                           s_in if c == 0 else S_mid[:, h, :], start=False, stop=True,
                                           skip_group_check=True)
                        mm.then_inc(hg_o, 1)
                    pe.wait_ge(hg_ob, ft + 1)
                    pe.wait_ge(hg_kdc, 4 * ft + 4)
                    for h in range(HB):
                        mm = pe.transpose(PS[:, 5, h * P:h * P + rows], ob[0:rows, h, :], ident[0:rows, 0:rows])
                    mm.then_inc(hg_oT, 1)
                enter(pe, g, "G")
                for n in by_stage[g, "G"]:
                    product(n, Q2 if products[n][4] == "branch" else xnT)
                enter(pe, g, "H")
                for n in by_stage[g, "H"]:
                    product(n, M)
                transpose_norm(g, "H", xn_ready)
                enter(pe, g, "I")
                pe.wait_ge(skT_in, 16 * (g + 1))
                qn = by_stage[g, "I"]

                def key_scores(h):
                    for n in qn[2 * h:2 * h + 2]:
                        pe.wait_ge(pj_free[n % 2], n // 2 + 1)
                    for ti, (tid, rows, c0) in enumerate(tiles):
                        o = top_no[g, h, ti]
                        if o >= 2:
                            pe.wait_ge(tk_cp, o - 1)
                        for p in range(2):
                            mm = pe.matmul(PS[0:rows, 2 + o % 2, p * P:(p + 1) * P], qp[:, h % 2, p, c0:c0 + rows],
                                           skT[:, (p * PH + h) * P:(p * PH + h + 1) * P], start=True, stop=True)
                        mm.then_inc(tk_sc, 1)

                for h in range(PH + 1):
                    if h < PH:
                        product(qn[2 * h], xnT)
                        product(qn[2 * h + 1], xnT)
                    if h >= 1:
                        key_scores(h - 1)

        @block.scalar
        def _(act):
            def leave():
                act.activation(mark_a[:, :], ident[:, 0:1], ACT.Copy).then_inc(bar_act, 1)

            act.wait_ge(consts, 23)
            act.wait_ge(lb_d, 1)
            act.activation(lb[:, :], lbl[:, 0, :], ACT.Sigmoid).then_inc(lb_a, 1)
            for b in range(4):
                act.wait_ge(sk_tr, b + 1)
                act.activation(skTs[:, 4 * b:4 * b + 4, :], PS[:, b, :].rearrange("p (a b) -> p a b", a=4), ACT.Copy)\
                   .then_inc(sk_cp, 1)
            act.wait_ge(sk_out, 16)
            act.wait_ge(rel_out, 16)
            leave()

            def norm_tiles(g, s):
                tiles = GROUPS[g]
                for ti, (tid, rows, c0) in enumerate(tiles):
                    act.activation(xn[0:rows, ti, :], hx[0:rows, ti, :], ACT.Square,
                                   accum_out=ss[0:rows, ti:ti + 1]).then_inc(n_sq, 1)
                act.wait_ge(n_ms, norm_batch[g, s] + 1)
                act.activation(rstd[:, 0:3], ss[:, 0:3], ACT.Sqrt).then_inc(n_rt, 1)

            def sigmoid_gates(g, s, W):
                for n in by_stage[g, s]:
                    if products[n][4] == "gate":
                        act.wait_ge(pj_ready, n + 1)
                        act.activation(sg[:, (products[n][5] - 28) % 8, 0:W], PS[:, n % 2, 0:W], ACT.Sigmoid)\
                           .then_inc(pj_free[n % 2], 1)

            for g, tiles in enumerate(GROUPS):
                W = width(g)
                enter(act, g, "A")
                act.wait_ge(x_in, x_tiles[g, "A"])
                norm_tiles(g, "A")
                for ti, (tid, rows, c0) in enumerate(tiles):
                    for half in range(2):
                        m = n_tr(g, "A", ti) + half
                        act.wait_ge(tr_ready, m + 1)
                        for k in range(4):
                            kk = 4 * half + k
                            i = act.activation(xnT[:, kk, c0:c0 + rows], PS[:, m % 4, k * P:k * P + rows], ACT.Copy,
                                               scale=gain_mix[:, kk:kk + 1])
                        i.then_inc(tr_free, 1)
                leave()

                enter(act, g, "B")
                for n in by_stage[g, "B"]:
                    _, _, b, kind, what, c, s, ti = products[n]
                    act.wait_ge(pj_ready, n + 1)
                    if what == "q":
                        i = act.activation(Q[:, c, 0:W], PS[:, n % 2, 0:W], ACT.Copy)
                    elif what == "k":
                        c -= 4
                        first = 0
                        if g == 0:
                            act.activation(kS[:, c, :], PS[:, n % 2, 0:DEC], ACT.Copy)
                            first = DEC
                        t0 = tiles[-2][0] * P
                        i = act.activation(kT[:, c, t0:t0 + 256], PS[:, n % 2, first:W], ACT.Copy)
                    else:
                        tid, rows, _ = tiles[ti]
                        dst = vS if tid == SAMPLE else v[:, tid, :]
                        i = act.activation(dst[0:rows, c - 1024:c - 768], PS[0:rows, n % 2, 0:256], ACT.Copy)
                    i.then_inc(pj_free[n % 2], 1)
                kt = kt_before[g]
                for i_, ti in enumerate(k_tiles[g]):
                    tid, rows, _ = tiles[ti]
                    act.wait_ge(kt_tr, kt + i_ + 1)
                    act.activation(T2[0:rows, ti, :], PS[0:rows, 2 + i_, :], ACT.Copy).then_inc(kt_cp, 1)
                if g == 0:
                    for t in range(4):
                        act.wait_ge(kt_tr, kt + len(k_tiles[g]) + t + 1)
                        act.activation(kT[:, :, REACH + t * P:REACH + (t + 1) * P],
                                       PS[:, 4 + t, :].rearrange("p (c t) -> p c t", c=CB), ACT.Copy).then_inc(kt_cp, 1)
                leave()

                enter(act, g, "C")

                def exps(i, step):
                    _, h, ti = step
                    rows, w = geometry(g, ti)
                    act.wait_ge(at_max, i + 1)
                    act.activation(sc[0:rows, i % 2, 0:w], sc[0:rows, i % 2, 0:w], ACT.Exp,
                                   bias=nmax[0:rows, i % 2:i % 2 + 1],
                                   accum_out=rsum[0:rows, i % 2:i % 2 + 1]).then_inc(at_exp, 1)

                def turned(i, step):
                    _, h, ti = step
                    rows, w = geometry(g, ti)
                    act.wait_ge(at_pT, i + 1)
                    if i >= 2:
                        act.wait_ge(at_pv, i - 1)
                    flat = PS[:, 6:8, :].rearrange("p a b -> p (a b)")
                    if rows == P:
                        j = act.activation(pt[:, i % 2, 0:w], flat[:, 0:w], ACT.Copy)
                    else:
                        act.activation(pt[:, i % 2, 0:512].rearrange("p (a b) -> p a b", b=P)[:, :, 0:rows],
                                       flat[:, 0:512].rearrange("p (a b) -> p a b", b=P)[:, :, 0:rows], ACT.Copy)
                        j = act.activation(pt[0:DEC, i % 2, 512:512 + rows], flat[0:DEC, 512:512 + rows], ACT.Copy)
                    j.then_inc(at_ptc, 1)

                prev = None
                for step in [s for s in att if s[0] == g] + [None]:
                    if step:
                        exps(att_no[step], step)
                    if prev:
                        turned(att_no[prev], prev)
                    prev = step
                leave()

                enter(act, g, "D")
                for ti, (tid, rows, c0) in enumerate(tiles):
                    act.wait_ge(oT_tr, tile_no[g, ti] + 1)
                    act.activation(Q[:, :, c0:c0 + rows],
                                   PS[:, 2 + ti, :].rearrange("p (c t) -> p c t", c=CB)[:, :, 0:rows], ACT.Copy)\
                       .then_inc(oT_cp, 1)
                sigmoid_gates(g, "D", W)
                leave()

                enter(act, g, "E")
                if any(k_tiles[q] for q in range(g + 1)):
                    act.wait_ge(kv_out, 32 * sum(len(k_tiles[q]) for q in range(g + 1)))
                for n in by_stage[g, "E"]:
                    _, _, b, kind, what, c, s, ti = products[n]
                    act.wait_ge(pj_ready, n + 1)
                    if what == "f":
                        i = act.activation(Q[:, c - 12, 0:W], PS[:, n % 2, 0:W], ACT.Sigmoid)
                    elif what == "qb":
                        i = act.activation(Q2[:, c - 20, 0:W], PS[:, n % 2, 0:W], ACT.Silu)
                    elif what == "i":
                        rows = tiles[ti][1]
                        i = act.activation(T1[0:rows, ti, c - 2048:c - 1792], PS[0:rows, n % 2, 0:256], ACT.Copy)
                    else:
                        rows = tiles[ti][1]
                        i = act.activation(T2[0:rows, ti, c - 3072:c - 2816], PS[0:rows, n % 2, 0:256], ACT.Silu)
                    i.then_inc(pj_free[n % 2], 1)
                act.wait_ge(f_fg, g + 1)
                act.activation(Q[:, :, 0:W], K2[:, :, 0:W], ACT.Ln).then_inc(f_ln, 1)
                leave()

                enter(act, g, "F")
                for ti, (tid, rows, c0) in enumerate(tiles):
                    ft = tile_no[g, ti]
                    act.wait_ge(hg_D, ft + 1)
                    view = E[:, :, :, :].rearrange("p l h t -> p (l h) t")[:, :, 0:rows]
                    act.activation(view, view, ACT.Exp)
                    act.activation(ecum[:, :, 0:rows], Q[:, :, c0:c0 + rows], ACT.Exp).then_inc(hg_E, 1)
                    for h in range(HB):
                        fh = ft * HB + h
                        act.wait_ge(hg_kdT, fh + 1)
                        if fh >= 1:
                            act.wait_ge(hg_st, fh)
                        act.activation(kdT[0:rows, :], PS[0:rows, 5, 0:P], ACT.Copy).then_inc(hg_kdc, 1)
                        act.wait_ge(hg_o, fh + 1)
                        if h == 0 and ft >= 1:
                            act.wait_ge(hg_oT, ft)
                        act.activation(ob[0:rows, h, :], PS[0:rows, 4, 0:P], ACT.Copy)
                        if fh >= 1:
                            act.wait_ge(hg_oc, fh)
                        act.activation(junk[0:rows, :], PS[0:rows, 4, 0:P], ACT.Square,
                                       accum_out=ssq[0:rows, h:h + 1]).then_inc(hg_oc, 1)
                    act.wait_ge(hg_ms, ft + 1)
                    act.activation(rsq[0:rows, :], ssq[0:rows, :], ACT.Sqrt).then_inc(hg_rt, 1)
                    act.wait_ge(hg_oT, ft + 1)
                    act.activation(Q2[:, :, c0:c0 + rows],
                                   PS[:, 5, :].rearrange("p (c t) -> p c t", c=CB)[:, :, 0:rows], ACT.Copy)\
                       .then_inc(hg_obc, 1)
                leave()

                enter(act, g, "G")
                sigmoid_gates(g, "G", W)
                leave()

                enter(act, g, "H")
                for n in by_stage[g, "H"][-2:]:
                    act.wait_ge(pj_free[n % 2], n // 2 + 1)
                norm_tiles(g, "H")
                for ti, (tid, rows, c0) in enumerate(tiles):
                    for half in range(2):
                        m = n_tr(g, "H", ti) + half
                        act.wait_ge(tr_ready, m + 1)
                        act.activation(xnT[:, 4 * half:4 * half + 4, c0:c0 + rows],
                                       PS[:, m % 4, :].rearrange("p (c t) -> p c t", c=4)[:, :, 0:rows], ACT.Copy)\
                           .then_inc(tr_free, 1)
                leave()

                enter(act, g, "I")
                act.wait_ge(h_out, 32 * (tile_no[g, len(tiles) - 1] + 1))
                qn = by_stage[g, "I"]

                def softmax_exps(o, rows):
                    act.wait_ge(tk_cv, o + 1)
                    act.activation(ge[0:rows, :], cv[0:rows, :], ACT.Exp, bias=ncv[0:rows, :],
                                   accum_out=gsum[0:rows, :]).then_inc(tk_exp, 1)

                for h in range(PH + 1):
                    if h < PH:
                        for p in range(2):
                            n = qn[2 * h + p]
                            act.wait_ge(pj_ready, n + 1)
                            if h >= 2:
                                act.wait_ge(tk_sc, top_no[g, h - 2, len(tiles) - 1] + 1)
                            act.activation(qp[:, h % 2, p, 0:W], PS[:, n % 2, 0:W], ACT.Copy).then_inc(pj_free[n % 2], 1)
                    if h >= 1:
                        for ti, (tid, rows, c0) in enumerate(tiles):
                            o = top_no[g, h - 1, ti]
                            act.wait_ge(tk_sc, o + 1)
                            if o >= 2:
                                act.wait_ge(tk_done, o - 1)
                            act.activation(s1[0:rows, o % 2], PS[0:rows, 2 + o % 2, 0:2 * P]
                                           .rearrange("p (a b) -> p a b", a=2), ACT.Copy).then_inc(tk_cp, 1)
                            if ti >= 1 or h >= 2:
                                softmax_exps(o - 1, tiles[ti - 1][1])
                o = top_no[g, PH - 1, len(tiles) - 1]
                softmax_exps(o, tiles[-1][1])
                leave()

            def expert_head(q, rows):
                act.wait_ge(ring_used, q * 32 + R + 16)
                act.activation(glu[0:rows, :], hid[0:rows, :], ACT.Gelu).then_inc(e_gelu, 1)

            def tile_end(it, rows):
                act.wait_ge(ring_used, it * 256 + R + 256)
                act.activation(xt[0:rows, :], acc[0:rows, :], ACT.Square, accum_out=ss[0:rows, 4:5]).then_inc(e_sq, 1)
                act.wait_ge(e_ms, it + 1)
                act.activation(rstd[0:rows, 4:5], ss[0:rows, 4:5], ACT.Sqrt).then_inc(e_rt, 1)

            with act.Fori(0, 8) as it:
                with act.Fori(0, PH) as h:
                    expert_head(it * PH + h, P)
                tile_end(it, P)
            for h in range(PH):
                expert_head(64 + h, DEC)
            tile_end(8, DEC)

        @block.vector
        def _(dve):
            chain = [0]

            def link(ins):
                chain[0] += 1
                ins.then_inc(dve_chain, 1)
                dve.wait_ge(dve_chain, chain[0])

            def leave():
                dve.memset(mark_d[:, :], 0.0).then_inc(bar_dve, 1)

            dve.wait_ge(rel_in, 16)
            dve.tensor_copy(rel[:, 0:383], rel[:, 383:384].to_broadcast([HA, 383])).then_inc(relE, 1)
            dve.memset(bias[:, :, :], NEG)
            dve.memset(S_tile[:, :, 0, :], 0.0)
            dve.memset(ss[:, :], 1.0)
            dve.memset(restart[:, :], 1.0).then_inc(dve_chain, 1)
            chain[0] += 1
            dve.wait_ge(dve_chain, chain[0])
            link(dve.memset(restart[:, :].rearrange("p (c t) -> p c t", t=CH)[:, :, 0:1], 0.0))
            dve.wait_ge(const_in, 80)
            dve.tensor_tensor(lbl[:, 0, :], lbl[:, 0, :], lbl[:, 1, :], ALU.subtract).then_inc(lb_d, 1)
            dve.wait_ge(lb_a, 1)
            link(dve.tensor_scalar(one_lb[:, :], lb[:, :], -1.0, 1.0, ALU.mult, ALU.add))
            leave()

            def norm_scale(g, s):
                tiles = GROUPS[g]
                dve.wait_ge(n_sq, norm_no[g, s, len(tiles) - 1] + 1)
                dve.tensor_scalar(ss[:, 0:3], ss[:, 0:3], 1.0 / D, EPS, ALU.mult, ALU.add).then_inc(n_ms, 1)
                dve.wait_ge(n_rt, norm_batch[g, s] + 1)
                link(dve.reciprocal(rstd[:, 0:3], rstd[:, 0:3]))

            def gated(g, stage, W):
                for n in by_stage[g, stage]:
                    _, _, b, kind, what, c, s, ti = products[n]
                    if what != "branch":
                        continue
                    dve.wait_ge(pj_ready, n + 1)
                    gn = gate_product(g, stage, c)
                    dve.wait_ge(pj_free[gn % 2], gn // 2 + 1)
                    if stage == "D":
                        dve.tensor_tensor(M[:, c, 0:W], PS[:, n % 2, 0:W], sg[:, c, 0:W], ALU.mult)\
                           .then_inc(pj_free[n % 2], 1)
                    else:
                        dve.tensor_tensor(sg[:, c, 0:W], PS[:, n % 2, 0:W], sg[:, c, 0:W], ALU.mult)\
                           .then_inc(pj_free[n % 2], 1)
                        dve.wait_ge(pj_free[n % 2], n // 2 + 1)
                        dve.tensor_tensor(M[:, c, 0:W], M[:, c, 0:W], sg[:, c, 0:W], ALU.add)

            for g, tiles in enumerate(GROUPS):
                W = width(g)
                nt = len(tiles)
                enter(dve, g, "A")
                norm_scale(g, "A")
                for ti, (tid, rows, c0) in enumerate(tiles):
                    dve.tensor_scalar(xn[0:rows, ti, :], hx[0:rows, ti, :], rstd[0:rows, ti:ti + 1], None, ALU.mult)\
                       .then_inc(xn_ready, 1)
                leave()
                enter(dve, g, "B")
                leave()

                enter(dve, g, "C")

                def bias_max(i, step):
                    _, h, ti = step
                    rows, w = geometry(g, ti)
                    bh = g * HA + h
                    dve.wait_ge(at_sc, i + 1)
                    dve.wait_ge(bias_in[bh % 2], 32 * (bh // 2 + 1))
                    if i >= 2:
                        dve.wait_ge(at_pT, i - 1)
                    b0 = 2 + 2 * (i % 2)
                    flat = PS[:, b0:b0 + 2, :].rearrange("p a b -> p (a b)")
                    off = WIN - w if rows == P else 0
                    dve.scalar_tensor_tensor(out=sc[0:rows, i % 2, 0:w], in0=flat[0:rows, 0:w], scalar=SCALE,
                                             in1=bias[0:rows, bh % 2, off:off + w], op0=ALU.mult, op1=ALU.add)\
                       .then_inc(at_biased, 1)
                    dve.wait_ge(at_biased, i + 1)
                    if i >= 2:
                        dve.wait_ge(at_exp, i - 1)
                    dve.tensor_reduce(nmax[0:rows, i % 2:i % 2 + 1], sc[0:rows, i % 2, 0:w], AX, ALU.max,
                                      negate=True).then_inc(at_max, 1)

                def scale_out(i, step):
                    _, h, ti = step
                    rows, w = geometry(g, ti)
                    dve.wait_ge(at_exp, i + 1)
                    dve.reciprocal(rinv[0:rows, i % 2:i % 2 + 1], rsum[0:rows, i % 2:i % 2 + 1]).then_inc(at_rinv, 1)
                    dve.wait_ge(at_rinv, i + 1)
                    dve.wait_ge(at_pv, i + 1)
                    dve.tensor_scalar(T1[0:rows, ti, h * 64:(h + 1) * 64], PS[0:rows, i % 2, 0:64],
                                      rinv[0:rows, i % 2:i % 2 + 1], None, ALU.mult).then_inc(at_oa, 1)

                prev = None
                for step in [s for s in att if s[0] == g] + [None]:
                    if step:
                        bias_max(att_no[step], step)
                    if prev:
                        scale_out(att_no[prev], prev)
                    prev = step
                leave()

                enter(dve, g, "D")
                gated(g, "D", W)
                leave()

                enter(dve, g, "E")
                fn = [n for n in by_stage[g, "E"] if products[n][4] == "f"]
                for h, n in enumerate(fn):
                    dve.wait_ge(pj_free[n % 2], n // 2 + 1)
                    i = dve.tensor_scalar(K2[:, h, 0:W], Q[:, h, 0:W], one_lb[:, h:h + 1], lb[:, h:h + 1],
                                          ALU.mult, ALU.add)
                i.then_inc(f_fg, 1)
                gn = [n for n in by_stage[g, "E"] if products[n][4] == "g"]
                for n in gn[-2:]:
                    dve.wait_ge(pj_free[n % 2], n // 2 + 1)
                for ti, (tid, rows, c0) in enumerate(tiles):
                    dve.tensor_tensor(T2[0:rows, ti, :], T2[0:rows, ti, :], gain_hgrn[0:rows, :], ALU.mult)
                dve.wait_ge(f_ln, g + 1)
                link(dve.tensor_scalar(K2[:, :, 0:W], K2[:, :, 0:W], -1.0, 1.0, ALU.mult, ALU.add))
                for h in range(HB):
                    dve.tensor_tensor_scan(Q[:, h, 0:W], restart[:, 0:W], Q[:, h, 0:W], 0.0, ALU.mult, ALU.add)
                leave()

                enter(dve, g, "F")
                dve.wait_ge(state_loaded, 16)
                for ti, (tid, rows, c0) in enumerate(tiles):
                    ft = tile_no[g, ti]
                    nch = rows // CH
                    if ft >= 1:
                        dve.wait_ge(hg_o, HB * ft)
                    cum = Q[:, :, c0:c0 + rows]
                    for lev, s in enumerate(LEVELS):
                        nb = rows // (2 * s)
                        c4 = cum.rearrange("p h (b t s) -> p h b t s", t=2, s=s)
                        e4 = E[:, lev, :, 0:rows].rearrange("p h (b t s) -> p h b t s", t=2, s=s)
                        ref = c4[:, :, :, 0, s - 1:s].to_broadcast([P, HB, nb, s])
                        dve.tensor_tensor(e4[:, :, :, 1, :], c4[:, :, :, 1, :], ref, ALU.subtract)
                        dve.tensor_tensor(e4[:, :, :, 0, :], ref, c4[:, :, :, 0, :], ALU.subtract)
                    c3 = cum.rearrange("p h (b s) -> p h b s", s=CH)
                    dve.tensor_tensor(E[:, NL, :, 0:rows].rearrange("p h (b s) -> p h b s", s=CH),
                                      c3[:, :, :, CH - 1:CH].to_broadcast([P, HB, nch, CH]), c3,
                                      ALU.subtract).then_inc(hg_D, 1)
                    dve.wait_ge(hg_E, ft + 1)
                    link(dve.tensor_copy(elast[:, :, 0:nch], ecum[:, :, CH - 1:rows:CH]))
                    dve.tensor_tensor(E[:, NL, :, 0:rows], E[:, NL, :, 0:rows], K2[:, :, c0:c0 + rows], ALU.mult)
                    dve.tensor_tensor(ecum[:, :, 0:rows], ecum[:, :, 0:rows], Q2[:, :, c0:c0 + rows], ALU.mult)\
                       .then_inc(hg_kq, 1)
                    for h in range(HB):
                        fh = ft * HB + h
                        if fh >= 1:
                            dve.wait_ge(hg_at, fh)
                        dve.tensor_tensor(Lq[:, :, 0:rows], E[:, 0:NL, h, 0:rows],
                                          Q2[:, h:h + 1, c0:c0 + rows].to_broadcast([P, NL, rows]), ALU.mult)
                        dve.tensor_tensor(Lk[:, :, 0:rows], E[:, 0:NL, h, 0:rows],
                                          K2[:, h:h + 1, c0:c0 + rows].to_broadcast([P, NL, rows]), ALU.mult)\
                           .then_inc(hg_L, 1)
                        dve.wait_ge(hg_at, fh + 1)
                        b0 = 2 * (fh % 2)
                        at = PS[:, b0:b0 + 2, :].rearrange("p a (b t) -> p (a b) t", t=P)[0:rows, 0:NL + 1, 0:rows]
                        link(dve.tensor_tensor(Am[0:rows, :, 0:rows], at, masks[0:rows, :, 0:rows], ALU.mult))
                        if fh >= 2:
                            dve.wait_ge(hg_o, fh - 1)
                        dve.tensor_reduce(attnT[0:rows, fh % 2, 0:rows],
                                          Am[0:rows, :, 0:rows].rearrange("p l t -> p t l"), AX, ALU.add)\
                           .then_inc(hg_red, 1)
                        dve.wait_ge(hg_st, fh + 1)
                        if ft >= 1:
                            dve.wait_ge(hg_o, fh - 3)
                        if ft == 1:
                            dve.wait_ge(st_out, 16)
                        s_in = S_tile[:, h, 1 if tid == SAMPLE else tid % 2, :]
                        i = dve.scalar_tensor_tensor(out=S_mid[:, h, :], in0=s_in, scalar=elast[:, h, 0:1],
                                                     in1=PS[:, 6, 0:P], op0=ALU.mult, op1=ALU.add)
                        if nch == 2:
                            link(i)
                            i = dve.scalar_tensor_tensor(out=S_tile[:, h, (tid + 1) % 2, :], in0=S_mid[:, h, :],
                                                         scalar=elast[:, h, 1:2], in1=PS[:, 7, 0:P],
                                                         op0=ALU.mult, op1=ALU.add)
                        i.then_inc(hg_S, 1)
                    dve.wait_ge(hg_oc, HB * ft + HB)
                    dve.tensor_scalar(ssq[0:rows, :], ssq[0:rows, :], 1.0 / P, EPS, ALU.mult, ALU.add).then_inc(hg_ms, 1)
                    dve.wait_ge(hg_rt, ft + 1)
                    link(dve.reciprocal(rsq[0:rows, :], rsq[0:rows, :]))
                    link(dve.tensor_tensor(ob[0:rows], ob[0:rows], rsq[0:rows, :].unsqueeze(2).to_broadcast([rows, HB, P]),
                                           ALU.mult))
                    dve.tensor_tensor(ob[0:rows].rearrange("p h d -> p (h d)"), ob[0:rows].rearrange("p h d -> p (h d)"),
                                      T2[0:rows, ti, :], ALU.mult).then_inc(hg_ob, 1)
                leave()

                enter(dve, g, "G")
                gated(g, "G", W)
                leave()

                enter(dve, g, "H")
                dve.wait_ge(x_in, x_tiles[g, "H"])
                for n in by_stage[g, "H"]:
                    _, _, b, kind, what, c, s, ti = products[n]
                    rows = tiles[ti][1]
                    dve.wait_ge(pj_ready, n + 1)
                    dve.tensor_tensor(hx[0:rows, ti, c:c + 256], PS[0:rows, n % 2, 0:256], hx[0:rows, ti, c:c + 256],
                                      ALU.add).then_inc(pj_free[n % 2], 1)
                norm_scale(g, "H")
                for ti, (tid, rows, c0) in enumerate(tiles):
                    dve.scalar_tensor_tensor(out=xn[0:rows, ti, :], in0=hx[0:rows, ti, :], scalar=rstd[0:rows, ti:ti + 1],
                                             in1=gain_ffn[0:rows, :], op0=ALU.mult, op1=ALU.mult).then_inc(xn_ready, 1)
                leave()

                enter(dve, g, "I")
                dve.wait_ge(h_out, 32 * (tile_no[g, nt - 1] + 1))
                for h in range(PH):
                    for ti, (tid, rows, c0) in enumerate(tiles):
                        o = top_no[g, h, ti]
                        r = slice(0, rows)
                        dve.wait_ge(tk_cp, o + 1)
                        for p in range(2):
                            i = dve.max(sv[r, p, 0:8], s1[r, o % 2, p, :])
                        link(i)
                        for p in range(2):
                            dve.max_index(si[r, p, 0:8], sv[r, p, 0:8], s1[r, o % 2, p, :])
                            i = dve.match_replace(s2[r, p, :], sv[r, p, 0:8], s1[r, o % 2, p, :], LOWEST)
                        link(i)
                        for p in range(2):
                            i = dve.max(sv[r, p, 8:16], s2[r, p, :])
                        link(i)
                        for p in range(2):
                            i = dve.max_index(si[r, p, 8:16], sv[r, p, 8:16], s2[r, p, :])
                        link(i)
                        dve.tensor_copy(sif[r], si[r])
                        link(dve.tensor_tensor(comb[r], sv[r, 0, :].unsqueeze(2).to_broadcast([rows, TOPK, TOPK]),
                                               sv[r, 1:2, :].to_broadcast([rows, TOPK, TOPK]), ALU.add))
                        cf = comb[r].rearrange("p a b -> p (a b)")
                        if o >= 1:
                            dve.wait_ge(tk_exp, o)
                        link(dve.max(cv[r, 0:8], cf))
                        dve.max_index(ci[r, 0:8], cv[r, 0:8], cf)
                        link(dve.match_replace(comb2[r], cv[r, 0:8], cf, LOWEST))
                        dve.tensor_scalar(ncv[r], cv[r, 0:1], -1.0, None, ALU.mult)
                        link(dve.max(cv[r, 8:16], comb2[r]))
                        link(dve.max_index(ci[r, 8:16], cv[r, 8:16], comb2[r]))
                        dve.tensor_scalar(ab[r, 0, :], ci[r], 4, None, ALU.logical_shift_right).then_inc(tk_cv, 1)
                        link(dve.tensor_scalar(ab[r, 1, :], ci[r], 15, None, ALU.bitwise_and))
                        link(dve.tensor_copy(abf[r], ab[r]))
                        for p in range(2):
                            i = dve.tensor_tensor(eq[r, p], abf[r, p, :].unsqueeze(2).to_broadcast([rows, TOPK, TOPK]),
                                                  iota16[r, :].unsqueeze(1).to_broadcast([rows, TOPK, TOPK]),
                                                  ALU.is_equal)
                        link(i)
                        for p in range(2):
                            i = dve.tensor_tensor(eq[r, p], eq[r, p], sif[r, p:p + 1, :].to_broadcast([rows, TOPK, TOPK]),
                                                  ALU.mult)
                        link(i)
                        link(dve.tensor_reduce(i12[r], eq[r], AX, ALU.add))
                        at = tid * P + h * TOPK
                        dve.scalar_tensor_tensor(out=idx[r, at:at + TOPK], in0=i12[r, 0, :], scalar=128.0, in1=i12[r, 1, :],
                                                 op0=ALU.mult, op1=ALU.add)
                        dve.wait_ge(tk_exp, o + 1)
                        link(dve.reciprocal(ginv[r], gsum[r]))
                        dve.tensor_scalar(gates[r, at:at + TOPK], ge[r], ginv[r], None, ALU.mult).then_inc(tk_done, 1)
                leave()

            dve.memset(hid[:, :], 0.0).then_inc(ring_used, R)
            dve.wait_ge(ring_used, R)

            def expert_head(q, rows):
                fills = 32 // R
                for j in range(TOPK):
                    dve.wait_ge(row_in[j % R], 16 * (fills * q + j // R + 1))
                    row = ring[0:rows, j % R, :]
                    dve.tensor_tensor_reduce(row, row, xt[0:rows, :], 1.0, 0.0, ALU.mult, ALU.add,
                                             hid[0:rows, j:j + 1]).then_inc(ring_used, 1)
                dve.wait_ge(e_gelu, q + 1)
                dve.tensor_tensor(wk[0:rows, :], glu[0:rows, :], gates[0:rows, bass.ds(q * TOPK, TOPK)], ALU.mult)\
                   .then_inc(e_w, 1)
                dve.wait_ge(e_w, q + 1)
                for j in range(TOPK, 2 * TOPK):
                    k = j - TOPK
                    dve.wait_ge(row_in[j % R], 16 * (fills * q + j // R + 1))
                    dve.wait_ge(ring_used, 32 * q + R + j)
                    dve.scalar_tensor_tensor(out=acc[0:rows, :], in0=ring[0:rows, j % R, :], scalar=wk[0:rows, k:k + 1],
                                             in1=acc[0:rows, :], op0=ALU.mult, op1=ALU.add).then_inc(ring_used, 1)

            def tile_end(it, rows):
                dve.wait_ge(e_sq, it + 1)
                dve.tensor_scalar(ss[0:rows, 4:5], ss[0:rows, 4:5], 1.0 / D, EPS, ALU.mult, ALU.add).then_inc(e_ms, 1)
                dve.wait_ge(e_rt, it + 1)
                dve.reciprocal(rstd[0:rows, 4:5], rstd[0:rows, 4:5]).then_inc(e_w2, 1)
                dve.wait_ge(e_w2, it + 1)
                dve.scalar_tensor_tensor(out=xt[0:rows, :], in0=acc[0:rows, :], scalar=rstd[0:rows, 4:5],
                                         in1=gain_final[0:rows, :], op0=ALU.mult, op1=ALU.mult).then_inc(e_y, 1)

            with dve.Fori(0, 8) as it:
                dve.wait_ge(xt_in, 32 * it + 32)
                dve.sem_inc(passed_dve, 1)
                with dve.Fori(0, PH) as h:
                    expert_head(it * PH + h, P)
                tile_end(it, P)
            dve.wait_ge(xt_in, 32 * 9)
            for h in range(PH):
                expert_head(64 + h, DEC)
            tile_end(8, DEC)


_INS = ["x_prompt", "x_sample", "cache_attn_k", "cache_attn_v", "state_hgrn", "norm_mix", "w_in", "rel_bias",
        "lb_logits", "hgrn_norm", "w_branch_a", "w_branch_b", "w_out", "norm_ffn", "peer_query", "peer_subkeys",
        "peer_u", "peer_v", "norm_final"]
_FLAT = {"peer_u": 1, "peer_v": 1}
_OUTS = [(1, SEQ, D), (1, DEC, D), (1, 1, 512, HA, 64), (1, 1, 512, HA, 64), (1, 1, HB, P, P),
         (1, 1, DEC, HA, 64), (1, 1, DEC, HA, 64), (1, 1, HB, P, P)]


def kernel(**inputs):
    import numpy as _np
    import concourse.bacc as _bacc
    from concourse import mybir as _mybir
    from concourse.bass_utils import run_bass_kernel_spmd as _run

    nc = _bacc.Bacc("TRN2", target_bir_lowering=False, num_devices=1)
    arrays, args = {}, []
    for name in _INS:
        a = _np.ascontiguousarray(inputs[name])
        if name in _FLAT:
            a = a[0]
        arrays[f"in_{name}"] = a
        args.append(nc.dram_tensor(f"in_{name}", a.shape, _mybir.dt.from_np(a.dtype), kind="ExternalInput").ap())
    for i, shape in enumerate(_OUTS):
        args.append(nc.dram_tensor(f"out_{i}", shape, _mybir.dt.float32, kind="ExternalOutput").ap())
    build(nc, *args)
    r = _run(nc, [arrays], core_ids=[0])
    got = [r.results[0][f"out_{i}"] for i in range(len(_OUTS))]
    return tuple(got)
```

```python
from contextlib import ExitStack

import concourse.bass as bass
from concourse import mybir

F32 = mybir.dt.float32
U32 = mybir.dt.uint32
ALU = mybir.AluOpType
ACT = mybir.ActivationFunctionType
AX = mybir.AxisListType.X

P = 128
D = 1024
DK = D // P
SEQ = 1024
DEC = 64
CH = 64
HA = 8
DA = 512
CB = DA // P
HB = 4
EPS = 1e-6
NREL = 513
CLIP = 256
REACH = 512
WIN = 640
SCALE = 64 ** -0.5
NEG = -1e30
LOWEST = -3.0e38
NEXP = 16384
PH = 8
TOPK = 16
NL = 6
LEVELS = [32, 16, 8, 4, 2, 1]
SAMPLE = 8
GROUPS = [[(SAMPLE, 64, 0), (0, 128, 64)], [(1, 128, 0), (2, 128, 128)], [(3, 128, 0), (4, 128, 128)],
          [(5, 128, 0), (6, 128, 128)], [(7, 128, 0)]]
NG = len(GROUPS)
WG = 256
STAGES = "ABCDEFGHI"
R = 8


def width(g):
    return sum(t[1] for t in GROUPS[g])


def slices(g):
    nt = len(GROUPS[g])
    rate = width(g) / 256
    return ([8] + [25 * rate] * 2 + [16 * rate] * (HA * nt // 4) + [22 * rate] * 2 + [30 * rate] * 2
            + [14, 14, 16] * nt + [22 * rate] * 2 + [20 * rate] * 2 + [12] * (PH * nt))


def expert_units(g):
    heads = [(tn, h) for tn in tiles_of(g) for h in range(PH)]
    order = [("u", *heads[0])]
    for a, b in zip(heads, heads[1:]):
        order += [("u", *b), ("v", *a)]
    return order + [("v", *heads[-1])]


def tiles_of(g):
    first = sum(len(GROUPS[q]) for q in range(g))
    return range(first, first + len(GROUPS[g]))


def interleave(mix, unit, tail):
    done = sum(1 for _ in mix(0))
    assert done == len(slices(0)), (done, len(slices(0)))
    m = 0
    for g in range(NG):
        units = expert_units(g)
        costs = slices(g + 1) if g + 1 < NG else []
        steps = mix(g + 1) if g + 1 < NG else iter(())
        spent = at = 0
        for u, (kind, tn, h) in enumerate(units):
            unit(m, kind, tn, h)
            while at < len(costs) and spent < sum(costs) * (u + 1) / len(units):
                next(steps)
                spent += costs[at]
                at += 1
            tail(m, kind, tn, h)
            m += 1
        for _ in steps:
            raise AssertionError("slices are left")
    return m


def stage_no(g, s):
    return 1 + g * len(STAGES) + STAGES.index(s)


def plan_projections():
    blocks, products = [], []

    def add(g, stage, w, nk, c0, nc_, kind, what):
        b = len(blocks)
        blocks.append((w, nk, c0, nc_))
        if kind == "fm":
            for s in range(nc_ // P):
                products.append((g, stage, b, "fm", what, c0 // P + s, s, None))
        else:
            for ti in range(len(GROUPS[g])):
                products.append((g, stage, b, "tm", what, c0, 0, ti))

    for g in range(len(GROUPS)):
        for c in (0, 256):
            add(g, "B", "w_in", 8, c, 256, "fm", "q")
        for c in (512, 768):
            add(g, "B", "w_in", 8, c, 256, "fm", "k")
        for c in (1024, 1280):
            add(g, "B", "w_in", 8, c, 256, "tm", "v")
        for i in range(4):
            add(g, "D", "w_in", 8, 3584 + 256 * i, 256, "fm", "gate")
            if i % 2:
                add(g, "D", "w_a", 4, 512 * (i // 2), 512, "fm", "branch")
        for c in (1536, 1792):
            add(g, "E", "w_in", 8, c, 256, "fm", "f")
        for c in (2560, 2816):
            add(g, "E", "w_in", 8, c, 256, "fm", "qb")
        for c in (2048, 2304):
            add(g, "E", "w_in", 8, c, 256, "tm", "i")
        for c in (3072, 3328):
            add(g, "E", "w_in", 8, c, 256, "tm", "g")
        for i in range(4):
            add(g, "G", "w_in", 8, 4608 + 256 * i, 256, "fm", "gate")
            if i % 2:
                add(g, "G", "w_b", 4, 512 * (i // 2), 512, "fm", "branch")
        for i in range(4):
            add(g, "H", "w_out", 8, 256 * i, 256, "tm", "o")
        for i in range(8):
            add(g, "I", "w_query", 8, 256 * i, 256, "fm", "query")
    return blocks, products


def build(nc, x_prompt, x_sample, cache_k, cache_v, state_in, norm_mix, w_in, rel_bias, lb_logits,
          hgrn_norm, w_a, w_b, w_out, norm_ffn, w_query, sub_keys, u_tab, v_tab, norm_final,
          y_prompt, y_sample, k_prompt, v_prompt, state_prompt, k_sample, v_sample, state_sample):
    weights = {"w_in": w_in[0], "w_a": w_a[0], "w_b": w_b[0], "w_out": w_out[0], "w_query": w_query[0]}
    xp, xs = x_prompt[0], x_sample[0]
    blocks, products = plan_projections()
    last_product = {}
    for n, pr in enumerate(products):
        last_product[pr[2]] = n
    by_stage = {}
    for n, pr in enumerate(products):
        by_stage.setdefault((pr[0], pr[1]), []).append(n)
    att = [(g, h, ti) for g in range(NG) for h in range(HA) for ti in range(len(GROUPS[g]))]
    att_no = {s: n for n, s in enumerate(att)}
    tile_no = {(g, ti): n for n, (g, ti) in enumerate((g, ti) for g in range(NG) for ti in range(len(GROUPS[g])))}
    norm_no = {}
    for g in range(NG):
        for s in "AH":
            for ti in range(len(GROUPS[g])):
                norm_no[g, s, ti] = len(norm_no)
    norm_batch = {(g, s): 2 * g + n for g in range(NG) for n, s in enumerate("AH")}
    top_no = {}
    for g in range(NG):
        for h in range(PH):
            for ti in range(len(GROUPS[g])):
                top_no[g, h, ti] = len(top_no)

    h_scr = nc.dram_tensor("h_scr", (SEQ + DEC, D), F32, kind="Internal").ap()
    xn_scr = nc.dram_tensor("xn_scr", (SEQ + DEC, D), F32, kind="Internal").ap()
    rel_scr = nc.dram_tensor("rel_scr", (HA, P, WIN), F32, kind="Internal").ap()
    sk_scr = nc.dram_tensor("sk_scr", (P, 16 * P), F32, kind="Internal").ap()

    def rows_of(ap_prompt, ap_sample, tid):
        return ap_sample if tid == SAMPLE else ap_prompt[tid * P:(tid + 1) * P, :]

    with ExitStack() as ctx:
        def sb(name, shape, dt=F32):
            return ctx.enter_context(nc.sbuf_tensor(name, shape, dt))

        def sem(name):
            return ctx.enter_context(nc.semaphore(name))

        PS = ctx.enter_context(nc.psum_tensor("PS", [P, 8, 512], F32))
        ident = sb("ident", [P, P])
        masks = sb("masks", [P, NL + 1, P])
        gain_mix = sb("gain_mix", [P, DK])
        gain_ffn = sb("gain_ffn", [P, D])
        gain_final = sb("gain_final", [P, D])
        gain_hgrn = sb("gain_hgrn", [P, DA])
        lbl = sb("lbl", [P, 2, HB])
        lb = sb("lb", [P, HB])
        one_lb = sb("one_lb", [P, HB])
        iota16 = sb("iota16", [P, TOPK])
        restart = sb("restart", [P, WG])
        mark_a = sb("mark_a", [P, 1])
        mark_d = sb("mark_d", [P, 1])
        xnT = sb("xnT", [P, DK, WG])
        M = sb("M", [P, DK, WG])
        kT = sb("kT", [P, CB, SEQ])
        v = sb("v", [P, SEQ // P, DA])
        kS = sb("kS", [P, CB, DEC])
        vS = sb("vS", [P, DA])
        Q = sb("Q", [P, CB, WG])
        K2 = sb("K2", [P, CB, WG])
        Q2 = sb("Q2", [P, CB, WG])
        T12 = sb("T12", [P, 2, 2, DA])
        T1 = T12[:, 0]
        T2 = T12[:, 1]
        skT = T12[:, :, :, :].rearrange("p a b c -> p (a b c)")
        wring = sb("wring", [P, 2, 2048])
        bias = sb("bias", [P, 2, WIN])
        S_tile = sb("S_tile", [P, HB, 2, P])
        S_mid = sb("S_mid", [P, HB, P])
        idx = sb("idx", [P, 9 * P], U32)
        gates = sb("gates", [P, 9 * P])
        ss = sb("ss", [P, 8])
        rstd = sb("rstd", [P, 8])
        tmp = sb("tmp", [P, 7680])
        ring = sb("ring", [P, R, D])
        xt = sb("xt", [P, 2, D])
        acc = sb("acc", [P, 2, D])
        ixs = sb("ixs", [P, 2, TOPK], U32)
        hid = sb("hid", [P, 2, TOPK])
        glu = sb("glu", [P, 2, TOPK])
        wk = sb("wk", [P, 2, TOPK])
        esum = sb("esum", [P, 2])
        erstd = sb("erstd", [P, 2])

        def part(at, *shape):
            n = 1
            for k in shape:
                n *= k
            ap = tmp[:, at:at + n]
            names = "abcd"[:len(shape)]
            if len(shape) == 1:
                return ap
            return ap.rearrange(f"p ({' '.join(names)}) -> p {' '.join(names)}", **dict(zip(names, shape)))

        hx = part(0, 2, D)
        xn = part(2 * D, 2, D)
        kc = part(0, 4, DA)
        sc = part(0, 2, WIN)
        pt = part(2 * WIN, 2, WIN)
        nmax = part(4 * WIN, 2)
        rsum = part(4 * WIN + 2, 2)
        rinv = part(4 * WIN + 4, 2)
        sg = part(0, DK, WG)
        E = part(0, NL + 1, HB, P)
        Lq = part(3584, NL, P)
        Lk = part(4352, NL, P)
        Am = part(5120, NL + 1, P)
        attnT = part(6016, 2, P)
        ecum = part(6272, HB, P)
        kdT = part(6784, P)
        ob = part(6912, HB, P)
        ssq = part(7424, HB)
        rsq = part(7428, HB)
        elast = part(7432, HB, 2)
        junk = part(7440, P)
        qp = part(0, 2, 2, WG)
        s1 = part(1024, 2, 2, P)
        s2 = part(1792, 2, P)
        comb = part(2048, TOPK, TOPK)
        comb2 = part(2304, TOPK * TOPK)
        eq = part(2560, 2, TOPK, TOPK)
        sv = part(3072, 2, TOPK)
        sif = part(3104, 2, TOPK)
        cv = part(3136, TOPK)
        abf = part(3152, 2, TOPK)
        i12 = part(3184, 2, TOPK)
        ge = part(3216, TOPK)
        gsum = part(3232, 1)
        ginv = part(3233, 1)
        ncv = part(3234, 1)
        si = part(3240, 2, TOPK).bitcast(U32)
        ci = part(3272, TOPK).bitcast(U32)
        ab = part(3288, 2, TOPK).bitcast(U32)
        rel = tmp[0:HA, 0:767]
        sk = part(1024, 16, P)
        skTs = part(1024 + 2048, 16, P)

        const_in, rel_in, sk_in, relE, rel_out, sk_tr, sk_cp, sk_out, consts, lb_d, lb_a, state_loaded = [
            sem(n) for n in ("const_in", "rel_in", "sk_in", "relE", "rel_out", "sk_tr", "sk_cp", "sk_out",
                             "consts", "lb_d", "lb_a", "state_loaded")]
        dve_chain = sem("dve_chain")
        bar_act, bar_dve = sem("bar_act"), sem("bar_dve")
        w_in_sem = [sem("w_landed0"), sem("w_landed1")]
        pj_ready = sem("pj_ready")
        pj_free = [sem("pj_free0"), sem("pj_free1")]
        x_in, n_sq, n_ms, n_rt, xn_ready, tr_ready = [sem(n) for n in (
            "x_in", "n_sq", "n_ms", "n_rt", "xn_ready", "tr_ready")]
        tr_free = sem("tr_free")
        kc_in, vc_in, kt_tr, kt_cp, kv_out = [sem(n) for n in ("kc_in", "vc_in", "kt_tr", "kt_cp", "kv_out")]
        bias_in = [sem("bias_in0"), sem("bias_in1")]
        at_sc, at_biased, at_max, at_exp, at_pT, at_ptc, at_pv, at_rinv, at_oa = [sem(n) for n in (
            "at_sc", "at_biased", "at_max", "at_exp", "at_pT", "at_ptc", "at_pv", "at_rinv", "at_oa")]
        oT_tr, oT_cp = sem("oT_tr"), sem("oT_cp")
        f_sig, f_fg, f_ln, g_silu = [sem(n) for n in ("f_sig", "f_fg", "f_ln", "g_silu")]
        hg_D, hg_E, hg_kq, hg_L, hg_at, hg_red, hg_kdT, hg_kdc, hg_st, hg_S, hg_o, hg_oc, hg_ms, hg_rt, hg_ob, \
            hg_oT, hg_obc, st_out = [sem(n) for n in (
                "hg_D", "hg_E", "hg_kq", "hg_L", "hg_at", "hg_red", "hg_kdT", "hg_kdc", "hg_st", "hg_S", "hg_o",
                "hg_oc", "hg_ms", "hg_rt", "hg_ob", "hg_oT", "hg_obc", "st_out")]
        h_out = sem("h_out")
        skT_in, tk_sc, tk_cp, tk_done, tk_cv, tk_exp = [sem(n) for n in (
            "skT_in", "tk_sc", "tk_cp", "tk_done", "tk_cv", "tk_exp")]
        xt_in = [sem("xt_in0"), sem("xt_in1")]
        row_in = [sem(f"row_in{r}") for r in range(R)]
        ring_used, ix_ready, e_gelu, e_w, e_sq, e_ms, e_rt, e_y, y_out, e_rs = [sem(n) for n in (
            "ring_used", "ix_ready", "e_gelu", "e_w", "e_sq", "e_ms", "e_rt", "e_y", "y_out", "e_rs")]

        passed, passed_dve, passed_sp = sem("passed"), sem("passed_dve"), sem("passed_sp")

        block = ctx.enter_context(nc.Block())

        def n_tr(g, s, ti):
            return 2 * norm_no[g, s, ti]

        def geometry(g, ti):
            tid, rows, _ = GROUPS[g][ti]
            return rows, (REACH + DEC if tid == SAMPLE else P * (min(tid, 4) + 1))

        def gate_product(g, s, c):
            return [n for n in by_stage[g, s] if products[n][4] == "gate" and (products[n][5] - 28) % 8 == c][0]

        tile_rows = [rows for tiles in GROUPS for _, rows, _ in tiles]
        tile_ids = [tid for tiles in GROUPS for tid, _, _ in tiles]

        def enter(eng, g, s):
            eng.wait_ge(bar_act, stage_no(g, s))
            eng.wait_ge(bar_dve, stage_no(g, s))

        k_tiles = {g: [ti for ti, (tid, _, _) in enumerate(GROUPS[g]) if tid >= 4] for g in range(NG)}
        kt_before = {g: sum(len(k_tiles[q]) for q in range(g)) + (4 if g > 0 else 0) for g in range(NG + 1)}
        x_tiles = {(g, s): 16 * (sum(2 * len(GROUPS[q]) for q in range(g)) + (2 if s == "H" else 1) * len(GROUPS[g]))
                   for g in range(NG) for s in "AH"}

        @block.sync
        def _(sp):
            with nc.allow_non_contiguous_dma(reason="small vectors laid over partitions"):
                sp.dma_start(gain_mix[:, :], norm_mix[0].rearrange("(k p) -> p k", p=P)).then_inc(const_in, 16)
                sp.dma_start(lbl[:, :, :], lb_logits.rearrange("a (h p) -> p a h", p=P)).then_inc(const_in, 16)
                sp.dma_start(rel[:, 383:767], bass.AP(rel_bias.tensor, NREL - 1, [[NREL, HA], [-1, 384]]))\
                  .then_inc(rel_in, 16)
            sp.dma_start(gain_ffn[:, :], bass.AP(norm_ffn.tensor, 0, [[0, P], [1, D]])).then_inc(const_in, 16)
            sp.dma_start(gain_final[:, :], bass.AP(norm_final.tensor, 0, [[0, P], [1, D]])).then_inc(const_in, 16)
            sp.dma_start(gain_hgrn[:, :], bass.AP(hgrn_norm.tensor, 0, [[0, P], [1, DA]])).then_inc(const_in, 16)
            sp.dma_start(sk, sub_keys[0].rearrange("a h k d -> k (a h) d")).then_inc(sk_in, 16)
            sp.dma_start(S_tile[:, :, 1, :], state_in[0, 0].rearrange("h k v -> k h v")).then_inc(state_loaded, 16)
            sp.wait_ge(relE, 1)
            lines = rel[:, 0:767]
            sp.dma_start(rel_scr, bass.AP(lines.tensor, lines.offset + 127, [list(lines.ap[0]), [-1, P], [1, WIN]]))\
              .then_inc(rel_out, 16)
            sp.wait_ge(sk_cp, 4)
            sp.dma_start(sk_scr, skTs.rearrange("p a b -> p (a b)")).then_inc(sk_out, 16)
            sp.wait_ge(rel_out, 16)
            sp.wait_ge(sk_out, 16)

            def load_weights(b):
                w, nk, c0, n = blocks[b]
                if b >= 2:
                    sp.wait_ge(pj_ready, last_product[b - 2] + 1)
                sp.dma_start(wring[:, b % 2, 0:nk * n].rearrange("p (k n) -> p k n", k=nk),
                             weights[w].rearrange("(k p) n -> p k n", p=P)[:, :, c0:c0 + n])\
                  .then_inc(w_in_sem[b % 2], 16)

            def load_stage(g, s):
                for b in sorted({products[n][2] for n in by_stage.get((g, s), [])}):
                    load_weights(b)

            for g, tiles in enumerate(GROUPS):
                enter(sp, g, "A")
                for ti, (tid, rows, _) in enumerate(tiles):
                    sp.dma_start(hx[0:rows, ti, :], rows_of(xp, xs, tid)).then_inc(x_in, 16)
                load_stage(g, "B")
                if g == 0:
                    enter(sp, g, "B")
                    sp.dma_start(kc, cache_k[0, 0].rearrange("(t p) h d -> p t (h d)", p=P)).then_inc(kc_in, 16)
                    sp.dma_start(v[:, 4:8, :], cache_v[0, 0].rearrange("(t p) h d -> p t (h d)", p=P))\
                      .then_inc(vc_in, 16)
                enter(sp, g, "C")
                for ti in k_tiles[g]:
                    tid, rows, _ = tiles[ti]
                    ko = k_sample[0, 0] if tid == SAMPLE else k_prompt[0, 0, (tid - 4) * P:(tid - 3) * P]
                    vo = v_sample[0, 0] if tid == SAMPLE else v_prompt[0, 0, (tid - 4) * P:(tid - 3) * P]
                    sp.dma_start(ko.rearrange("t h d -> t (h d)"), T2[0:rows, ti, :]).then_inc(kv_out, 16)
                    vt = vS[0:rows, :] if tid == SAMPLE else v[:, tid, :]
                    sp.dma_start(vo.rearrange("t h d -> t (h d)"), vt).then_inc(kv_out, 16)
                for h in range(HA):
                    bh = g * HA + h
                    if bh >= 2:
                        q = att_no[((bh - 2) // HA, (bh - 2) % HA, len(GROUPS[(bh - 2) // HA]) - 1)]
                        sp.wait_ge(at_biased, q + 1)
                    for t0, j0 in ((0, 0), (64, 64)):
                        sp.dma_start(bias[t0:t0 + 64, bh % 2, j0:j0 + 576], rel_scr[h, t0:t0 + 64, j0:j0 + 576])\
                          .then_inc(bias_in[bh % 2], 16)
                load_stage(g, "D")
                load_stage(g, "E")
                if g == 0:
                    sp.wait_ge(hg_S, HB)
                    sp.dma_start(state_sample[0, 0].rearrange("h k v -> k h v"), S_mid[:, :, :]).then_inc(st_out, 16)
                load_stage(g, "G")
                enter(sp, g, "H")
                for ti, (tid, rows, _) in enumerate(tiles):
                    sp.dma_start(hx[0:rows, ti, :], rows_of(xp, xs, tid)).then_inc(x_in, 16)
                load_stage(g, "H")
                enter(sp, g, "I")
                sp.dma_start(skT, sk_scr).then_inc(skT_in, 16)
                for ti, (tid, rows, _) in enumerate(tiles):
                    sp.dma_start(h_scr[tid * P:tid * P + rows, :], hx[0:rows, ti, :]).then_inc(h_out, 16)
                    sp.dma_start(xn_scr[tid * P:tid * P + rows, :], xn[0:rows, ti, :]).then_inc(h_out, 16)
                load_stage(g, "I")
            sp.wait_ge(hg_S, HB * 9)
            sp.dma_start(state_prompt[0, 0].rearrange("h k v -> k h v"), S_tile[:, :, 0, :]).then_inc(st_out, 16)
            sp.wait_ge(kv_out, 32 * 5)
            sp.wait_ge(st_out, 32)
            sp.wait_ge(y_out, 16 * 9)

        @block.gpsimd
        def _(pool):
            pool.memset(ident[:, :], 0.0).then_inc(consts, 1)
            pool.memset(masks[:, :, :], 0.0).then_inc(consts, 1)
            for lev, s in enumerate(LEVELS):
                pool.wait_ge(consts, 2 + lev)
                pool.memset(masks[:, lev, :].rearrange("p (b t s) -> p b t s", t=2, s=s)[:, :, 1, :], 1.0)\
                    .then_inc(consts, 1)
            pool.wait_ge(consts, 8)
            n = 8
            for m in (ident[:, :], masks[:, NL, :]):
                pool.affine_select(out=m, in_=m, compare_op=ALU.not_equal, fill=1.0, base=0,
                                   pattern=[[-1, P]], channel_multiplier=1).then_inc(consts, 1)
                n += 1
            for lev, s in enumerate(LEVELS):
                m = masks[:, lev, :].rearrange("p (b w) -> p b w", w=2 * s)
                nb = P // (2 * s)
                pool.affine_select(out=m, in_=m, compare_op=ALU.is_ge, fill=0.0, base=0,
                                   pattern=[[-2 * s, nb], [0, 2 * s]], channel_multiplier=1).then_inc(consts, 1)
                n += 1
            for lev, s in enumerate(LEVELS):
                m = masks[:, lev, :].rearrange("p (b w) -> p b w", w=2 * s)
                nb = P // (2 * s)
                pool.wait_ge(consts, n)
                pool.affine_select(out=m, in_=m, compare_op=ALU.is_ge, fill=0.0, base=s - 1,
                                   pattern=[[2 * s, nb], [0, 2 * s]], channel_multiplier=-1).then_inc(consts, 1)
                n += 1
            pool.iota(iota16[:, :], pattern=[[1, TOPK]], base=0, channel_multiplier=0,
                      allow_small_or_imprecise_dtypes=True).then_inc(consts, 1)

            def gathers(q, m, odd, table, rows):
                pool.tensor_copy(ixs[0:rows, odd, :], idx[0:rows, bass.ds(q * TOPK, TOPK)]).then_inc(ix_ready, 1)
                pool.wait_ge(ix_ready, m + 1)
                for k in range(TOPK):
                    pool.wait_ge(ring_used, m * TOPK + k + 1)
                    pool.sem_inc(passed, 1)
                    pool.indirect_dma_start(
                        ring[0:rows, k % R, :], None, table,
                        bass.IndirectOffsetOnAxis(ap=ixs[0:rows, odd, k:k + 1], axis=0))\
                        .then_inc(row_in[k % R], 16)

            def load_tile(tn, tid, rows):
                if tn >= 2:
                    pool.wait_ge(y_out, 16 * (tn - 1))
                pool.dma_start(xt[0:rows, tn % 2, :], xn_scr[tid * P:tid * P + rows, :]).then_inc(xt_in[tn % 2], 16)
                pool.dma_start(acc[0:rows, tn % 2, :], h_scr[tid * P:tid * P + rows, :]).then_inc(xt_in[tn % 2], 16)

            for g, tiles in enumerate(GROUPS):
                pool.wait_ge(bar_dve, stage_no(g + 1, "A"))
                pool.wait_ge(h_out, 32 * (tile_no[g, len(tiles) - 1] + 1))
                q0 = tile_no[g, 0] * PH
                load_tile(tile_no[g, 0], *tiles[0][0:2])
                gathers(q0, 2 * q0, 0, u_tab, tiles[0][1])
                for ti, (tid, rows, _) in enumerate(tiles):
                    q0 = tile_no[g, ti] * PH
                    with pool.Fori(q0, q0 + PH - 1) as q:
                        gathers(q + 1, q * 2 + 1, 1, u_tab, rows)
                        gathers(q, q * 2 + 2, 0, v_tab, rows)
                    q = q0 + PH - 1
                    if ti + 1 < len(tiles):
                        load_tile(tile_no[g, ti] + 1, *tiles[ti + 1][0:2])
                        gathers(q + 1, 2 * q + 1, 1, u_tab, tiles[ti + 1][1])
                        gathers(q, 2 * q + 2, 0, v_tab, rows)
                    else:
                        gathers(q, 2 * q + 1, 1, v_tab, rows)

        @block.tensor
        def _(pe):
            def product(n, act_in):
                g, _, b, kind, what, _, s, ti = products[n]
                _, nk, _, ncol = blocks[b]
                w = wring[:, b % 2, 0:nk * ncol].rearrange("p (k n) -> p k n", k=nk)
                pe.wait_ge(w_in_sem[b % 2], 16 * (b // 2 + 1))
                if n >= 2:
                    pe.wait_ge(pj_free[n % 2], n // 2)
                for k in range(nk):
                    if kind == "fm":
                        W = width(g)
                        mm = pe.matmul(PS[:, n % 2, 0:W], w[:, k, s * P:(s + 1) * P], act_in[:, k, 0:W],
                                       start=(k == 0), stop=(k == nk - 1))
                    else:
                        _, rows, c0 = GROUPS[g][ti]
                        mm = pe.matmul(PS[0:rows, n % 2, 0:ncol], act_in[:, k, c0:c0 + rows], w[:, k, :],
                                       start=(k == 0), stop=(k == nk - 1))
                mm.then_inc(pj_ready, 1)

            def transpose_norm(g, s, source_sem):
                for ti, (tid, rows, c0) in enumerate(GROUPS[g]):
                    pe.wait_ge(source_sem, norm_no[g, s, ti] + 1)
                    for half in range(2):
                        m = n_tr(g, s, ti) + half
                        if m >= 4:
                            pe.wait_ge(tr_free, m - 3)
                        for k in range(4):
                            kk = 4 * half + k
                            mm = pe.transpose(PS[:, m % 4, k * P:k * P + rows], xn[0:rows, ti, kk * P:(kk + 1) * P],
                                              ident[0:rows, 0:rows])
                        mm.then_inc(tr_ready, 1)

            pe.wait_ge(consts, 23)
            pe.wait_ge(sk_in, 16)
            for b in range(4):
                for k in range(4):
                    mm = pe.transpose(PS[:, b, k * P:(k + 1) * P], sk[:, 4 * b + k, :], ident[:, :])
                mm.then_inc(sk_tr, 1)

            def mix(g):
                tiles = GROUPS[g]
                nt = len(tiles)
                enter(pe, g, "A")
                transpose_norm(g, "A", xn_ready)
                yield
                enter(pe, g, "B")
                for n in by_stage[g, "B"][:8]:
                    product(n, xnT)
                yield
                for n in by_stage[g, "B"][8:]:
                    product(n, xnT)
                for n in by_stage[g, "B"][-2:]:
                    pe.wait_ge(pj_free[n % 2], n // 2 + 1)
                kt = kt_before[g]
                for i, ti in enumerate(k_tiles[g]):
                    tid, rows, c0 = tiles[ti]
                    src = kS if tid == SAMPLE else kT[:, :, tid * P:(tid + 1) * P]
                    for c in range(CB):
                        mm = pe.transpose(PS[0:rows, 2 + i, c * P:(c + 1) * P], src[:, c, 0:rows], ident[:, :])
                    mm.then_inc(kt_tr, 1)
                if g == 0:
                    pe.wait_ge(kc_in, 16)
                    for t in range(4):
                        for c in range(CB):
                            mm = pe.transpose(PS[:, 4 + t, c * P:(c + 1) * P], kc[:, t, c * P:(c + 1) * P], ident[:, :])
                        mm.then_inc(kt_tr, 1)
                yield
                enter(pe, g, "C")
                if g == 0:
                    pe.wait_ge(vc_in, 16)
                steps = [s for s in att if s[0] == g]

                def keys_of(ti):
                    tid, rows, _ = tiles[ti]
                    if tid == SAMPLE:
                        return [(kT[:, :, REACH + t * P:REACH + (t + 1) * P], v[:, 4 + t, :], P) for t in range(4)] + [
                            (kS, vS, DEC)]
                    return [(kT[:, :, t * P:(t + 1) * P], v[:, t, :], P) for t in range(max(0, tid - 4), tid + 1)]

                def scores(step):
                    i = att_no[step]
                    _, h, ti = step
                    tid, rows, c0 = tiles[ti]
                    if i >= 2:
                        pe.wait_ge(at_biased, i - 1)
                    p0 = 64 * (h % 2)
                    q = Q[p0:p0 + 64, h // 2, c0:c0 + rows]
                    bank = 2 + 2 * (i % 2)
                    for n, (kk, _, nk) in enumerate(keys_of(ti)):
                        mm = pe.matmul(PS[0:rows, bank + n // 4, (n % 4) * P:(n % 4) * P + nk], q,
                                       kk[p0:p0 + 64, h // 2, 0:nk], start=True, stop=True)
                    mm.then_inc(at_sc, 1)

                def values(step):
                    i = att_no[step]
                    _, h, ti = step
                    tid, rows, c0 = tiles[ti]
                    pe.wait_ge(at_exp, i + 1)
                    if i >= 1:
                        pe.wait_ge(at_ptc, i)
                    kv = keys_of(ti)
                    for n, (_, _, nk) in enumerate(kv):
                        mm = pe.transpose(PS[0:nk, 6 + n // 4, (n % 4) * P:(n % 4) * P + rows],
                                          sc[0:rows, i % 2, n * P:n * P + nk], ident[0:rows, 0:rows])
                    mm.then_inc(at_pT, 1)
                    pe.wait_ge(at_ptc, i + 1)
                    if i >= 2:
                        pe.wait_ge(at_oa, i - 1)
                    for n, (_, vv, nk) in enumerate(kv):
                        mm = pe.matmul(PS[0:rows, i % 2, 0:64], pt[0:nk, i % 2, n * P:n * P + rows],
                                       vv[0:nk, h * 64:(h + 1) * 64], start=(n == 0), stop=(n == len(kv) - 1))
                    mm.then_inc(at_pv, 1)

                for k in range(len(steps) + 1):
                    if k < len(steps):
                        scores(steps[k])
                    if k >= 1:
                        values(steps[k - 1])
                    if k >= 1 and k % 4 == 0:
                        yield
                enter(pe, g, "D")
                for ti, (tid, rows, c0) in enumerate(tiles):
                    for c in range(CB):
                        mm = pe.transpose(PS[:, 2 + ti, c * P:c * P + rows], T1[0:rows, ti, c * P:(c + 1) * P],
                                          ident[0:rows, 0:rows])
                    mm.then_inc(oT_tr, 1)
                pe.wait_ge(oT_cp, tile_no[g, nt - 1] + 1)
                for i, n in enumerate(by_stage[g, "D"]):
                    product(n, Q if products[n][4] == "branch" else xnT)
                    if i % 8 == 7:
                        yield
                enter(pe, g, "E")
                for n in by_stage[g, "E"][:8]:
                    product(n, xnT)
                yield
                for n in by_stage[g, "E"][8:]:
                    product(n, xnT)
                yield
                enter(pe, g, "F")
                pe.wait_ge(state_loaded, 16)
                for ti, (tid, rows, c0) in enumerate(tiles):
                    ft = tile_no[g, ti]
                    nch = rows // CH
                    pe.wait_ge(hg_kq, ft + 1)
                    yield
                    for h in range(HB):
                        fh = ft * HB + h
                        if fh >= 1:
                            pe.wait_ge(hg_kdc, fh)
                        if h == 0 and ft >= 1:
                            pe.wait_ge(hg_obc, ft)
                        pe.transpose(PS[0:rows, 5, 0:P], E[:, NL, h, 0:rows], ident[:, :]).then_inc(hg_kdT, 1)
                        pe.wait_ge(hg_L, fh + 1)
                        if fh >= 2:
                            pe.wait_ge(hg_red, fh - 1)
                        b0 = 2 * (fh % 2)
                        for lev in range(NL):
                            pe.matmul(PS[0:rows, b0 + lev // 4, (lev % 4) * P:(lev % 4) * P + rows],
                                      Lk[:, lev, 0:rows], Lq[:, lev, 0:rows], start=True, stop=True)
                        pe.matmul(PS[0:rows, b0 + 1, 2 * P:2 * P + rows], K2[:, h, c0:c0 + rows],
                                  Q2[:, h, c0:c0 + rows], start=True, stop=True).then_inc(hg_at, 1)
                        pe.wait_ge(hg_kdc, fh + 1)
                        if fh >= 1:
                            pe.wait_ge(hg_S, fh)
                        for c in range(nch):
                            mm = pe.matmul(PS[:, 6 + c, 0:P], kdT[c * CH:(c + 1) * CH, :],
                                           T1[c * CH:(c + 1) * CH, ti, h * P:(h + 1) * P], start=True, stop=True)
                        mm.then_inc(hg_st, 1)
                        pe.wait_ge(hg_red, fh + 1)
                        if fh >= 1:
                            pe.wait_ge(hg_oc, fh)
                        pe.matmul(PS[0:rows, 4, 0:P], attnT[0:rows, fh % 2, 0:rows], T1[0:rows, ti, h * P:(h + 1) * P],
                                  start=True, stop=True, skip_group_check=True)
                        pe.wait_ge(hg_S, fh + 1)
                        s_in = S_tile[:, h, 1 if tid == SAMPLE else tid % 2, :]
                        for c in range(nch):
                            mm = pe.matmul(PS[c * CH:(c + 1) * CH, 4, 0:P], ecum[:, h, c * CH:(c + 1) * CH],
                                           s_in if c == 0 else S_mid[:, h, :], start=False, stop=True,
                                           skip_group_check=True)
                        mm.then_inc(hg_o, 1)
                        if h == 1:
                            yield
                    pe.wait_ge(hg_ob, ft + 1)
                    pe.wait_ge(hg_kdc, 4 * ft + 4)
                    for h in range(HB):
                        mm = pe.transpose(PS[:, 5, h * P:h * P + rows], ob[0:rows, h, :], ident[0:rows, 0:rows])
                    mm.then_inc(hg_oT, 1)
                    yield
                enter(pe, g, "G")
                for i, n in enumerate(by_stage[g, "G"]):
                    product(n, Q2 if products[n][4] == "branch" else xnT)
                    if i % 8 == 7:
                        yield
                enter(pe, g, "H")
                for n in by_stage[g, "H"][:2 * nt]:
                    product(n, M)
                yield
                for n in by_stage[g, "H"][2 * nt:]:
                    product(n, M)
                transpose_norm(g, "H", xn_ready)
                yield
                enter(pe, g, "I")
                pe.wait_ge(skT_in, 16 * (g + 1))
                qn = by_stage[g, "I"]

                def key_scores(h, ti):
                    if ti == 0:
                        for n in qn[2 * h:2 * h + 2]:
                            pe.wait_ge(pj_free[n % 2], n // 2 + 1)
                    tid, rows, c0 = tiles[ti]
                    o = top_no[g, h, ti]
                    if o >= 2:
                        pe.wait_ge(tk_cp, o - 1)
                    for p in range(2):
                        mm = pe.matmul(PS[0:rows, 2 + o % 2, p * P:(p + 1) * P], qp[:, h % 2, p, c0:c0 + rows],
                                       skT[:, (p * PH + h) * P:(p * PH + h + 1) * P], start=True, stop=True)
                    mm.then_inc(tk_sc, 1)

                def head_of(i):
                    h, ti = divmod(i, nt)
                    if ti == 0 and h + 1 < PH:
                        product(qn[2 * h + 2], xnT)
                        product(qn[2 * h + 3], xnT)
                    key_scores(h, ti)

                product(qn[0], xnT)
                product(qn[1], xnT)
                head_of(0)
                for i in range(PH * nt):
                    if i + 1 < PH * nt:
                        head_of(i + 1)
                    yield

            def nothing(m, kind, tn, h):
                pass

            interleave(mix, nothing, nothing)

        @block.scalar
        def _(act):
            def leave():
                act.activation(mark_a[:, :], ident[:, 0:1], ACT.Copy).then_inc(bar_act, 1)

            act.wait_ge(consts, 23)
            act.wait_ge(lb_d, 1)
            act.activation(lb[:, :], lbl[:, 0, :], ACT.Sigmoid).then_inc(lb_a, 1)
            for b in range(4):
                act.wait_ge(sk_tr, b + 1)
                act.activation(skTs[:, 4 * b:4 * b + 4, :], PS[:, b, :].rearrange("p (a b) -> p a b", a=4), ACT.Copy)\
                   .then_inc(sk_cp, 1)
            act.wait_ge(sk_out, 16)
            act.wait_ge(rel_out, 16)
            leave()

            def norm_tiles(g, s):
                tiles = GROUPS[g]
                for ti, (tid, rows, c0) in enumerate(tiles):
                    act.activation(xn[0:rows, ti, :], hx[0:rows, ti, :], ACT.Square,
                                   accum_out=ss[0:rows, ti:ti + 1]).then_inc(n_sq, 1)
                act.wait_ge(n_ms, norm_batch[g, s] + 1)
                act.activation(rstd[:, 0:2], ss[:, 0:2], ACT.Sqrt).then_inc(n_rt, 1)

            def sigmoid_gates(g, s, W, half):
                for n in by_stage[g, s][8 * half:8 * half + 8]:
                    if products[n][4] == "gate":
                        act.wait_ge(pj_ready, n + 1)
                        act.activation(sg[:, (products[n][5] - 28) % 8, 0:W], PS[:, n % 2, 0:W], ACT.Sigmoid)\
                           .then_inc(pj_free[n % 2], 1)

            def mix(g):
                tiles = GROUPS[g]
                nt = len(tiles)
                W = width(g)
                enter(act, g, "A")
                act.wait_ge(x_in, x_tiles[g, "A"])
                norm_tiles(g, "A")
                for ti, (tid, rows, c0) in enumerate(tiles):
                    for half in range(2):
                        m = n_tr(g, "A", ti) + half
                        act.wait_ge(tr_ready, m + 1)
                        for k in range(4):
                            kk = 4 * half + k
                            i = act.activation(xnT[:, kk, c0:c0 + rows], PS[:, m % 4, k * P:k * P + rows], ACT.Copy,
                                               scale=gain_mix[:, kk:kk + 1])
                        i.then_inc(tr_free, 1)
                leave()
                yield

                enter(act, g, "B")
                for n in by_stage[g, "B"]:
                    _, _, b, kind, what, c, s, ti = products[n]
                    act.wait_ge(pj_ready, n + 1)
                    if what == "q":
                        i = act.activation(Q[:, c, 0:W], PS[:, n % 2, 0:W], ACT.Copy)
                    elif what == "k":
                        c -= 4
                        first = 0
                        if g == 0:
                            act.activation(kS[:, c, :], PS[:, n % 2, 0:DEC], ACT.Copy)
                            first = DEC
                        t0 = tiles[1 if g == 0 else 0][0] * P
                        i = act.activation(kT[:, c, t0:t0 + W - first], PS[:, n % 2, first:W], ACT.Copy)
                    else:
                        tid, rows, _ = tiles[ti]
                        dst = vS if tid == SAMPLE else v[:, tid, :]
                        i = act.activation(dst[0:rows, c - 1024:c - 768], PS[0:rows, n % 2, 0:256], ACT.Copy)
                    i.then_inc(pj_free[n % 2], 1)
                    if n == by_stage[g, "B"][7]:
                        yield
                kt = kt_before[g]
                for i_, ti in enumerate(k_tiles[g]):
                    tid, rows, _ = tiles[ti]
                    act.wait_ge(kt_tr, kt + i_ + 1)
                    act.activation(T2[0:rows, ti, :], PS[0:rows, 2 + i_, :], ACT.Copy).then_inc(kt_cp, 1)
                if g == 0:
                    for t in range(4):
                        act.wait_ge(kt_tr, kt + len(k_tiles[g]) + t + 1)
                        act.activation(kT[:, :, REACH + t * P:REACH + (t + 1) * P],
                                       PS[:, 4 + t, :].rearrange("p (c t) -> p c t", c=CB), ACT.Copy).then_inc(kt_cp, 1)
                leave()
                yield

                enter(act, g, "C")

                def exps(i, step):
                    _, h, ti = step
                    rows, w = geometry(g, ti)
                    act.wait_ge(at_max, i + 1)
                    act.activation(sc[0:rows, i % 2, 0:w], sc[0:rows, i % 2, 0:w], ACT.Exp,
                                   bias=nmax[0:rows, i % 2:i % 2 + 1],
                                   accum_out=rsum[0:rows, i % 2:i % 2 + 1]).then_inc(at_exp, 1)

                def turned(i, step):
                    _, h, ti = step
                    rows, w = geometry(g, ti)
                    act.wait_ge(at_pT, i + 1)
                    if i >= 2:
                        act.wait_ge(at_pv, i - 1)
                    flat = PS[:, 6:8, :].rearrange("p a b -> p (a b)")
                    if rows == P:
                        j = act.activation(pt[:, i % 2, 0:w], flat[:, 0:w], ACT.Copy)
                    else:
                        act.activation(pt[:, i % 2, 0:512].rearrange("p (a b) -> p a b", b=P)[:, :, 0:rows],
                                       flat[:, 0:512].rearrange("p (a b) -> p a b", b=P)[:, :, 0:rows], ACT.Copy)
                        j = act.activation(pt[0:DEC, i % 2, 512:512 + rows], flat[0:DEC, 512:512 + rows], ACT.Copy)
                    j.then_inc(at_ptc, 1)

                steps = [s for s in att if s[0] == g]
                for k in range(len(steps) + 1):
                    if k < len(steps):
                        exps(att_no[steps[k]], steps[k])
                    if k >= 1:
                        turned(att_no[steps[k - 1]], steps[k - 1])
                    if k == len(steps):
                        leave()
                    if k >= 1 and k % 4 == 0:
                        yield

                enter(act, g, "D")
                for ti, (tid, rows, c0) in enumerate(tiles):
                    act.wait_ge(oT_tr, tile_no[g, ti] + 1)
                    act.activation(Q[:, :, c0:c0 + rows],
                                   PS[:, 2 + ti, :].rearrange("p (c t) -> p c t", c=CB)[:, :, 0:rows], ACT.Copy)\
                       .then_inc(oT_cp, 1)
                sigmoid_gates(g, "D", W, 0)
                yield
                sigmoid_gates(g, "D", W, 1)
                leave()
                yield

                enter(act, g, "E")
                if any(k_tiles[q] for q in range(g + 1)):
                    act.wait_ge(kv_out, 32 * sum(len(k_tiles[q]) for q in range(g + 1)))
                for n in by_stage[g, "E"]:
                    _, _, b, kind, what, c, s, ti = products[n]
                    act.wait_ge(pj_ready, n + 1)
                    if what == "f":
                        i = act.activation(Q[:, c - 12, 0:W], PS[:, n % 2, 0:W], ACT.Sigmoid)
                    elif what == "qb":
                        i = act.activation(Q2[:, c - 20, 0:W], PS[:, n % 2, 0:W], ACT.Silu)
                    elif what == "i":
                        rows = tiles[ti][1]
                        i = act.activation(T1[0:rows, ti, c - 2048:c - 1792], PS[0:rows, n % 2, 0:256], ACT.Copy)
                    else:
                        rows = tiles[ti][1]
                        i = act.activation(T2[0:rows, ti, c - 3072:c - 2816], PS[0:rows, n % 2, 0:256], ACT.Silu)
                    i.then_inc(pj_free[n % 2], 1)
                    if n == by_stage[g, "E"][7]:
                        act.wait_ge(f_fg, g + 1)
                        act.activation(Q[:, :, 0:W], K2[:, :, 0:W], ACT.Ln).then_inc(f_ln, 1)
                        yield
                leave()
                yield

                enter(act, g, "F")
                for ti, (tid, rows, c0) in enumerate(tiles):
                    ft = tile_no[g, ti]
                    act.wait_ge(hg_D, ft + 1)
                    view = E[:, :, :, :].rearrange("p l h t -> p (l h) t")[:, :, 0:rows]
                    act.activation(view, view, ACT.Exp)
                    act.activation(ecum[:, :, 0:rows], Q[:, :, c0:c0 + rows], ACT.Exp).then_inc(hg_E, 1)
                    yield
                    for h in range(HB):
                        fh = ft * HB + h
                        act.wait_ge(hg_kdT, fh + 1)
                        if fh >= 1:
                            act.wait_ge(hg_st, fh)
                        act.activation(kdT[0:rows, :], PS[0:rows, 5, 0:P], ACT.Copy).then_inc(hg_kdc, 1)
                        act.wait_ge(hg_o, fh + 1)
                        if h == 0 and ft >= 1:
                            act.wait_ge(hg_oT, ft)
                        act.activation(ob[0:rows, h, :], PS[0:rows, 4, 0:P], ACT.Copy)
                        if fh >= 1:
                            act.wait_ge(hg_oc, fh)
                        act.activation(junk[0:rows, :], PS[0:rows, 4, 0:P], ACT.Square,
                                       accum_out=ssq[0:rows, h:h + 1]).then_inc(hg_oc, 1)
                        if h == 1:
                            yield
                    act.wait_ge(hg_ms, ft + 1)
                    act.activation(rsq[0:rows, :], ssq[0:rows, :], ACT.Sqrt).then_inc(hg_rt, 1)
                    act.wait_ge(hg_oT, ft + 1)
                    act.activation(Q2[:, :, c0:c0 + rows],
                                   PS[:, 5, :].rearrange("p (c t) -> p c t", c=CB)[:, :, 0:rows], ACT.Copy)\
                       .then_inc(hg_obc, 1)
                    if ti == nt - 1:
                        leave()
                    yield

                enter(act, g, "G")
                sigmoid_gates(g, "G", W, 0)
                yield
                sigmoid_gates(g, "G", W, 1)
                leave()
                yield

                enter(act, g, "H")
                yield
                for n in by_stage[g, "H"][-2:]:
                    act.wait_ge(pj_free[n % 2], n // 2 + 1)
                norm_tiles(g, "H")
                for ti, (tid, rows, c0) in enumerate(tiles):
                    for half in range(2):
                        m = n_tr(g, "H", ti) + half
                        act.wait_ge(tr_ready, m + 1)
                        act.activation(xnT[:, 4 * half:4 * half + 4, c0:c0 + rows],
                                       PS[:, m % 4, :].rearrange("p (c t) -> p c t", c=4)[:, :, 0:rows], ACT.Copy)\
                           .then_inc(tr_free, 1)
                leave()
                yield

                enter(act, g, "I")
                act.wait_ge(h_out, 32 * (tile_no[g, len(tiles) - 1] + 1))
                qn = by_stage[g, "I"]

                def copy_scores(i):
                    h, ti = divmod(i, nt)
                    rows = tiles[ti][1]
                    if ti == 0:
                        for p in range(2):
                            n = qn[2 * h + p]
                            act.wait_ge(pj_ready, n + 1)
                            if h >= 2:
                                act.wait_ge(tk_sc, top_no[g, h - 2, nt - 1] + 1)
                            act.activation(qp[:, h % 2, p, 0:W], PS[:, n % 2, 0:W], ACT.Copy).then_inc(pj_free[n % 2], 1)
                    o = top_no[g, h, ti]
                    act.wait_ge(tk_sc, o + 1)
                    if o >= 2:
                        act.wait_ge(tk_done, o - 1)
                    act.activation(s1[0:rows, o % 2], PS[0:rows, 2 + o % 2, 0:2 * P]
                                   .rearrange("p (a b) -> p a b", a=2), ACT.Copy).then_inc(tk_cp, 1)

                copy_scores(0)
                for i in range(PH * nt):
                    if i + 1 < PH * nt:
                        copy_scores(i + 1)
                    h, ti = divmod(i, nt)
                    rows = tiles[ti][1]
                    o = top_no[g, h, ti]
                    act.wait_ge(tk_cv, o + 1)
                    act.activation(ge[0:rows, :], cv[0:rows, :], ACT.Exp, bias=ncv[0:rows, :],
                                   accum_out=gsum[0:rows, :]).then_inc(tk_exp, 1)
                    if i == PH * nt - 1:
                        leave()
                    yield

            ended = []

            def unit(m, kind, tn, h):
                pass

            def tail(m, kind, tn, h):
                rows = tile_rows[tn]
                if kind == "u":
                    q = tn * PH + h
                    act.wait_ge(ring_used, R + TOPK * (m + 1))
                    act.activation(glu[0:rows, q % 2, :], hid[0:rows, q % 2, :], ACT.Gelu).then_inc(e_gelu, 1)
                for t, last in ended:
                    finish_tile(t, m - last)
                if kind == "v" and h == PH - 1:
                    ended.append((tn, m))
                    finish_tile(tn, 0)

            def finish_tile(tn, step):
                rows, s = tile_rows[tn], tn % 2
                if step == 0:
                    act.wait_ge(ring_used, R + TOPK * (ended[-1][1] + 1))
                    act.activation(xt[0:rows, s, :], acc[0:rows, s, :], ACT.Square,
                                   accum_out=esum[0:rows, s:s + 1]).then_inc(e_sq, 1)
                elif step == 1:
                    act.wait_ge(e_ms, tn + 1)
                    act.activation(erstd[0:rows, s:s + 1], esum[0:rows, s:s + 1], ACT.Sqrt).then_inc(e_rt, 1)
                elif step == 2:
                    tid = tile_ids[tn]
                    act.wait_ge(e_y, tn + 1)
                    act.dma_start(rows_of(y_prompt[0], y_sample[0], tid), acc[0:rows, s, :]).then_inc(y_out, 16)

            m = interleave(mix, unit, tail)
            for step in (1, 2):
                finish_tile(ended[-1][0], step)

        @block.vector
        def _(dve):
            chain = [0]

            def link(ins):
                chain[0] += 1
                ins.then_inc(dve_chain, 1)
                dve.wait_ge(dve_chain, chain[0])

            def leave():
                dve.memset(mark_d[:, :], 0.0).then_inc(bar_dve, 1)

            dve.wait_ge(rel_in, 16)
            dve.tensor_copy(rel[:, 0:383], rel[:, 383:384].to_broadcast([HA, 383])).then_inc(relE, 1)
            dve.memset(bias[:, :, :], NEG)
            dve.memset(S_tile[:, :, 0, :], 0.0)
            dve.memset(ss[:, :], 1.0)
            dve.memset(restart[:, :], 1.0).then_inc(dve_chain, 1)
            chain[0] += 1
            dve.wait_ge(dve_chain, chain[0])
            link(dve.memset(restart[:, :].rearrange("p (c t) -> p c t", t=CH)[:, :, 0:1], 0.0))
            dve.wait_ge(const_in, 80)
            dve.tensor_tensor(lbl[:, 0, :], lbl[:, 0, :], lbl[:, 1, :], ALU.subtract).then_inc(lb_d, 1)
            dve.wait_ge(lb_a, 1)
            link(dve.tensor_scalar(one_lb[:, :], lb[:, :], -1.0, 1.0, ALU.mult, ALU.add))
            leave()

            def norm_scale(g, s):
                tiles = GROUPS[g]
                dve.wait_ge(n_sq, norm_no[g, s, len(tiles) - 1] + 1)
                dve.tensor_scalar(ss[:, 0:2], ss[:, 0:2], 1.0 / D, EPS, ALU.mult, ALU.add).then_inc(n_ms, 1)
                dve.wait_ge(n_rt, norm_batch[g, s] + 1)
                link(dve.reciprocal(rstd[:, 0:2], rstd[:, 0:2]))

            def gated(g, stage, W, half):
                for n in by_stage[g, stage][8 * half:8 * half + 8]:
                    _, _, b, kind, what, c, s, ti = products[n]
                    if what != "branch":
                        continue
                    dve.wait_ge(pj_ready, n + 1)
                    gn = gate_product(g, stage, c)
                    dve.wait_ge(pj_free[gn % 2], gn // 2 + 1)
                    if stage == "D":
                        dve.tensor_tensor(M[:, c, 0:W], PS[:, n % 2, 0:W], sg[:, c, 0:W], ALU.mult)\
                           .then_inc(pj_free[n % 2], 1)
                    else:
                        dve.tensor_tensor(sg[:, c, 0:W], PS[:, n % 2, 0:W], sg[:, c, 0:W], ALU.mult)\
                           .then_inc(pj_free[n % 2], 1)
                        dve.wait_ge(pj_free[n % 2], n // 2 + 1)
                        dve.tensor_tensor(M[:, c, 0:W], M[:, c, 0:W], sg[:, c, 0:W], ALU.add)

            def mix(g):
                tiles = GROUPS[g]
                W = width(g)
                nt = len(tiles)
                enter(dve, g, "A")
                norm_scale(g, "A")
                for ti, (tid, rows, c0) in enumerate(tiles):
                    dve.tensor_scalar(xn[0:rows, ti, :], hx[0:rows, ti, :], rstd[0:rows, ti:ti + 1], None, ALU.mult)\
                       .then_inc(xn_ready, 1)
                leave()
                yield
                enter(dve, g, "B")
                yield
                leave()
                yield

                enter(dve, g, "C")

                def bias_max(i, step):
                    _, h, ti = step
                    rows, w = geometry(g, ti)
                    bh = g * HA + h
                    dve.wait_ge(at_sc, i + 1)
                    dve.wait_ge(bias_in[bh % 2], 32 * (bh // 2 + 1))
                    if i >= 2:
                        dve.wait_ge(at_pT, i - 1)
                    b0 = 2 + 2 * (i % 2)
                    flat = PS[:, b0:b0 + 2, :].rearrange("p a b -> p (a b)")
                    off = WIN - w if rows == P else 0
                    dve.scalar_tensor_tensor(out=sc[0:rows, i % 2, 0:w], in0=flat[0:rows, 0:w], scalar=SCALE,
                                             in1=bias[0:rows, bh % 2, off:off + w], op0=ALU.mult, op1=ALU.add)\
                       .then_inc(at_biased, 1)
                    dve.wait_ge(at_biased, i + 1)
                    if i >= 2:
                        dve.wait_ge(at_exp, i - 1)
                    dve.tensor_reduce(nmax[0:rows, i % 2:i % 2 + 1], sc[0:rows, i % 2, 0:w], AX, ALU.max,
                                      negate=True).then_inc(at_max, 1)

                def scale_out(i, step):
                    _, h, ti = step
                    rows, w = geometry(g, ti)
                    dve.wait_ge(at_exp, i + 1)
                    dve.reciprocal(rinv[0:rows, i % 2:i % 2 + 1], rsum[0:rows, i % 2:i % 2 + 1]).then_inc(at_rinv, 1)
                    dve.wait_ge(at_rinv, i + 1)
                    dve.wait_ge(at_pv, i + 1)
                    dve.tensor_scalar(T1[0:rows, ti, h * 64:(h + 1) * 64], PS[0:rows, i % 2, 0:64],
                                      rinv[0:rows, i % 2:i % 2 + 1], None, ALU.mult).then_inc(at_oa, 1)

                steps = [s for s in att if s[0] == g]
                for k in range(len(steps) + 1):
                    if k < len(steps):
                        bias_max(att_no[steps[k]], steps[k])
                    if k >= 1:
                        scale_out(att_no[steps[k - 1]], steps[k - 1])
                    if k == len(steps):
                        leave()
                    if k >= 1 and k % 4 == 0:
                        yield

                enter(dve, g, "D")
                gated(g, "D", W, 0)
                yield
                gated(g, "D", W, 1)
                leave()
                yield

                enter(dve, g, "E")
                fn = [n for n in by_stage[g, "E"] if products[n][4] == "f"]
                for h, n in enumerate(fn):
                    dve.wait_ge(pj_free[n % 2], n // 2 + 1)
                    i = dve.tensor_scalar(K2[:, h, 0:W], Q[:, h, 0:W], one_lb[:, h:h + 1], lb[:, h:h + 1],
                                          ALU.mult, ALU.add)
                i.then_inc(f_fg, 1)
                dve.wait_ge(f_ln, g + 1)
                link(dve.tensor_scalar(K2[:, :, 0:W], K2[:, :, 0:W], -1.0, 1.0, ALU.mult, ALU.add))
                for h in range(HB):
                    dve.tensor_tensor_scan(Q[:, h, 0:W], restart[:, 0:W], Q[:, h, 0:W], 0.0, ALU.mult, ALU.add)
                yield
                gn = [n for n in by_stage[g, "E"] if products[n][4] == "g"]
                for n in gn[-2:]:
                    dve.wait_ge(pj_free[n % 2], n // 2 + 1)
                for ti, (tid, rows, c0) in enumerate(tiles):
                    dve.tensor_tensor(T2[0:rows, ti, :], T2[0:rows, ti, :], gain_hgrn[0:rows, :], ALU.mult)
                leave()
                yield

                enter(dve, g, "F")
                dve.wait_ge(state_loaded, 16)
                for ti, (tid, rows, c0) in enumerate(tiles):
                    ft = tile_no[g, ti]
                    nch = rows // CH
                    if ft >= 1:
                        dve.wait_ge(hg_o, HB * ft)
                    cum = Q[:, :, c0:c0 + rows]
                    for lev, s in enumerate(LEVELS):
                        nb = rows // (2 * s)
                        c4 = cum.rearrange("p h (b t s) -> p h b t s", t=2, s=s)
                        e4 = E[:, lev, :, 0:rows].rearrange("p h (b t s) -> p h b t s", t=2, s=s)
                        ref = c4[:, :, :, 0, s - 1:s].to_broadcast([P, HB, nb, s])
                        dve.tensor_tensor(e4[:, :, :, 1, :], c4[:, :, :, 1, :], ref, ALU.subtract)
                        dve.tensor_tensor(e4[:, :, :, 0, :], ref, c4[:, :, :, 0, :], ALU.subtract)
                    c3 = cum.rearrange("p h (b s) -> p h b s", s=CH)
                    dve.tensor_tensor(E[:, NL, :, 0:rows].rearrange("p h (b s) -> p h b s", s=CH),
                                      c3[:, :, :, CH - 1:CH].to_broadcast([P, HB, nch, CH]), c3,
                                      ALU.subtract).then_inc(hg_D, 1)
                    dve.wait_ge(hg_E, ft + 1)
                    link(dve.tensor_copy(elast[:, :, 0:nch], ecum[:, :, CH - 1:rows:CH]))
                    dve.tensor_tensor(E[:, NL, :, 0:rows], E[:, NL, :, 0:rows], K2[:, :, c0:c0 + rows], ALU.mult)
                    dve.tensor_tensor(ecum[:, :, 0:rows], ecum[:, :, 0:rows], Q2[:, :, c0:c0 + rows], ALU.mult)\
                       .then_inc(hg_kq, 1)
                    yield
                    for h in range(HB):
                        fh = ft * HB + h
                        if fh >= 1:
                            dve.wait_ge(hg_at, fh)
                        dve.tensor_tensor(Lq[:, :, 0:rows], E[:, 0:NL, h, 0:rows],
                                          Q2[:, h:h + 1, c0:c0 + rows].to_broadcast([P, NL, rows]), ALU.mult)
                        dve.tensor_tensor(Lk[:, :, 0:rows], E[:, 0:NL, h, 0:rows],
                                          K2[:, h:h + 1, c0:c0 + rows].to_broadcast([P, NL, rows]), ALU.mult)\
                           .then_inc(hg_L, 1)
                        dve.wait_ge(hg_at, fh + 1)
                        b0 = 2 * (fh % 2)
                        at = PS[:, b0:b0 + 2, :].rearrange("p a (b t) -> p (a b) t", t=P)[0:rows, 0:NL + 1, 0:rows]
                        link(dve.tensor_tensor(Am[0:rows, :, 0:rows], at, masks[0:rows, :, 0:rows], ALU.mult))
                        if fh >= 2:
                            dve.wait_ge(hg_o, fh - 1)
                        dve.tensor_reduce(attnT[0:rows, fh % 2, 0:rows],
                                          Am[0:rows, :, 0:rows].rearrange("p l t -> p t l"), AX, ALU.add)\
                           .then_inc(hg_red, 1)
                        dve.wait_ge(hg_st, fh + 1)
                        if ft >= 1:
                            dve.wait_ge(hg_o, fh - 3)
                        if ft == 1:
                            dve.wait_ge(st_out, 16)
                        s_in = S_tile[:, h, 1 if tid == SAMPLE else tid % 2, :]
                        i = dve.scalar_tensor_tensor(out=S_mid[:, h, :], in0=s_in, scalar=elast[:, h, 0:1],
                                                     in1=PS[:, 6, 0:P], op0=ALU.mult, op1=ALU.add)
                        if nch == 2:
                            link(i)
                            i = dve.scalar_tensor_tensor(out=S_tile[:, h, (tid + 1) % 2, :], in0=S_mid[:, h, :],
                                                         scalar=elast[:, h, 1:2], in1=PS[:, 7, 0:P],
                                                         op0=ALU.mult, op1=ALU.add)
                        i.then_inc(hg_S, 1)
                        if h == 1:
                            yield
                    dve.wait_ge(hg_oc, HB * ft + HB)
                    dve.tensor_scalar(ssq[0:rows, :], ssq[0:rows, :], 1.0 / P, EPS, ALU.mult, ALU.add).then_inc(hg_ms, 1)
                    dve.wait_ge(hg_rt, ft + 1)
                    link(dve.reciprocal(rsq[0:rows, :], rsq[0:rows, :]))
                    link(dve.tensor_tensor(ob[0:rows], ob[0:rows], rsq[0:rows, :].unsqueeze(2).to_broadcast([rows, HB, P]),
                                           ALU.mult))
                    dve.tensor_tensor(ob[0:rows].rearrange("p h d -> p (h d)"), ob[0:rows].rearrange("p h d -> p (h d)"),
                                      T2[0:rows, ti, :], ALU.mult).then_inc(hg_ob, 1)
                    if ti == nt - 1:
                        leave()
                    yield

                enter(dve, g, "G")
                gated(g, "G", W, 0)
                yield
                gated(g, "G", W, 1)
                leave()
                yield

                enter(dve, g, "H")
                dve.wait_ge(x_in, x_tiles[g, "H"])
                for n in by_stage[g, "H"]:
                    _, _, b, kind, what, c, s, ti = products[n]
                    rows = tiles[ti][1]
                    dve.wait_ge(pj_ready, n + 1)
                    dve.tensor_tensor(hx[0:rows, ti, c:c + 256], PS[0:rows, n % 2, 0:256], hx[0:rows, ti, c:c + 256],
                                      ALU.add).then_inc(pj_free[n % 2], 1)
                    if n == by_stage[g, "H"][2 * nt - 1]:
                        yield
                norm_scale(g, "H")
                for ti, (tid, rows, c0) in enumerate(tiles):
                    dve.scalar_tensor_tensor(out=xn[0:rows, ti, :], in0=hx[0:rows, ti, :], scalar=rstd[0:rows, ti:ti + 1],
                                             in1=gain_ffn[0:rows, :], op0=ALU.mult, op1=ALU.mult).then_inc(xn_ready, 1)
                leave()
                yield

                enter(dve, g, "I")
                dve.wait_ge(h_out, 32 * (tile_no[g, nt - 1] + 1))
                for h in range(PH):
                    for ti, (tid, rows, c0) in enumerate(tiles):
                        o = top_no[g, h, ti]
                        r = slice(0, rows)
                        dve.wait_ge(tk_cp, o + 1)
                        for p in range(2):
                            i = dve.max(sv[r, p, 0:8], s1[r, o % 2, p, :])
                        link(i)
                        for p in range(2):
                            dve.max_index(si[r, p, 0:8], sv[r, p, 0:8], s1[r, o % 2, p, :])
                            i = dve.match_replace(s2[r, p, :], sv[r, p, 0:8], s1[r, o % 2, p, :], LOWEST)
                        link(i)
                        for p in range(2):
                            i = dve.max(sv[r, p, 8:16], s2[r, p, :])
                        link(i)
                        for p in range(2):
                            i = dve.max_index(si[r, p, 8:16], sv[r, p, 8:16], s2[r, p, :])
                        link(i)
                        dve.tensor_copy(sif[r], si[r])
                        link(dve.tensor_tensor(comb[r], sv[r, 0, :].unsqueeze(2).to_broadcast([rows, TOPK, TOPK]),
                                               sv[r, 1:2, :].to_broadcast([rows, TOPK, TOPK]), ALU.add))
                        cf = comb[r].rearrange("p a b -> p (a b)")
                        if o >= 1:
                            dve.wait_ge(tk_exp, o)
                        link(dve.max(cv[r, 0:8], cf))
                        dve.max_index(ci[r, 0:8], cv[r, 0:8], cf)
                        link(dve.match_replace(comb2[r], cv[r, 0:8], cf, LOWEST))
                        dve.tensor_scalar(ncv[r], cv[r, 0:1], -1.0, None, ALU.mult)
                        link(dve.max(cv[r, 8:16], comb2[r]))
                        link(dve.max_index(ci[r, 8:16], cv[r, 8:16], comb2[r]))
                        dve.tensor_scalar(ab[r, 0, :], ci[r], 4, None, ALU.logical_shift_right).then_inc(tk_cv, 1)
                        link(dve.tensor_scalar(ab[r, 1, :], ci[r], 15, None, ALU.bitwise_and))
                        link(dve.tensor_copy(abf[r], ab[r]))
                        for p in range(2):
                            i = dve.tensor_tensor(eq[r, p], abf[r, p, :].unsqueeze(2).to_broadcast([rows, TOPK, TOPK]),
                                                  iota16[r, :].unsqueeze(1).to_broadcast([rows, TOPK, TOPK]),
                                                  ALU.is_equal)
                        link(i)
                        for p in range(2):
                            i = dve.tensor_tensor(eq[r, p], eq[r, p], sif[r, p:p + 1, :].to_broadcast([rows, TOPK, TOPK]),
                                                  ALU.mult)
                        link(i)
                        link(dve.tensor_reduce(i12[r], eq[r], AX, ALU.add))
                        at = tile_no[g, ti] * P + h * TOPK
                        dve.scalar_tensor_tensor(out=idx[r, at:at + TOPK], in0=i12[r, 0, :], scalar=128.0, in1=i12[r, 1, :],
                                                 op0=ALU.mult, op1=ALU.add)
                        dve.wait_ge(tk_exp, o + 1)
                        link(dve.reciprocal(ginv[r], gsum[r]))
                        dve.tensor_scalar(gates[r, at:at + TOPK], ge[r], ginv[r], None, ALU.mult).then_inc(tk_done, 1)
                        if h == PH - 1 and ti == nt - 1:
                            leave()
                        yield

            dve.memset(hid[:, :, :], 0.0).then_inc(ring_used, R)
            dve.wait_ge(ring_used, R)

            def unit(m, kind, tn, h):
                rows, q, s = tile_rows[tn], tn * PH + h, tn % 2
                if kind == "u":
                    dve.wait_ge(xt_in[s], 32 * (tn // 2 + 1))
                else:
                    dve.wait_ge(e_gelu, q + 1)
                    dve.tensor_tensor(wk[0:rows, q % 2, :], glu[0:rows, q % 2, :], gates[0:rows, q * TOPK:(q + 1) * TOPK],
                                      ALU.mult).then_inc(e_w, 1)
                    dve.wait_ge(e_w, q + 1)
                for k in range(TOPK):
                    dve.wait_ge(row_in[k % R], 16 * (TOPK // R * m + k // R + 1))
                    row = ring[0:rows, k % R, :]
                    if kind == "u":
                        dve.tensor_tensor_reduce(row, row, xt[0:rows, s, :], 1.0, 0.0, ALU.mult, ALU.add,
                                                 hid[0:rows, q % 2, k:k + 1]).then_inc(ring_used, 1)
                    else:
                        dve.wait_ge(ring_used, R + TOPK * m + k)
                        dve.scalar_tensor_tensor(out=acc[0:rows, s, :], in0=row, scalar=wk[0:rows, q % 2, k:k + 1],
                                                 in1=acc[0:rows, s, :], op0=ALU.mult, op1=ALU.add)\
                           .then_inc(ring_used, 1)

            ended = []

            def tail(m, kind, tn, h):
                for t, last in ended:
                    finish_tile(t, m - last)
                if kind == "v" and h == PH - 1:
                    ended.append((tn, m))

            def finish_tile(tn, step):
                rows, s = tile_rows[tn], tn % 2
                if step == 1:
                    dve.wait_ge(e_sq, tn + 1)
                    dve.tensor_scalar(esum[0:rows, s:s + 1], esum[0:rows, s:s + 1], 1.0 / D, EPS, ALU.mult, ALU.add)\
                       .then_inc(e_ms, 1)
                elif step == 2:
                    dve.wait_ge(e_rt, tn + 1)
                    dve.reciprocal(erstd[0:rows, s:s + 1], erstd[0:rows, s:s + 1]).then_inc(e_rs, 1)
                    dve.wait_ge(e_rs, tn + 1)
                    dve.scalar_tensor_tensor(out=acc[0:rows, s, :], in0=acc[0:rows, s, :], scalar=erstd[0:rows, s:s + 1],
                                             in1=gain_final[0:rows, :], op0=ALU.mult, op1=ALU.mult).then_inc(e_y, 1)

            interleave(mix, unit, tail)
            for step in (1, 2):
                finish_tile(ended[-1][0], step)


_INS = ["x_prompt", "x_sample", "cache_attn_k", "cache_attn_v", "state_hgrn", "norm_mix", "w_in", "rel_bias",
        "lb_logits", "hgrn_norm", "w_branch_a", "w_branch_b", "w_out", "norm_ffn", "peer_query", "peer_subkeys",
        "peer_u", "peer_v", "norm_final"]
_FLAT = {"peer_u": 1, "peer_v": 1}
_OUTS = [(1, SEQ, D), (1, DEC, D), (1, 1, 512, HA, 64), (1, 1, 512, HA, 64), (1, 1, HB, P, P),
         (1, 1, DEC, HA, 64), (1, 1, DEC, HA, 64), (1, 1, HB, P, P)]


def kernel(**inputs):
    import numpy as _np
    import concourse.bacc as _bacc
    from concourse import mybir as _mybir
    from concourse.bass_utils import run_bass_kernel_spmd as _run

    nc = _bacc.Bacc("TRN2", target_bir_lowering=False, num_devices=1)
    arrays, args = {}, []
    for name in _INS:
        a = _np.ascontiguousarray(inputs[name])
        if name in _FLAT:
            a = a[0]
        arrays[f"in_{name}"] = a
        args.append(nc.dram_tensor(f"in_{name}", a.shape, _mybir.dt.from_np(a.dtype), kind="ExternalInput").ap())
    for i, shape in enumerate(_OUTS):
        args.append(nc.dram_tensor(f"out_{i}", shape, _mybir.dt.float32, kind="ExternalOutput").ap())
    build(nc, *args)
    r = _run(nc, [arrays], core_ids=[0])
    got = [r.results[0][f"out_{i}"] for i in range(len(_OUTS))]
    return tuple(got)
```

```python
from contextlib import ExitStack

import concourse.bass as bass
from concourse import mybir

F32 = mybir.dt.float32
U32 = mybir.dt.uint32
ALU = mybir.AluOpType
ACT = mybir.ActivationFunctionType
AX = mybir.AxisListType.X

P = 128
D = 1024
DK = D // P
SEQ = 1024
DEC = 64
CH = 64
HA = 8
DA = 512
CB = DA // P
HB = 4
EPS = 1e-6
NREL = 513
CLIP = 256
REACH = 512
WIN = 640
SCALE = 64 ** -0.5
NEG = -1e30
LOWEST = -3.0e38
NEXP = 16384
PH = 8
TOPK = 16
NL = 6
LEVELS = [32, 16, 8, 4, 2, 1]
SAMPLE = 8
GROUPS = [[(SAMPLE, 64, 0), (0, 128, 64)], [(1, 128, 0), (2, 128, 128)], [(3, 128, 0), (4, 128, 128)],
          [(5, 128, 0), (6, 128, 128)], [(7, 128, 0)]]
NG = len(GROUPS)
WG = 256
STAGES = "ABCDEFGHI"
KV = 6
CACHE = 2
NW = 3
R = 8


def width(g):
    return sum(t[1] for t in GROUPS[g])


def slices(g):
    nt = len(GROUPS[g])
    rate = width(g) / 256
    branch = [8 * rate, 8 * rate] * 2
    return ([10] + [14 * rate] * 3 + [15] * (HA * nt // 4) + branch + [8 * rate, 8 * rate, 6 * rate, 6 * rate]
            + [10,11,12] * nt + branch + [12 * rate, 12 * rate, 12 * rate] + [10.5] * (PH * nt))


def expert_units(g):
    heads = [tn * PH + h for tn in tiles_of(g) for h in range(PH)]
    units = [(heads[0], None, None), (heads[1], None, None)]
    for q in heads[:-2]:
        units += [(q + 2, q, 0), (q + 2, q, 1)]
    return units + [(None, heads[-2], None), (None, heads[-1], None)]


def unit_rows(uq, vq, half):
    if half is None:
        return [("u", uq, k) if vq is None else ("v", vq, k) for k in range(TOPK)]
    return [row for k in range(half * TOPK // 2, (half + 1) * TOPK // 2) for row in (("u", uq, k), ("v", vq, k))]


def tiles_of(g):
    first = sum(len(GROUPS[q]) for q in range(g))
    return range(first, first + len(GROUPS[g]))


def interleave(mix, unit, tail, meanwhile=None):
    done = sum(1 for rows in mix(0) if rows is None)
    assert done == len(slices(0)), (done, len(slices(0)))
    m = 0
    for g in range(NG):
        units = expert_units(g)
        costs = slices(g + 1) if g + 1 < NG else []
        steps = mix(g + 1) if g + 1 < NG else iter(())
        spent = at = 0
        for u, now in enumerate(units):
            unit(m, *now)
            while at < len(costs) and spent < sum(costs) * (u + 1) / len(units):
                rows = next(steps)
                while rows is not None:
                    for n in (1, 2):
                        if u + n < len(units) and (units[u + n][1] is None or
                                                   all(x[0] != units[u + n][1] for x in units[u:])):
                            rows = meanwhile(m + n, *units[u + n], rows)
                    rows = next(steps)
                spent += costs[at]
                at += 1
            tail(m, *now)
            m += 1
        for _ in steps:
            raise AssertionError("slices are left")
    return m


def stage_no(g, s):
    return 1 + g * len(STAGES) + STAGES.index(s)


def plan_projections():
    blocks, products = [], []

    def add(g, stage, w, nk, c0, nc_, kind, what):
        b = len(blocks)
        blocks.append((w, nk, c0, nc_))
        if kind == "fm":
            for s in range(nc_ // P):
                products.append((g, stage, b, "fm", what, c0 // P + s, s, None))
        else:
            for ti in range(len(GROUPS[g])):
                products.append((g, stage, b, "tm", what, c0, 0, ti))

    for g in range(len(GROUPS)):
        for c in (0, 256):
            add(g, "B", "w_in", 8, c, 256, "fm", "q")
        for c in (512, 768):
            add(g, "B", "w_in", 8, c, 256, "fm", "k")
        for c in (1024, 1280):
            add(g, "B", "w_in", 8, c, 256, "tm", "v")
        for i in range(4):
            add(g, "D", "w_in", 8, 3584 + 256 * i, 256, "fm", "gate")
            if i % 2:
                add(g, "D", "w_a", 4, 512 * (i // 2), 512, "fm", "branch")
        for c in (1536, 1792):
            add(g, "E", "w_in", 8, c, 256, "fm", "f")
        for c in (2560, 2816):
            add(g, "E", "w_in", 8, c, 256, "fm", "qb")
        for c in (2048, 2304):
            add(g, "E", "w_in", 8, c, 256, "tm", "i")
        for c in (3072, 3328):
            add(g, "E", "w_in", 8, c, 256, "tm", "g")
        for i in range(4):
            add(g, "G", "w_in", 8, 4608 + 256 * i, 256, "fm", "gate")
            if i % 2:
                add(g, "G", "w_b", 4, 512 * (i // 2), 512, "fm", "branch")
        for i in range(4):
            add(g, "H", "w_out", 8, 256 * i, 256, "tm", "o")
        for i in range(8):
            add(g, "I", "w_query", 8, 256 * i, 256, "fm", "query")
    return blocks, products


def build(nc, x_prompt, x_sample, cache_k, cache_v, state_in, norm_mix, w_in, rel_bias, lb_logits,
          hgrn_norm, w_a, w_b, w_out, norm_ffn, w_query, sub_keys, u_tab, v_tab, norm_final,
          y_prompt, y_sample, k_prompt, v_prompt, state_prompt, k_sample, v_sample, state_sample):
    weights = {"w_in": w_in[0], "w_a": w_a[0], "w_b": w_b[0], "w_out": w_out[0], "w_query": w_query[0]}
    xp, xs = x_prompt[0], x_sample[0]
    blocks, products = plan_projections()
    last_product = {}
    for n, pr in enumerate(products):
        last_product[pr[2]] = n
    by_stage = {}
    for n, pr in enumerate(products):
        by_stage.setdefault((pr[0], pr[1]), []).append(n)
    att = [(g, h, ti) for g in range(NG) for h in range(HA) for ti in range(len(GROUPS[g]))]
    att_no = {s: n for n, s in enumerate(att)}
    tile_no = {(g, ti): n for n, (g, ti) in enumerate((g, ti) for g in range(NG) for ti in range(len(GROUPS[g])))}
    norm_no = {}
    for g in range(NG):
        for s in "AH":
            for ti in range(len(GROUPS[g])):
                norm_no[g, s, ti] = len(norm_no)
    norm_batch = {(g, s): 2 * g + n for g in range(NG) for n, s in enumerate("AH")}
    top_no = {}
    for g in range(NG):
        for h in range(PH):
            for ti in range(len(GROUPS[g])):
                top_no[g, h, ti] = len(top_no)

    h_scr = nc.dram_tensor("h_scr", (SEQ + DEC, D), F32, kind="Internal").ap()
    xn_scr = nc.dram_tensor("xn_scr", (SEQ + DEC, D), F32, kind="Internal").ap()
    rel_scr = nc.dram_tensor("rel_scr", (HA, P, WIN), F32, kind="Internal").ap()
    sk_scr = nc.dram_tensor("sk_scr", (P, 16 * P), F32, kind="Internal").ap()

    def rows_of(ap_prompt, ap_sample, tid):
        return ap_sample if tid == SAMPLE else ap_prompt[tid * P:(tid + 1) * P, :]

    with ExitStack() as ctx:
        def sb(name, shape, dt=F32):
            return ctx.enter_context(nc.sbuf_tensor(name, shape, dt))

        def sem(name):
            return ctx.enter_context(nc.semaphore(name))

        PS = ctx.enter_context(nc.psum_tensor("PS", [P, 8, 512], F32))
        ident = sb("ident", [P, P])
        masks = sb("masks", [P, NL + 1, P])
        gain_mix = sb("gain_mix", [P, DK])
        gain_ffn = sb("gain_ffn", [P, D])
        gain_final = sb("gain_final", [P, D])
        gain_hgrn = sb("gain_hgrn", [P, DA])
        lbl = sb("lbl", [P, 2, HB])
        lb = sb("lb", [P, HB])
        one_lb = sb("one_lb", [P, HB])
        iota16 = sb("iota16", [P, TOPK])
        restart = sb("restart", [P, WG])
        mark_a = sb("mark_a", [P, 1])
        mark_d = sb("mark_d", [P, 1])
        xnT = sb("xnT", [P, DK, WG])
        M = sb("M", [P, DK, WG])
        kT = sb("kT", [P, CB, KV * P])
        v = sb("v", [P, KV, DA])
        kS = sb("kS", [P, CB, DEC])
        vS = sb("vS", [P, DA])
        Q = sb("Q", [P, CB, WG])
        K2 = sb("K2", [P, CB, WG])
        Q2 = sb("Q2", [P, CB, WG])
        T12 = sb("T12", [P, 2, 2, DA])
        T1 = T12[:, 0]
        T2 = T12[:, 1]
        skT = T12[:, :, :, :].rearrange("p a b c -> p (a b c)")
        wring = sb("wring", [P, NW, 2048])
        bias = sb("bias", [P, 2, WIN])
        S_tile = sb("S_tile", [P, HB, 2, P])
        S_mid = sb("S_mid", [P, HB, P])
        idx = sb("idx", [P, 9 * P], U32)
        gates = sb("gates", [P, 9 * P])
        ss = sb("ss", [P, 8])
        rstd = sb("rstd", [P, 8])
        tmp = sb("tmp", [P, 7680])
        ring = sb("ring", [P, R, D])
        xt = sb("xt", [P, 2, D])
        acc = sb("acc", [P, 2, D])
        ixs = sb("ixs", [P, 2, TOPK], U32)
        hid = sb("hid", [P, 2, TOPK])
        glu = sb("glu", [P, 2, TOPK])
        wk = sb("wk", [P, 2, TOPK])
        esum = sb("esum", [P, 2])
        erstd = sb("erstd", [P, 2])

        def part(at, *shape):
            n = 1
            for k in shape:
                n *= k
            ap = tmp[:, at:at + n]
            names = "abcd"[:len(shape)]
            if len(shape) == 1:
                return ap
            return ap.rearrange(f"p ({' '.join(names)}) -> p {' '.join(names)}", **dict(zip(names, shape)))

        hx = part(0, 2, D)
        xn = part(2 * D, 2, D)
        kc = part(0, 4, DA)
        sc = part(0, 2, WIN)
        pt = part(2 * WIN, 2, WIN)
        nmax = part(4 * WIN, 2)
        rsum = part(4 * WIN + 2, 2)
        rinv = part(4 * WIN + 4, 2)
        sg = part(0, DK, WG)
        E = part(0, NL + 1, HB, P)
        Lq = part(3584, NL, P)
        Lk = part(4352, NL, P)
        Am = part(5120, NL + 1, P)
        attnT = part(6016, 2, P)
        ecum = part(6272, HB, P)
        kdT = part(6784, P)
        ob = part(6912, HB, P)
        ssq = part(7424, HB)
        rsq = part(7428, HB)
        elast = part(7432, HB, 2)
        junk = part(7440, P)
        qp = part(4096, 2, 2, WG)
        s1 = part(5120, 2, 2, P)
        s2 = part(5888, 2, P)
        comb = part(6144, TOPK, TOPK)
        comb2 = part(6400, TOPK * TOPK)
        eq = part(6656, 2, TOPK, TOPK)
        sv = part(7168, 2, TOPK)
        sif = part(7200, 2, TOPK)
        cv = part(7232, TOPK)
        abf = part(7248, 2, TOPK)
        i12 = part(7280, 2, TOPK)
        ge = part(7312, TOPK)
        gsum = part(7328, 1)
        ginv = part(7329, 1)
        ncv = part(7330, 1)
        si = part(7336, 2, TOPK).bitcast(U32)
        ci = part(7368, TOPK).bitcast(U32)
        ab = part(7384, 2, TOPK).bitcast(U32)
        rel = tmp[0:HA, 4096:4863]
        sk = M[:, :, :].rearrange("p a (b c) -> p (a b) c", c=P)
        skTs = skT.rearrange("p (a b) -> p a b", a=16)

        const_in, rel_in, sk_in, relE, rel_out, sk_tr, sk_cp, sk_out, consts, lb_d, lb_a, state_loaded = [
            sem(n) for n in ("const_in", "rel_in", "sk_in", "relE", "rel_out", "sk_tr", "sk_cp", "sk_out",
                             "consts", "lb_d", "lb_a", "state_loaded")]
        dve_chain = sem("dve_chain")
        bar_act, bar_dve = sem("bar_act"), sem("bar_dve")
        w_in_sem = [sem(f"w_landed{n}") for n in range(NW)]
        pj_ready = sem("pj_ready")
        pj_free = [sem("pj_free0"), sem("pj_free1")]
        x_in, n_sq, n_ms, n_rt, n_rs, xn_ready, tr_ready = [sem(n) for n in (
            "x_in", "n_sq", "n_ms", "n_rt", "n_rs", "xn_ready", "tr_ready")]
        tr_free = sem("tr_free")
        kc_in, vc_in, kt_tr, kt_cp, kv_out = [sem(n) for n in ("kc_in", "vc_in", "kt_tr", "kt_cp", "kv_out")]
        bias_in = [sem("bias_in0"), sem("bias_in1")]
        at_sc, at_biased, at_max, at_exp, at_pT, at_ptc, at_pv, at_rinv, at_oa = [sem(n) for n in (
            "at_sc", "at_biased", "at_max", "at_exp", "at_pT", "at_ptc", "at_pv", "at_rinv", "at_oa")]
        oT_tr, oT_cp = sem("oT_tr"), sem("oT_cp")
        f_sig, f_fg, f_ln, g_silu = [sem(n) for n in ("f_sig", "f_fg", "f_ln", "g_silu")]
        hg_D, hg_E, hg_kq, hg_L, hg_at, hg_red, hg_kdT, hg_kdc, hg_st, hg_S, hg_o, hg_oc, hg_ms, hg_rt, hg_ob, \
            hg_oT, hg_obc, st_out = [sem(n) for n in (
                "hg_D", "hg_E", "hg_kq", "hg_L", "hg_at", "hg_red", "hg_kdT", "hg_kdc", "hg_st", "hg_S", "hg_o",
                "hg_oc", "hg_ms", "hg_rt", "hg_ob", "hg_oT", "hg_obc", "st_out")]
        h_out = sem("h_out")
        skT_in, tk_sc, tk_cp, tk_done, tk_cv, tk_exp = [sem(n) for n in (
            "skT_in", "tk_sc", "tk_cp", "tk_done", "tk_cv", "tk_exp")]
        xt_in = [sem("xt_in0"), sem("xt_in1")]
        row_in = [sem(f"row_in{r}") for r in range(R)]
        ring_used, ix_ready, e_gelu, e_w, e_sq, e_ms, e_rt, e_y, y_out, e_rs = [sem(n) for n in (
            "ring_used", "ix_ready", "e_gelu", "e_w", "e_sq", "e_ms", "e_rt", "e_y", "y_out", "e_rs")]

        passed, passed_dve, passed_sp = sem("passed"), sem("passed_dve"), sem("passed_sp")

        block = ctx.enter_context(nc.Block())

        def n_tr(g, s, ti):
            return 2 * norm_no[g, s, ti]

        def geometry(g, ti):
            tid, rows, _ = GROUPS[g][ti]
            return rows, (REACH + DEC if tid == SAMPLE else P * (min(tid, 4) + 1))

        def gate_product(g, s, c):
            return [n for n in by_stage[g, s] if products[n][4] == "gate" and (products[n][5] - 28) % 8 == c][0]

        tile_rows = [rows for tiles in GROUPS for _, rows, _ in tiles]
        tile_ids = [tid for tiles in GROUPS for tid, _, _ in tiles]

        def enter(eng, g, s):
            eng.wait_ge(bar_act, stage_no(g, s))
            eng.wait_ge(bar_dve, stage_no(g, s))

        k_tiles = {g: [ti for ti, (tid, _, _) in enumerate(GROUPS[g]) if tid >= 4] for g in range(NG)}
        kt_before = {g: sum(len(k_tiles[q]) for q in range(g)) + (4 if g > 0 else 0) for g in range(NG + 1)}
        x_tiles = {(g, s): 16 * (sum(2 * len(GROUPS[q]) for q in range(g)) + (2 if s == "H" else 1) * len(GROUPS[g]))
                   for g in range(NG) for s in "AH"}

        @block.sync
        def _(sp):
            with nc.allow_non_contiguous_dma(reason="small vectors laid over partitions"):
                sp.dma_start(gain_mix[:, :], norm_mix[0].rearrange("(k p) -> p k", p=P)).then_inc(const_in, 16)
                sp.dma_start(lbl[:, :, :], lb_logits.rearrange("a (h p) -> p a h", p=P)).then_inc(const_in, 16)
                sp.dma_start(rel[:, 383:767], bass.AP(rel_bias.tensor, NREL - 1, [[NREL, HA], [-1, 384]]))\
                  .then_inc(rel_in, 16)
            sp.dma_start(gain_ffn[:, :], bass.AP(norm_ffn.tensor, 0, [[0, P], [1, D]])).then_inc(const_in, 16)
            sp.dma_start(gain_final[:, :], bass.AP(norm_final.tensor, 0, [[0, P], [1, D]])).then_inc(const_in, 16)
            sp.dma_start(gain_hgrn[:, :], bass.AP(hgrn_norm.tensor, 0, [[0, P], [1, DA]])).then_inc(const_in, 16)
            sp.dma_start(sk, sub_keys[0].rearrange("a h k d -> k (a h) d")).then_inc(sk_in, 16)
            sp.dma_start(S_tile[:, :, 1, :], state_in[0, 0].rearrange("h k v -> k h v")).then_inc(state_loaded, 16)
            for ti, (tid, rows, _) in enumerate(GROUPS[0]):
                sp.dma_start(hx[0:rows, ti, :], rows_of(xp, xs, tid)).then_inc(x_in, 16)
            sp.wait_ge(relE, 1)
            lines = rel[:, 0:767]
            sp.dma_start(rel_scr, bass.AP(lines.tensor, lines.offset + 127, [list(lines.ap[0]), [-1, P], [1, WIN]]))\
              .then_inc(rel_out, 16)
            sp.wait_ge(sk_cp, 4)
            sp.dma_start(sk_scr, skTs.rearrange("p a b -> p (a b)")).then_inc(sk_out, 16)

            def load_weights(b):
                w, nk, c0, n = blocks[b]
                if b >= NW:
                    sp.wait_ge(pj_ready, last_product[b - NW] + 1)
                sp.dma_start(wring[:, b % NW, 0:nk * n].rearrange("p (k n) -> p k n", k=nk),
                             weights[w].rearrange("(k p) n -> p k n", p=P)[:, :, c0:c0 + n])\
                  .then_inc(w_in_sem[b % NW], 16)

            def load_stage(g, s, part=slice(None)):
                for b in sorted({products[n][2] for n in by_stage.get((g, s), [])})[part]:
                    load_weights(b)

            ahead, others = slice(0, NW), slice(NW, None)

            for g, tiles in enumerate(GROUPS):
                load_stage(g, "B", ahead)
                if g > 0:
                    enter(sp, g, "A")
                    sp.wait_ge(h_out, 32 * tile_no[g, 0])
                    for ti, (tid, rows, _) in enumerate(tiles):
                        sp.dma_start(hx[0:rows, ti, :], rows_of(xp, xs, tid)).then_inc(x_in, 16)
                load_stage(g, "B", others)
                if g == 0:
                    enter(sp, g, "B")
                    sp.dma_start(kc, cache_k[0, 0].rearrange("(t p) h d -> p t (h d)", p=P)).then_inc(kc_in, 16)
                    sp.dma_start(v[:, CACHE:CACHE + 4, :], cache_v[0, 0].rearrange("(t p) h d -> p t (h d)", p=P))\
                      .then_inc(vc_in, 16)
                enter(sp, g, "C")
                for ti in k_tiles[g]:
                    tid, rows, _ = tiles[ti]
                    ko = k_sample[0, 0] if tid == SAMPLE else k_prompt[0, 0, (tid - 4) * P:(tid - 3) * P]
                    vo = v_sample[0, 0] if tid == SAMPLE else v_prompt[0, 0, (tid - 4) * P:(tid - 3) * P]
                    sp.dma_start(ko.rearrange("t h d -> t (h d)"), T2[0:rows, ti, :]).then_inc(kv_out, 16)
                    vt = vS[0:rows, :] if tid == SAMPLE else v[:, tid % KV, :]
                    sp.dma_start(vo.rearrange("t h d -> t (h d)"), vt).then_inc(kv_out, 16)
                if g == 0:
                    sp.wait_ge(rel_out, 16)
                for h in range(HA):
                    bh = g * HA + h
                    if bh >= 2:
                        q = att_no[((bh - 2) // HA, (bh - 2) % HA, len(GROUPS[(bh - 2) // HA]) - 1)]
                        sp.wait_ge(at_biased, q + 1)
                    for t0, j0 in ((0, 0), (64, 64)):
                        sp.dma_start(bias[t0:t0 + 64, bh % 2, j0:j0 + 576], rel_scr[h, t0:t0 + 64, j0:j0 + 576])\
                          .then_inc(bias_in[bh % 2], 16)
                load_stage(g, "D")
                load_stage(g, "E")
                if g == 0:
                    sp.wait_ge(hg_S, HB)
                    sp.dma_start(state_sample[0, 0].rearrange("h k v -> k h v"), S_mid[:, :, :]).then_inc(st_out, 16)
                load_stage(g, "G", ahead)
                enter(sp, g, "G")
                if g == 0:
                    sp.wait_ge(sk_out, 16)
                sp.dma_start(skT, sk_scr).then_inc(skT_in, 16)
                load_stage(g, "G", others)
                load_stage(g, "H", ahead)
                enter(sp, g, "H")
                for ti, (tid, rows, _) in enumerate(tiles):
                    sp.dma_start(hx[0:rows, ti, :], rows_of(xp, xs, tid)).then_inc(x_in, 16)
                load_stage(g, "H", others)
                load_stage(g, "I", ahead)
                enter(sp, g, "I")
                for ti, (tid, rows, _) in enumerate(tiles):
                    sp.dma_start(h_scr[tid * P:tid * P + rows, :], hx[0:rows, ti, :]).then_inc(h_out, 16)
                    sp.dma_start(xn_scr[tid * P:tid * P + rows, :], xn[0:rows, ti, :]).then_inc(h_out, 16)
                load_stage(g, "I", others)
            sp.wait_ge(hg_S, HB * 9)
            sp.dma_start(state_prompt[0, 0].rearrange("h k v -> k h v"), S_tile[:, :, 0, :]).then_inc(st_out, 16)
            sp.wait_ge(kv_out, 32 * 5)
            sp.wait_ge(st_out, 32)
            sp.wait_ge(y_out, 16 * 9)

        @block.gpsimd
        def _(pool):
            pool.memset(ident[:, :], 0.0).then_inc(consts, 1)
            pool.memset(masks[:, :, :], 0.0).then_inc(consts, 1)
            for lev, s in enumerate(LEVELS):
                pool.wait_ge(consts, 2 + lev)
                pool.memset(masks[:, lev, :].rearrange("p (b t s) -> p b t s", t=2, s=s)[:, :, 1, :], 1.0)\
                    .then_inc(consts, 1)
            pool.wait_ge(consts, 8)
            n = 8
            for m in (ident[:, :], masks[:, NL, :]):
                pool.affine_select(out=m, in_=m, compare_op=ALU.not_equal, fill=1.0, base=0,
                                   pattern=[[-1, P]], channel_multiplier=1).then_inc(consts, 1)
                n += 1
            for lev, s in enumerate(LEVELS):
                m = masks[:, lev, :].rearrange("p (b w) -> p b w", w=2 * s)
                nb = P // (2 * s)
                pool.affine_select(out=m, in_=m, compare_op=ALU.is_ge, fill=0.0, base=0,
                                   pattern=[[-2 * s, nb], [0, 2 * s]], channel_multiplier=1).then_inc(consts, 1)
                n += 1
            for lev, s in enumerate(LEVELS):
                m = masks[:, lev, :].rearrange("p (b w) -> p b w", w=2 * s)
                nb = P // (2 * s)
                pool.wait_ge(consts, n)
                pool.affine_select(out=m, in_=m, compare_op=ALU.is_ge, fill=0.0, base=s - 1,
                                   pattern=[[2 * s, nb], [0, 2 * s]], channel_multiplier=-1).then_inc(consts, 1)
                n += 1
            pool.iota(iota16[:, :], pattern=[[1, TOPK]], base=0, channel_multiplier=0,
                      allow_small_or_imprecise_dtypes=True).then_inc(consts, 1)

            def gather_half(m, half, heads):
                for n, (kind, q, rows) in enumerate(heads):
                    pool.tensor_copy(ixs[0:rows, kind, 8 * half:8 * half + 8],
                                     idx[0:rows, bass.ds(q * TOPK + 8 * half, 8)]).then_inc(ix_ready, 1)
                pool.wait_ge(ix_ready, m * 2 + (half + 1) * len(heads))
                for n in range(8 * len(heads)):
                    kind, _, rows = heads[n % len(heads)]
                    k = 8 * half + n // len(heads)
                    pool.wait_ge(ring_used, m * TOPK + 8 * half * len(heads) + n + 1)
                    pool.sem_inc(passed, 1)
                    pool.indirect_dma_start(
                        ring[0:rows, n % R, :], None, (u_tab, v_tab)[kind],
                        bass.IndirectOffsetOnAxis(ap=ixs[0:rows, kind, k:k + 1], axis=0))\
                        .then_inc(row_in[n % R], 16)

            def gathers(m, *heads):
                gather_half(m, 0, heads)
                gather_half(m, 1, heads)

            U_ROWS, V_ROWS = 0, 1

            def load_tile(tn, tid, rows):
                if tn >= 2:
                    pool.wait_ge(y_out, 16 * (tn - 1))
                pool.dma_start(xt[0:rows, tn % 2, :], xn_scr[tid * P:tid * P + rows, :]).then_inc(xt_in[tn % 2], 16)
                pool.dma_start(acc[0:rows, tn % 2, :], h_scr[tid * P:tid * P + rows, :]).then_inc(xt_in[tn % 2], 16)

            for g, tiles in enumerate(GROUPS):
                pool.wait_ge(h_out, 32 * (tile_no[g, len(tiles) - 1] + 1))
                q0 = tile_no[g, 0] * PH
                load_tile(tile_no[g, 0], *tiles[0][0:2])
                pool.wait_ge(tk_done, top_no[g, 0, 0] + 1)
                rows = tiles[0][1]
                gathers(2 * q0, (U_ROWS, q0, rows))
                pool.wait_ge(tk_done, top_no[g, 1, 0] + 1)
                gathers(2 * q0 + 1, (U_ROWS, q0 + 1, rows))
                for ti, (tid, rows, _) in enumerate(tiles):
                    q0 = tile_no[g, ti] * PH
                    with pool.Fori(q0, q0 + PH - 2) as q:
                        pool.wait_ge(tk_done, q * len(tiles) + (top_no[g, 2, ti] + 1 - q0 * len(tiles)))
                        gathers(q * 2 + 2, (U_ROWS, q + 2, rows), (V_ROWS, q, rows))
                    if ti + 1 < len(tiles):
                        load_tile(tile_no[g, ti] + 1, *tiles[ti + 1][0:2])
                    for q in (q0 + PH - 2, q0 + PH - 1):
                        if ti + 1 < len(tiles):
                            pool.wait_ge(tk_done, top_no[g, q - q0 - PH + 2, ti + 1] + 1)
                            gathers(2 * q + 2, (U_ROWS, q + 2, tiles[ti + 1][1]), (V_ROWS, q, rows))
                        else:
                            gathers(q + q0 + PH, (V_ROWS, q, rows))

        @block.tensor
        def _(pe):
            def product(n, act_in):
                g, _, b, kind, what, _, s, ti = products[n]
                _, nk, _, ncol = blocks[b]
                w = wring[:, b % NW, 0:nk * ncol].rearrange("p (k n) -> p k n", k=nk)
                pe.wait_ge(w_in_sem[b % NW], 16 * (b // NW + 1))
                if n >= 2:
                    pe.wait_ge(pj_free[n % 2], n // 2)
                for k in range(nk):
                    if kind == "fm":
                        W = width(g)
                        mm = pe.matmul(PS[:, n % 2, 0:W], w[:, k, s * P:(s + 1) * P], act_in[:, k, 0:W],
                                       start=(k == 0), stop=(k == nk - 1))
                    else:
                        _, rows, c0 = GROUPS[g][ti]
                        mm = pe.matmul(PS[0:rows, n % 2, 0:ncol], act_in[:, k, c0:c0 + rows], w[:, k, :],
                                       start=(k == 0), stop=(k == nk - 1))
                mm.then_inc(pj_ready, 1)

            def transpose_norm(g, s, source_sem):
                for ti, (tid, rows, c0) in enumerate(GROUPS[g]):
                    pe.wait_ge(source_sem, norm_no[g, s, ti] + 1)
                    for half in range(2):
                        m = n_tr(g, s, ti) + half
                        if m >= 4:
                            pe.wait_ge(tr_free, m - 3)
                        for k in range(4):
                            kk = 4 * half + k
                            mm = pe.transpose(PS[:, m % 4, k * P:k * P + rows], xn[0:rows, ti, kk * P:(kk + 1) * P],
                                              ident[0:rows, 0:rows])
                        mm.then_inc(tr_ready, 1)

            pe.wait_ge(consts, 23)
            pe.wait_ge(sk_in, 16)
            for b in range(4):
                for k in range(4):
                    mm = pe.transpose(PS[:, b, k * P:(k + 1) * P], sk[:, 4 * b + k, :], ident[:, :])
                mm.then_inc(sk_tr, 1)

            def mix(g):
                tiles = GROUPS[g]
                nt = len(tiles)
                enter(pe, g, "A")
                transpose_norm(g, "A", xn_ready)
                yield
                enter(pe, g, "B")
                for i, n in enumerate(by_stage[g, "B"]):
                    product(n, xnT)
                    if i in (3, 7):
                        yield
                for n in by_stage[g, "B"][-2:]:
                    pe.wait_ge(pj_free[n % 2], n // 2 + 1)
                kt = kt_before[g]
                for i, ti in enumerate(k_tiles[g]):
                    tid, rows, c0 = tiles[ti]
                    src = kS if tid == SAMPLE else kT[:, :, tid % KV * P:(tid % KV + 1) * P]
                    for c in range(CB):
                        mm = pe.transpose(PS[0:rows, 2 + i, c * P:(c + 1) * P], src[:, c, 0:rows], ident[:, :])
                    mm.then_inc(kt_tr, 1)
                if g == 0:
                    pe.wait_ge(kc_in, 16)
                    for t in range(4):
                        for c in range(CB):
                            mm = pe.transpose(PS[:, 4 + t, c * P:(c + 1) * P], kc[:, t, c * P:(c + 1) * P], ident[:, :])
                        mm.then_inc(kt_tr, 1)
                yield
                enter(pe, g, "C")
                if g == 0:
                    pe.wait_ge(vc_in, 16)
                steps = [s for s in att if s[0] == g]

                def keys_of(ti):
                    tid, rows, _ = tiles[ti]
                    if tid == SAMPLE:
                        return [(kT[:, :, t * P:(t + 1) * P], v[:, t, :], P) for t in range(CACHE, CACHE + 4)] + [
                            (kS, vS, DEC)]
                    return [(kT[:, :, t % KV * P:(t % KV + 1) * P], v[:, t % KV, :], P)
                            for t in range(max(0, tid - 4), tid + 1)]

                def scores(step):
                    i = att_no[step]
                    _, h, ti = step
                    tid, rows, c0 = tiles[ti]
                    if i >= 2:
                        pe.wait_ge(at_biased, i - 1)
                    p0 = 64 * (h % 2)
                    q = Q[p0:p0 + 64, h // 2, c0:c0 + rows]
                    bank = 2 + 2 * (i % 2)
                    for n, (kk, _, nk) in enumerate(keys_of(ti)):
                        mm = pe.matmul(PS[0:rows, bank + n // 4, (n % 4) * P:(n % 4) * P + nk], q,
                                       kk[p0:p0 + 64, h // 2, 0:nk], start=True, stop=True)
                    mm.then_inc(at_sc, 1)

                def values(step):
                    i = att_no[step]
                    _, h, ti = step
                    tid, rows, c0 = tiles[ti]
                    pe.wait_ge(at_exp, i + 1)
                    if i >= 1:
                        pe.wait_ge(at_ptc, i)
                    kv = keys_of(ti)
                    for n, (_, _, nk) in enumerate(kv):
                        mm = pe.transpose(PS[0:nk, 6 + n // 4, (n % 4) * P:(n % 4) * P + rows],
                                          sc[0:rows, i % 2, n * P:n * P + nk], ident[0:rows, 0:rows])
                    mm.then_inc(at_pT, 1)
                    pe.wait_ge(at_ptc, i + 1)
                    if i >= 2:
                        pe.wait_ge(at_oa, i - 1)
                    for n, (_, vv, nk) in enumerate(kv):
                        mm = pe.matmul(PS[0:rows, i % 2, 0:64], pt[0:nk, i % 2, n * P:n * P + rows],
                                       vv[0:nk, h * 64:(h + 1) * 64], start=(n == 0), stop=(n == len(kv) - 1))
                    mm.then_inc(at_pv, 1)

                for k in range(len(steps) + 1):
                    if k < len(steps):
                        scores(steps[k])
                    if k >= 1:
                        values(steps[k - 1])
                    if k >= 1 and k % 4 == 0:
                        yield
                enter(pe, g, "D")
                for ti, (tid, rows, c0) in enumerate(tiles):
                    for c in range(CB):
                        mm = pe.transpose(PS[:, 2 + ti, c * P:c * P + rows], T1[0:rows, ti, c * P:(c + 1) * P],
                                          ident[0:rows, 0:rows])
                    mm.then_inc(oT_tr, 1)
                pe.wait_ge(oT_cp, tile_no[g, nt - 1] + 1)
                for i, n in enumerate(by_stage[g, "D"]):
                    product(n, Q if products[n][4] == "branch" else xnT)
                    if i % 4 == 3:
                        yield
                for i, n in enumerate(by_stage[g, "E"]):
                    product(n, xnT)
                    if i in (3, 7, 7 + 2 * nt, 7 + 4 * nt):
                        yield
                enter(pe, g, "F")
                pe.wait_ge(state_loaded, 16)
                for ti, (tid, rows, c0) in enumerate(tiles):
                    ft = tile_no[g, ti]
                    nch = rows // CH
                    pe.wait_ge(hg_kq, ft + 1)
                    yield
                    for h in range(HB):
                        fh = ft * HB + h
                        if fh >= 1:
                            pe.wait_ge(hg_kdc, fh)
                        if h == 0 and ft >= 1:
                            pe.wait_ge(hg_obc, ft)
                        pe.transpose(PS[0:rows, 5, 0:P], E[:, NL, h, 0:rows], ident[:, :]).then_inc(hg_kdT, 1)
                        pe.wait_ge(hg_L, fh + 1)
                        if fh >= 2:
                            pe.wait_ge(hg_red, fh - 1)
                        b0 = 2 * (fh % 2)
                        for lev in range(NL):
                            pe.matmul(PS[0:rows, b0 + lev // 4, (lev % 4) * P:(lev % 4) * P + rows],
                                      Lk[:, lev, 0:rows], Lq[:, lev, 0:rows], start=True, stop=True)
                        pe.matmul(PS[0:rows, b0 + 1, 2 * P:2 * P + rows], K2[:, h, c0:c0 + rows],
                                  Q2[:, h, c0:c0 + rows], start=True, stop=True).then_inc(hg_at, 1)
                        pe.wait_ge(hg_kdc, fh + 1)
                        if fh >= 1:
                            pe.wait_ge(hg_S, fh)
                        for c in range(nch):
                            mm = pe.matmul(PS[:, 6 + c, 0:P], kdT[c * CH:(c + 1) * CH, :],
                                           T1[c * CH:(c + 1) * CH, ti, h * P:(h + 1) * P], start=True, stop=True)
                        mm.then_inc(hg_st, 1)
                        pe.wait_ge(hg_red, fh + 1)
                        if fh >= 1:
                            pe.wait_ge(hg_oc, fh)
                        pe.matmul(PS[0:rows, 4, 0:P], attnT[0:rows, fh % 2, 0:rows], T1[0:rows, ti, h * P:(h + 1) * P],
                                  start=True, stop=True, skip_group_check=True)
                        pe.wait_ge(hg_S, fh + 1)
                        s_in = S_tile[:, h, 1 if tid == SAMPLE else tid % 2, :]
                        for c in range(nch):
                            mm = pe.matmul(PS[c * CH:(c + 1) * CH, 4, 0:P], ecum[:, h, c * CH:(c + 1) * CH],
                                           s_in if c == 0 else S_mid[:, h, :], start=False, stop=True,
                                           skip_group_check=True)
                        mm.then_inc(hg_o, 1)
                        if h == 1:
                            yield
                    pe.wait_ge(hg_ob, ft + 1)
                    pe.wait_ge(hg_kdc, 4 * ft + 4)
                    for h in range(HB):
                        mm = pe.transpose(PS[:, 5, h * P:h * P + rows], ob[0:rows, h, :], ident[0:rows, 0:rows])
                    mm.then_inc(hg_oT, 1)
                    yield
                for i, n in enumerate(by_stage[g, "G"]):
                    if i == 4:
                        enter(pe, g, "G")
                    product(n, Q2 if products[n][4] == "branch" else xnT)
                    if i % 4 == 3:
                        yield
                enter(pe, g, "H")
                for n in by_stage[g, "H"][:2 * nt]:
                    product(n, M)
                yield
                for n in by_stage[g, "H"][2 * nt:]:
                    product(n, M)
                yield
                transpose_norm(g, "H", xn_ready)
                yield
                enter(pe, g, "I")
                pe.wait_ge(skT_in, 16 * (g + 1))
                qn = by_stage[g, "I"]

                def key_scores(h, ti):
                    if ti == 0:
                        for n in qn[2 * h:2 * h + 2]:
                            pe.wait_ge(pj_free[n % 2], n // 2 + 1)
                    tid, rows, c0 = tiles[ti]
                    o = top_no[g, h, ti]
                    if o >= 2:
                        pe.wait_ge(tk_cp, o - 1)
                    for p in range(2):
                        mm = pe.matmul(PS[0:rows, 2 + o % 2, p * P:(p + 1) * P], qp[:, h % 2, p, c0:c0 + rows],
                                       skT[:, (p * PH + h) * P:(p * PH + h + 1) * P], start=True, stop=True)
                    mm.then_inc(tk_sc, 1)

                def head_of(i):
                    h, ti = divmod(i, nt)
                    if ti == 0 and h + 1 < PH:
                        product(qn[2 * h + 2], xnT)
                        product(qn[2 * h + 3], xnT)
                    key_scores(h, ti)

                product(qn[0], xnT)
                product(qn[1], xnT)
                head_of(0)
                for i in range(PH * nt):
                    if i + 1 < PH * nt:
                        head_of(i + 1)
                    yield

            def nothing(m, uq, vq, half):
                pass

            interleave(mix, nothing, nothing)

        @block.scalar
        def _(act):
            def leave():
                act.activation(mark_a[:, :], ident[:, 0:1], ACT.Copy).then_inc(bar_act, 1)

            act.wait_ge(consts, 23)
            act.wait_ge(lb_d, 1)
            act.activation(lb[:, :], lbl[:, 0, :], ACT.Sigmoid).then_inc(lb_a, 1)
            for b in range(4):
                act.wait_ge(sk_tr, b + 1)
                act.activation(skTs[:, 4 * b:4 * b + 4, :], PS[:, b, :].rearrange("p (a b) -> p a b", a=4), ACT.Copy)\
                   .then_inc(sk_cp, 1)
            leave()

            def norm_tiles(g, s):
                tiles = GROUPS[g]
                for ti, (tid, rows, c0) in enumerate(tiles):
                    act.activation(xn[0:rows, ti, :], hx[0:rows, ti, :], ACT.Square,
                                   accum_out=ss[0:rows, ti:ti + 1]).then_inc(n_sq, 1)
                act.wait_ge(n_ms, norm_batch[g, s] + 1)
                act.activation(rstd[:, 0:2], ss[:, 0:2], ACT.Sqrt).then_inc(n_rt, 1)

            def sigmoid_gates(g, s, W):
                for i, n in enumerate(by_stage[g, s]):
                    if products[n][4] == "gate":
                        act.wait_ge(pj_ready, n + 1)
                        act.activation(sg[:, (products[n][5] - 28) % 8, 0:W], PS[:, n % 2, 0:W], ACT.Sigmoid)\
                           .then_inc(pj_free[n % 2], 1)
                    if i == len(by_stage[g, s]) - 1:
                        leave()
                    if i % 4 == 3:
                        yield

            def mix(g):
                tiles = GROUPS[g]
                nt = len(tiles)
                W = width(g)
                enter(act, g, "A")
                act.wait_ge(x_in, x_tiles[g, "A"])
                norm_tiles(g, "A")
                act.wait_ge(n_rs, g + 1)
                for ti, (tid, rows, c0) in enumerate(tiles):
                    act.activation(xn[0:rows, ti, :], hx[0:rows, ti, :], ACT.Copy, scale=rstd[0:rows, ti:ti + 1])\
                       .then_inc(xn_ready, 1)
                for ti, (tid, rows, c0) in enumerate(tiles):
                    for half in range(2):
                        m = n_tr(g, "A", ti) + half
                        act.wait_ge(tr_ready, m + 1)
                        for k in range(4):
                            kk = 4 * half + k
                            i = act.activation(xnT[:, kk, c0:c0 + rows], PS[:, m % 4, k * P:k * P + rows], ACT.Copy,
                                               scale=gain_mix[:, kk:kk + 1])
                        i.then_inc(tr_free, 1)
                leave()
                yield

                enter(act, g, "B")
                if g == 0:
                    act.wait_ge(sk_out, 16)
                for n in by_stage[g, "B"]:
                    _, _, b, kind, what, c, s, ti = products[n]
                    act.wait_ge(pj_ready, n + 1)
                    if what == "q":
                        i = act.activation(Q[:, c, 0:W], PS[:, n % 2, 0:W], ACT.Copy)
                    elif what == "k":
                        c -= 4
                        for tid, rows, c0 in tiles:
                            t0 = tid % KV * P
                            dst = kS[:, c, :] if tid == SAMPLE else kT[:, c, t0:t0 + P]
                            i = act.activation(dst, PS[:, n % 2, c0:c0 + rows], ACT.Copy)
                    else:
                        tid, rows, _ = tiles[ti]
                        dst = vS if tid == SAMPLE else v[:, tid % KV, :]
                        i = act.activation(dst[0:rows, c - 1024:c - 768], PS[0:rows, n % 2, 0:256], ACT.Copy)
                    i.then_inc(pj_free[n % 2], 1)
                    if n in (by_stage[g, "B"][3], by_stage[g, "B"][7]):
                        yield
                kt = kt_before[g]
                for i_, ti in enumerate(k_tiles[g]):
                    tid, rows, _ = tiles[ti]
                    act.wait_ge(kt_tr, kt + i_ + 1)
                    act.activation(T2[0:rows, ti, :], PS[0:rows, 2 + i_, :], ACT.Copy).then_inc(kt_cp, 1)
                if g == 0:
                    for t in range(4):
                        act.wait_ge(kt_tr, kt + len(k_tiles[g]) + t + 1)
                        act.activation(kT[:, :, (CACHE + t) * P:(CACHE + t + 1) * P],
                                       PS[:, 4 + t, :].rearrange("p (c t) -> p c t", c=CB), ACT.Copy).then_inc(kt_cp, 1)
                leave()
                yield

                enter(act, g, "C")

                def exps(i, step):
                    _, h, ti = step
                    rows, w = geometry(g, ti)
                    act.wait_ge(at_max, i + 1)
                    act.activation(sc[0:rows, i % 2, 0:w], sc[0:rows, i % 2, 0:w], ACT.Exp,
                                   bias=nmax[0:rows, i % 2:i % 2 + 1],
                                   accum_out=rsum[0:rows, i % 2:i % 2 + 1]).then_inc(at_exp, 1)

                def turned(i, step):
                    _, h, ti = step
                    rows, w = geometry(g, ti)
                    act.wait_ge(at_pT, i + 1)
                    if i >= 2:
                        act.wait_ge(at_pv, i - 1)
                    flat = PS[:, 6:8, :].rearrange("p a b -> p (a b)")
                    if rows == P:
                        j = act.activation(pt[:, i % 2, 0:w], flat[:, 0:w], ACT.Copy)
                    else:
                        act.activation(pt[:, i % 2, 0:512].rearrange("p (a b) -> p a b", b=P)[:, :, 0:rows],
                                       flat[:, 0:512].rearrange("p (a b) -> p a b", b=P)[:, :, 0:rows], ACT.Copy)
                        j = act.activation(pt[0:DEC, i % 2, 512:512 + rows], flat[0:DEC, 512:512 + rows], ACT.Copy)
                    j.then_inc(at_ptc, 1)

                def scaled(i, step):
                    _, h, ti = step
                    rows = tiles[ti][1]
                    act.wait_ge(at_rinv, i + 1)
                    act.wait_ge(at_pv, i + 1)
                    act.activation(T1[0:rows, ti, h * 64:(h + 1) * 64], PS[0:rows, i % 2, 0:64], ACT.Copy,
                                   scale=rinv[0:rows, i % 2:i % 2 + 1]).then_inc(at_oa, 1)

                steps = [s for s in att if s[0] == g]
                for k in range(len(steps) + 1):
                    if k >= 1:
                        turned(att_no[steps[k - 1]], steps[k - 1])
                    if k < len(steps):
                        exps(att_no[steps[k]], steps[k])
                    if k >= 2:
                        scaled(att_no[steps[k - 2]], steps[k - 2])
                    if k == len(steps):
                        scaled(att_no[steps[k - 1]], steps[k - 1])
                        leave()
                    if k >= 1 and k % 4 == 0:
                        yield

                enter(act, g, "D")
                for ti, (tid, rows, c0) in enumerate(tiles):
                    act.wait_ge(oT_tr, tile_no[g, ti] + 1)
                    act.activation(Q[:, :, c0:c0 + rows],
                                   PS[:, 2 + ti, :].rearrange("p (c t) -> p c t", c=CB)[:, :, 0:rows], ACT.Copy)\
                       .then_inc(oT_cp, 1)
                yield from sigmoid_gates(g, "D", W)

                enter(act, g, "E")
                if any(k_tiles[q] for q in range(g + 1)):
                    act.wait_ge(kv_out, 32 * sum(len(k_tiles[q]) for q in range(g + 1)))
                for n in by_stage[g, "E"]:
                    _, _, b, kind, what, c, s, ti = products[n]
                    act.wait_ge(pj_ready, n + 1)
                    if what == "f":
                        i = act.activation(Q[:, c - 12, 0:W], PS[:, n % 2, 0:W], ACT.Sigmoid)
                    elif what == "qb":
                        i = act.activation(Q2[:, c - 20, 0:W], PS[:, n % 2, 0:W], ACT.Silu)
                    elif what == "i":
                        rows = tiles[ti][1]
                        i = act.activation(T1[0:rows, ti, c - 2048:c - 1792], PS[0:rows, n % 2, 0:256], ACT.Copy)
                    else:
                        rows = tiles[ti][1]
                        i = act.activation(T2[0:rows, ti, c - 3072:c - 2816], PS[0:rows, n % 2, 0:256], ACT.Silu)
                    i.then_inc(pj_free[n % 2], 1)
                    if n == by_stage[g, "E"][3]:
                        act.wait_ge(f_fg, g + 1)
                        act.activation(Q[:, :, 0:W], K2[:, :, 0:W], ACT.Ln).then_inc(f_ln, 1)
                        yield
                    if n in (by_stage[g, "E"][7], by_stage[g, "E"][7 + 2 * nt]):
                        yield
                leave()
                yield

                enter(act, g, "F")
                for ti, (tid, rows, c0) in enumerate(tiles):
                    ft = tile_no[g, ti]
                    act.wait_ge(hg_D, ft + 1)
                    view = E[:, :, :, :].rearrange("p l h t -> p (l h) t")[:, :, 0:rows]
                    act.activation(view, view, ACT.Exp)
                    act.activation(ecum[:, :, 0:rows], Q[:, :, c0:c0 + rows], ACT.Exp).then_inc(hg_E, 1)
                    yield
                    for h in range(HB):
                        fh = ft * HB + h
                        act.wait_ge(hg_kdT, fh + 1)
                        if fh >= 1:
                            act.wait_ge(hg_st, fh)
                        act.activation(kdT[0:rows, :], PS[0:rows, 5, 0:P], ACT.Copy).then_inc(hg_kdc, 1)
                        act.wait_ge(hg_o, fh + 1)
                        if h == 0 and ft >= 1:
                            act.wait_ge(hg_oT, ft)
                        act.activation(ob[0:rows, h, :], PS[0:rows, 4, 0:P], ACT.Copy)
                        if fh >= 1:
                            act.wait_ge(hg_oc, fh)
                        act.activation(junk[0:rows, :], PS[0:rows, 4, 0:P], ACT.Square,
                                       accum_out=ssq[0:rows, h:h + 1]).then_inc(hg_oc, 1)
                        if h == 1:
                            yield
                    act.wait_ge(hg_ms, ft + 1)
                    act.activation(rsq[0:rows, :], ssq[0:rows, :], ACT.Sqrt).then_inc(hg_rt, 1)
                    act.wait_ge(hg_oT, ft + 1)
                    act.activation(Q2[:, :, c0:c0 + rows],
                                   PS[:, 5, :].rearrange("p (c t) -> p c t", c=CB)[:, :, 0:rows], ACT.Copy)\
                       .then_inc(hg_obc, 1)
                    if ti == nt - 1:
                        leave()
                    yield

                enter(act, g, "G")
                yield from sigmoid_gates(g, "G", W)

                enter(act, g, "H")
                yield
                yield
                for n in by_stage[g, "H"][-2:]:
                    act.wait_ge(pj_free[n % 2], n // 2 + 1)
                norm_tiles(g, "H")
                for ti, (tid, rows, c0) in enumerate(tiles):
                    for half in range(2):
                        m = n_tr(g, "H", ti) + half
                        act.wait_ge(tr_ready, m + 1)
                        act.activation(xnT[:, 4 * half:4 * half + 4, c0:c0 + rows],
                                       PS[:, m % 4, :].rearrange("p (c t) -> p c t", c=4)[:, :, 0:rows], ACT.Copy)\
                           .then_inc(tr_free, 1)
                leave()
                yield

                enter(act, g, "I")
                qn = by_stage[g, "I"]

                def copy_scores(i):
                    h, ti = divmod(i, nt)
                    rows = tiles[ti][1]
                    if ti == 0:
                        for p in range(2):
                            n = qn[2 * h + p]
                            act.wait_ge(pj_ready, n + 1)
                            if h >= 2:
                                act.wait_ge(tk_sc, top_no[g, h - 2, nt - 1] + 1)
                            act.activation(qp[:, h % 2, p, 0:W], PS[:, n % 2, 0:W], ACT.Copy).then_inc(pj_free[n % 2], 1)
                    o = top_no[g, h, ti]
                    act.wait_ge(tk_sc, o + 1)
                    if o >= 2:
                        act.wait_ge(tk_done, o - 1)
                    act.activation(s1[0:rows, o % 2], PS[0:rows, 2 + o % 2, 0:2 * P]
                                   .rearrange("p (a b) -> p a b", a=2), ACT.Copy).then_inc(tk_cp, 1)

                copy_scores(0)
                for i in range(PH * nt):
                    if i + 1 < PH * nt:
                        copy_scores(i + 1)
                    h, ti = divmod(i, nt)
                    rows = tiles[ti][1]
                    o = top_no[g, h, ti]
                    act.wait_ge(tk_cv, o + 1)
                    act.activation(ge[0:rows, :], cv[0:rows, :], ACT.Exp, bias=ncv[0:rows, :],
                                   accum_out=gsum[0:rows, :]).then_inc(tk_exp, 1)
                    if i == PH * nt - 1:
                        leave()
                    yield

            ended = []

            def unit(m, uq, vq, half):
                pass

            def tail(m, uq, vq, half):
                if uq is not None and half != 0:
                    rows = tile_rows[uq // PH]
                    act.wait_ge(ring_used, R + TOPK * (m + 1))
                    act.activation(glu[0:rows, uq % 2, :], hid[0:rows, uq % 2, :], ACT.Gelu).then_inc(e_gelu, 1)
                for t, last in ended:
                    finish_tile(t, m - last)
                if vq is not None and vq % PH == PH - 1 and half != 0:
                    ended.append((vq // PH, m))
                    finish_tile(vq // PH, 0)

            def finish_tile(tn, step):
                rows, s = tile_rows[tn], tn % 2
                if step == 0:
                    act.wait_ge(ring_used, R + TOPK * (ended[-1][1] + 1))
                    act.activation(xt[0:rows, s, :], acc[0:rows, s, :], ACT.Square,
                                   accum_out=esum[0:rows, s:s + 1]).then_inc(e_sq, 1)
                elif step == 1:
                    act.wait_ge(e_ms, tn + 1)
                    act.activation(erstd[0:rows, s:s + 1], esum[0:rows, s:s + 1], ACT.Sqrt).then_inc(e_rt, 1)
                elif step == 3:
                    tid = tile_ids[tn]
                    act.wait_ge(e_y, tn + 1)
                    act.dma_start(rows_of(y_prompt[0], y_sample[0], tid), acc[0:rows, s, :]).then_inc(y_out, 16)

            m = interleave(mix, unit, tail)
            for step in (1, 3):
                finish_tile(ended[-1][0], step)

        @block.vector
        def _(dve):
            chain = [0]

            def link(ins):
                chain[0] += 1
                ins.then_inc(dve_chain, 1)
                dve.wait_ge(dve_chain, chain[0])

            def linked(ins):
                chain[0] += 1
                now = chain[0]
                ins.then_inc(dve_chain, 1)
                yield 1
                dve.wait_ge(dve_chain, now)

            def leave():
                dve.memset(mark_d[:, :], 0.0).then_inc(bar_dve, 1)

            dve.wait_ge(rel_in, 16)
            dve.tensor_copy(rel[:, 0:383], rel[:, 383:384].to_broadcast([HA, 383])).then_inc(relE, 1)
            dve.memset(bias[:, :, :], NEG)
            dve.memset(S_tile[:, :, 0, :], 0.0)
            dve.memset(ss[:, :], 1.0)
            dve.memset(restart[:, :], 1.0).then_inc(dve_chain, 1)
            chain[0] += 1
            dve.wait_ge(dve_chain, chain[0])
            link(dve.memset(restart[:, :].rearrange("p (c t) -> p c t", t=CH)[:, :, 0:1], 0.0))
            dve.wait_ge(const_in, 80)
            dve.tensor_tensor(lbl[:, 0, :], lbl[:, 0, :], lbl[:, 1, :], ALU.subtract).then_inc(lb_d, 1)
            dve.wait_ge(lb_a, 1)
            link(dve.tensor_scalar(one_lb[:, :], lb[:, :], -1.0, 1.0, ALU.mult, ALU.add))
            leave()

            def norm_scale(g, s):
                tiles = GROUPS[g]
                dve.wait_ge(n_sq, norm_no[g, s, len(tiles) - 1] + 1)
                dve.tensor_scalar(ss[:, 0:2], ss[:, 0:2], 1.0 / D, EPS, ALU.mult, ALU.add).then_inc(n_ms, 1)
                yield 2
                dve.wait_ge(n_rt, norm_batch[g, s] + 1)
                i = dve.reciprocal(rstd[:, 0:2], rstd[:, 0:2])
                if s == "A":
                    i.then_inc(n_rs, 1)
                else:
                    link(i)

            def gated(g, stage, W):
                for i, n in enumerate(by_stage[g, stage]):
                    _, _, b, kind, what, c, s, ti = products[n]
                    if what != "branch":
                        if i % 4 == 3:
                            yield
                        continue
                    yield 3
                    dve.wait_ge(pj_ready, n + 1)
                    gn = gate_product(g, stage, c)
                    dve.wait_ge(pj_free[gn % 2], gn // 2 + 1)
                    if stage == "D":
                        dve.tensor_tensor(M[:, c, 0:W], PS[:, n % 2, 0:W], sg[:, c, 0:W], ALU.mult)\
                           .then_inc(pj_free[n % 2], 1)
                    else:
                        dve.tensor_tensor(sg[:, c, 0:W], PS[:, n % 2, 0:W], sg[:, c, 0:W], ALU.mult)\
                           .then_inc(pj_free[n % 2], 1)
                        dve.wait_ge(pj_free[n % 2], n // 2 + 1)
                        dve.tensor_tensor(M[:, c, 0:W], M[:, c, 0:W], sg[:, c, 0:W], ALU.add)
                    if i == len(by_stage[g, stage]) - 1:
                        leave()
                    if i % 4 == 3:
                        yield

            def mix(g):
                tiles = GROUPS[g]
                W = width(g)
                nt = len(tiles)
                enter(dve, g, "A")
                yield 4
                yield from norm_scale(g, "A")
                leave()
                yield
                enter(dve, g, "B")
                yield
                yield
                leave()
                yield

                enter(dve, g, "C")

                def bias_max(i, step):
                    _, h, ti = step
                    rows, w = geometry(g, ti)
                    bh = g * HA + h
                    dve.wait_ge(at_sc, i + 1)
                    dve.wait_ge(bias_in[bh % 2], 32 * (bh // 2 + 1))
                    if i >= 2:
                        dve.wait_ge(at_pT, i - 1)
                    b0 = 2 + 2 * (i % 2)
                    flat = PS[:, b0:b0 + 2, :].rearrange("p a b -> p (a b)")
                    off = WIN - w if rows == P else 0
                    dve.scalar_tensor_tensor(out=sc[0:rows, i % 2, 0:w], in0=flat[0:rows, 0:w], scalar=SCALE,
                                             in1=bias[0:rows, bh % 2, off:off + w], op0=ALU.mult, op1=ALU.add)\
                       .then_inc(at_biased, 1)
                    dve.wait_ge(at_biased, i + 1)
                    if i >= 2:
                        dve.wait_ge(at_exp, i - 1)
                    dve.tensor_reduce(nmax[0:rows, i % 2:i % 2 + 1], sc[0:rows, i % 2, 0:w], AX, ALU.max,
                                      negate=True).then_inc(at_max, 1)

                def inverse_sum(i, step):
                    _, h, ti = step
                    rows, w = geometry(g, ti)
                    dve.wait_ge(at_exp, i + 1)
                    if i >= 2:
                        dve.wait_ge(at_oa, i - 1)
                    dve.reciprocal(rinv[0:rows, i % 2:i % 2 + 1], rsum[0:rows, i % 2:i % 2 + 1]).then_inc(at_rinv, 1)

                steps = [s for s in att if s[0] == g]
                for k in range(len(steps) + 1):
                    if k < len(steps):
                        bias_max(att_no[steps[k]], steps[k])
                    if k >= 1:
                        yield 4
                        inverse_sum(att_no[steps[k - 1]], steps[k - 1])
                    if k == len(steps):
                        leave()
                    if k >= 1 and k % 4 == 0:
                        yield

                enter(dve, g, "D")
                yield from gated(g, "D", W)

                enter(dve, g, "E")
                fn = [n for n in by_stage[g, "E"] if products[n][4] == "f"]
                for h, n in enumerate(fn):
                    yield 2
                    dve.wait_ge(pj_free[n % 2], n // 2 + 1)
                    i = dve.tensor_scalar(K2[:, h, 0:W], Q[:, h, 0:W], one_lb[:, h:h + 1], lb[:, h:h + 1],
                                          ALU.mult, ALU.add)
                i.then_inc(f_fg, 1)
                yield
                yield 2
                dve.wait_ge(f_ln, g + 1)
                link(dve.tensor_scalar(K2[:, :, 0:W], K2[:, :, 0:W], -1.0, 1.0, ALU.mult, ALU.add))
                for h in range(HB):
                    dve.tensor_tensor_scan(Q[:, h, 0:W], restart[:, 0:W], Q[:, h, 0:W], 0.0, ALU.mult, ALU.add)
                yield
                yield
                yield 8
                gn = [n for n in by_stage[g, "E"] if products[n][4] == "g"]
                for n in gn[-2:]:
                    dve.wait_ge(pj_free[n % 2], n // 2 + 1)
                for ti, (tid, rows, c0) in enumerate(tiles):
                    dve.tensor_tensor(T2[0:rows, ti, :], T2[0:rows, ti, :], gain_hgrn[0:rows, :], ALU.mult)
                leave()
                yield

                enter(dve, g, "F")
                dve.wait_ge(state_loaded, 16)
                for ti, (tid, rows, c0) in enumerate(tiles):
                    ft = tile_no[g, ti]
                    nch = rows // CH
                    if ft >= 1:
                        dve.wait_ge(hg_o, HB * ft)
                    cum = Q[:, :, c0:c0 + rows]
                    for lev, s in enumerate(LEVELS):
                        nb = rows // (2 * s)
                        c4 = cum.rearrange("p h (b t s) -> p h b t s", t=2, s=s)
                        e4 = E[:, lev, :, 0:rows].rearrange("p h (b t s) -> p h b t s", t=2, s=s)
                        ref = c4[:, :, :, 0, s - 1:s].to_broadcast([P, HB, nb, s])
                        dve.tensor_tensor(e4[:, :, :, 1, :], c4[:, :, :, 1, :], ref, ALU.subtract)
                        dve.tensor_tensor(e4[:, :, :, 0, :], ref, c4[:, :, :, 0, :], ALU.subtract)
                    c3 = cum.rearrange("p h (b s) -> p h b s", s=CH)
                    dve.tensor_tensor(E[:, NL, :, 0:rows].rearrange("p h (b s) -> p h b s", s=CH),
                                      c3[:, :, :, CH - 1:CH].to_broadcast([P, HB, nch, CH]), c3,
                                      ALU.subtract).then_inc(hg_D, 1)
                    yield 6
                    dve.wait_ge(hg_E, ft + 1)
                    link(dve.tensor_copy(elast[:, :, 0:nch], ecum[:, :, CH - 1:rows:CH]))
                    dve.tensor_tensor(E[:, NL, :, 0:rows], E[:, NL, :, 0:rows], K2[:, :, c0:c0 + rows], ALU.mult)
                    dve.tensor_tensor(ecum[:, :, 0:rows], ecum[:, :, 0:rows], Q2[:, :, c0:c0 + rows], ALU.mult)\
                       .then_inc(hg_kq, 1)
                    yield
                    for h in range(HB):
                        fh = ft * HB + h
                        if fh >= 1:
                            dve.wait_ge(hg_at, fh)
                        dve.tensor_tensor(Lq[:, :, 0:rows], E[:, 0:NL, h, 0:rows],
                                          Q2[:, h:h + 1, c0:c0 + rows].to_broadcast([P, NL, rows]), ALU.mult)
                        dve.tensor_tensor(Lk[:, :, 0:rows], E[:, 0:NL, h, 0:rows],
                                          K2[:, h:h + 1, c0:c0 + rows].to_broadcast([P, NL, rows]), ALU.mult)\
                           .then_inc(hg_L, 1)
                        yield 4
                        dve.wait_ge(hg_at, fh + 1)
                        b0 = 2 * (fh % 2)
                        at = PS[:, b0:b0 + 2, :].rearrange("p a (b t) -> p (a b) t", t=P)[0:rows, 0:NL + 1, 0:rows]
                        link(dve.tensor_tensor(Am[0:rows, :, 0:rows], at, masks[0:rows, :, 0:rows], ALU.mult))
                        if fh >= 2:
                            dve.wait_ge(hg_o, fh - 1)
                        dve.tensor_reduce(attnT[0:rows, fh % 2, 0:rows],
                                          Am[0:rows, :, 0:rows].rearrange("p l t -> p t l"), AX, ALU.add)\
                           .then_inc(hg_red, 1)
                        yield 1
                        dve.wait_ge(hg_st, fh + 1)
                        if ft >= 1:
                            dve.wait_ge(hg_o, fh - 3)
                        if ft == 1:
                            dve.wait_ge(st_out, 16)
                        s_in = S_tile[:, h, 1 if tid == SAMPLE else tid % 2, :]
                        i = dve.scalar_tensor_tensor(out=S_mid[:, h, :], in0=s_in, scalar=elast[:, h, 0:1],
                                                     in1=PS[:, 6, 0:P], op0=ALU.mult, op1=ALU.add)
                        if nch == 2:
                            link(i)
                            i = dve.scalar_tensor_tensor(out=S_tile[:, h, (tid + 1) % 2, :], in0=S_mid[:, h, :],
                                                         scalar=elast[:, h, 1:2], in1=PS[:, 7, 0:P],
                                                         op0=ALU.mult, op1=ALU.add)
                        i.then_inc(hg_S, 1)
                        if h == 1:
                            yield
                    yield 2
                    dve.wait_ge(hg_oc, HB * ft + HB)
                    dve.tensor_scalar(ssq[0:rows, :], ssq[0:rows, :], 1.0 / P, EPS, ALU.mult, ALU.add).then_inc(hg_ms, 1)
                    dve.wait_ge(hg_rt, ft + 1)
                    link(dve.reciprocal(rsq[0:rows, :], rsq[0:rows, :]))
                    link(dve.tensor_tensor(ob[0:rows], ob[0:rows], rsq[0:rows, :].unsqueeze(2).to_broadcast([rows, HB, P]),
                                           ALU.mult))
                    dve.tensor_tensor(ob[0:rows].rearrange("p h d -> p (h d)"), ob[0:rows].rearrange("p h d -> p (h d)"),
                                      T2[0:rows, ti, :], ALU.mult).then_inc(hg_ob, 1)
                    if ti == nt - 1:
                        leave()
                    yield

                enter(dve, g, "G")
                yield from gated(g, "G", W)

                enter(dve, g, "H")
                dve.wait_ge(x_in, x_tiles[g, "H"])
                for n in by_stage[g, "H"]:
                    _, _, b, kind, what, c, s, ti = products[n]
                    rows = tiles[ti][1]
                    yield 2
                    dve.wait_ge(pj_ready, n + 1)
                    dve.tensor_tensor(hx[0:rows, ti, c:c + 256], PS[0:rows, n % 2, 0:256], hx[0:rows, ti, c:c + 256],
                                      ALU.add).then_inc(pj_free[n % 2], 1)
                    if n == by_stage[g, "H"][2 * nt - 1]:
                        yield
                yield
                yield from norm_scale(g, "H")
                for ti, (tid, rows, c0) in enumerate(tiles):
                    dve.scalar_tensor_tensor(out=xn[0:rows, ti, :], in0=hx[0:rows, ti, :], scalar=rstd[0:rows, ti:ti + 1],
                                             in1=gain_ffn[0:rows, :], op0=ALU.mult, op1=ALU.mult).then_inc(xn_ready, 1)
                leave()
                yield

                enter(dve, g, "I")
                for h in range(PH):
                    for ti, (tid, rows, c0) in enumerate(tiles):
                        o = top_no[g, h, ti]
                        r = slice(0, rows)
                        yield 2
                        dve.wait_ge(tk_cp, o + 1)
                        for p in range(2):
                            i = dve.max(sv[r, p, 0:8], s1[r, o % 2, p, :])
                        yield from linked(i)
                        for p in range(2):
                            dve.max_index(si[r, p, 0:8], sv[r, p, 0:8], s1[r, o % 2, p, :])
                            i = dve.match_replace(s2[r, p, :], sv[r, p, 0:8], s1[r, o % 2, p, :], LOWEST)
                        yield from linked(i)
                        for p in range(2):
                            i = dve.max(sv[r, p, 8:16], s2[r, p, :])
                        yield from linked(i)
                        for p in range(2):
                            i = dve.max_index(si[r, p, 8:16], sv[r, p, 8:16], s2[r, p, :])
                        yield from linked(i)
                        dve.tensor_copy(sif[r], si[r])
                        yield from linked(dve.tensor_tensor(comb[r], sv[r, 0, :].unsqueeze(2).to_broadcast([rows, TOPK, TOPK]),
                                                            sv[r, 1:2, :].to_broadcast([rows, TOPK, TOPK]), ALU.add))
                        cf = comb[r].rearrange("p a b -> p (a b)")
                        if o >= 1:
                            dve.wait_ge(tk_exp, o)
                        yield from linked(dve.max(cv[r, 0:8], cf))
                        dve.max_index(ci[r, 0:8], cv[r, 0:8], cf)
                        yield from linked(dve.match_replace(comb2[r], cv[r, 0:8], cf, LOWEST))
                        dve.tensor_scalar(ncv[r], cv[r, 0:1], -1.0, None, ALU.mult)
                        yield from linked(dve.max(cv[r, 8:16], comb2[r]))
                        yield from linked(dve.max_index(ci[r, 8:16], cv[r, 8:16], comb2[r]))
                        dve.tensor_scalar(ab[r, 0, :], ci[r], 4, None, ALU.logical_shift_right).then_inc(tk_cv, 1)
                        yield from linked(dve.tensor_scalar(ab[r, 1, :], ci[r], 15, None, ALU.bitwise_and))
                        yield from linked(dve.tensor_copy(abf[r], ab[r]))
                        square = [rows, 2, TOPK, TOPK]
                        yield from linked(dve.tensor_tensor(
                            eq[r], abf[r].unsqueeze(3).to_broadcast(square),
                            iota16[r, :].unsqueeze(1).unsqueeze(1).to_broadcast(square), ALU.is_equal))
                        yield from linked(dve.tensor_tensor(
                            eq[r], eq[r], sif[r].unsqueeze(2).to_broadcast(square), ALU.mult))
                        yield from linked(dve.tensor_reduce(i12[r], eq[r], AX, ALU.add))
                        at = tile_no[g, ti] * P + h * TOPK
                        dve.scalar_tensor_tensor(out=idx[r, at:at + TOPK], in0=i12[r, 0, :], scalar=128.0, in1=i12[r, 1, :],
                                                 op0=ALU.mult, op1=ALU.add)
                        dve.wait_ge(tk_exp, o + 1)
                        link(dve.reciprocal(ginv[r], gsum[r]))
                        dve.tensor_scalar(gates[r, at:at + TOPK], ge[r], ginv[r], None, ALU.mult).then_inc(tk_done, 1)
                        if h == PH - 1 and ti == nt - 1:
                            leave()
                        yield

            dve.memset(hid[:, :, :], 0.0).then_inc(ring_used, R)
            dve.wait_ge(ring_used, R)

            taken = {}

            latest = [0]

            def unit(m, uq, vq, half, count=TOPK):
                first = taken.get(m, 0)
                taken[m] = min(first + count, TOPK)
                left = count - (taken[m] - first)
                if taken[m] == first:
                    return left
                if first == 0 and uq is not None:
                    dve.wait_ge(xt_in[uq // PH % 2], 32 * (uq // PH // 2 + 1))
                if first == 0 and vq is not None and half != 1:
                    rows = tile_rows[vq // PH]
                    dve.wait_ge(e_gelu, vq + 1)
                    dve.tensor_tensor(wk[0:rows, vq % 2, :], glu[0:rows, vq % 2, :],
                                      gates[0:rows, vq * TOPK:(vq + 1) * TOPK], ALU.mult).then_inc(e_w, 1)
                for n, (kind, q, k) in list(enumerate(unit_rows(uq, vq, half)))[first:taken[m]]:
                    row_no = TOPK * m + n
                    rows, s = tile_rows[q // PH], q // PH % 2
                    dve.wait_ge(row_in[row_no % R], 16 * (row_no // R + 1))
                    row = ring[0:rows, row_no % R, :]
                    if kind == "u":
                        dve.tensor_tensor_reduce(row, row, xt[0:rows, s, :], 1.0, 0.0, ALU.mult, ALU.add,
                                                 hid[0:rows, q % 2, k:k + 1]).then_inc(ring_used, 1)
                    else:
                        if k == 0:
                            dve.wait_ge(e_w, q + 1)
                        dve.wait_ge(ring_used, R + latest[0])
                        dve.scalar_tensor_tensor(out=acc[0:rows, s, :], in0=row, scalar=wk[0:rows, q % 2, k:k + 1],
                                                 in1=acc[0:rows, s, :], op0=ALU.mult, op1=ALU.add)\
                           .then_inc(ring_used, 1)
                        latest[0] = row_no + 1
                return left

            ended = []

            def tail(m, uq, vq, half):
                for t, last in ended:
                    finish_tile(t, m - last)
                if vq is not None and vq % PH == PH - 1 and half != 0:
                    ended.append((vq // PH, m))

            def finish_tile(tn, step):
                rows, s = tile_rows[tn], tn % 2
                if step == 1:
                    dve.wait_ge(e_sq, tn + 1)
                    dve.tensor_scalar(esum[0:rows, s:s + 1], esum[0:rows, s:s + 1], 1.0 / D, EPS, ALU.mult, ALU.add)\
                       .then_inc(e_ms, 1)
                elif step == 3:
                    dve.wait_ge(e_rt, tn + 1)
                    dve.reciprocal(erstd[0:rows, s:s + 1], erstd[0:rows, s:s + 1]).then_inc(e_rs, 1)
                    dve.wait_ge(e_rs, tn + 1)
                    dve.scalar_tensor_tensor(out=acc[0:rows, s, :], in0=acc[0:rows, s, :], scalar=erstd[0:rows, s:s + 1],
                                             in1=gain_final[0:rows, :], op0=ALU.mult, op1=ALU.mult).then_inc(e_y, 1)

            interleave(mix, unit, tail, meanwhile=unit)
            for step in (1, 3):
                finish_tile(ended[-1][0], step)


_INS = ["x_prompt", "x_sample", "cache_attn_k", "cache_attn_v", "state_hgrn", "norm_mix", "w_in", "rel_bias",
        "lb_logits", "hgrn_norm", "w_branch_a", "w_branch_b", "w_out", "norm_ffn", "peer_query", "peer_subkeys",
        "peer_u", "peer_v", "norm_final"]
_FLAT = {"peer_u": 1, "peer_v": 1}
_OUTS = [(1, SEQ, D), (1, DEC, D), (1, 1, 512, HA, 64), (1, 1, 512, HA, 64), (1, 1, HB, P, P),
         (1, 1, DEC, HA, 64), (1, 1, DEC, HA, 64), (1, 1, HB, P, P)]


def kernel(**inputs):
    import numpy as _np
    import concourse.bacc as _bacc
    from concourse import mybir as _mybir
    from concourse.bass_utils import run_bass_kernel_spmd as _run

    nc = _bacc.Bacc("TRN2", target_bir_lowering=False, num_devices=1)
    arrays, args = {}, []
    for name in _INS:
        a = _np.ascontiguousarray(inputs[name])
        if name in _FLAT:
            a = a[0]
        arrays[f"in_{name}"] = a
        args.append(nc.dram_tensor(f"in_{name}", a.shape, _mybir.dt.from_np(a.dtype), kind="ExternalInput").ap())
    for i, shape in enumerate(_OUTS):
        args.append(nc.dram_tensor(f"out_{i}", shape, _mybir.dt.float32, kind="ExternalOutput").ap())
    build(nc, *args)
    r = _run(nc, [arrays], core_ids=[0])
    got = [r.results[0][f"out_{i}"] for i in range(len(_OUTS))]
    return tuple(got)
```
